# Optimizing a Trainium2 kernel written in Bass

```python
import jax, jax.numpy as jnp
from jax import lax
import numpy as np

D_MODEL = 1024
BATCH = 1
SEQ = 1024
DEPTH = 2

GRID_W = 64
CTX_LEN = 256
EPS = 1e-6
NEG_INF = -1e30

LRU_WIDTH = D_MODEL
LRU_HEADS = 16
LRU_BLOCK = LRU_WIDTH // LRU_HEADS
LRU_C = 8.0
CONV_W = 4
CONV_LEFT = 2
FNET_WIDTH = D_MODEL
FNET_GROUPS = 8
FNET_GROUP_DIM = FNET_WIDTH // FNET_GROUPS
L0_IN_WIDTH = 2 * LRU_WIDTH + 2 * FNET_WIDTH
L0_MIX_WIDTH = LRU_WIDTH + FNET_WIDTH
HEAD_DIM = 64
N_Q_HEADS = D_MODEL // HEAD_DIM
N_KV_HEADS = 4
GQA_GROUP = N_Q_HEADS // N_KV_HEADS
Q_WIDTH = N_Q_HEADS * HEAD_DIM
KV_WIDTH = N_KV_HEADS * HEAD_DIM
L1_IN_WIDTH = 2 * Q_WIDTH + 2 * KV_WIDTH
WINDOW = 128
BLOCK = 128
ROPE_BASE = 10000.0

kernel_name = "hybrid_rglru_fourier_window_gqa_ctx_prefix"

def rms_norm(x, g):
    xf = x.astype(jnp.float32)
    y = xf * lax.rsqrt(jnp.mean(xf * xf, axis=-1, keepdims=True) + EPS)
    return (y * g.astype(jnp.float32)).astype(x.dtype)

def modulation(cvec, w_mod, b_mod):
    m = jax.nn.silu(cvec) @ w_mod + b_mod
    return jnp.split(m, 3, axis=-1)

def centred_depthwise_conv(u, w, b):
    n = u.shape[1]
    up = jnp.pad(u, ((0, 0), (CONV_LEFT, CONV_W - 1 - CONV_LEFT), (0, 0)))
    out = b + up[:, 0:n] * w[0]
    for k in range(1, CONV_W):
        out = out + up[:, k:k + n] * w[k]
    return out

def block_diag_linear(u, w, b):
    bsz, n, _ = u.shape
    y = jnp.einsum('bnhd,hde->bnhe', u.reshape(bsz, n, LRU_HEADS, LRU_BLOCK), w)
    return y.reshape(bsz, n, LRU_WIDTH) + b

def rglru_coeffs(u, w_a, b_a, w_x, b_x, lam):
    uf = u.astype(jnp.float32)
    r = jax.nn.sigmoid(block_diag_linear(uf, w_a.astype(jnp.float32), b_a.astype(jnp.float32)))
    i = jax.nn.sigmoid(block_diag_linear(uf, w_x.astype(jnp.float32), b_x.astype(jnp.float32)))
    log_a = -LRU_C * r * jax.nn.softplus(-lam.astype(jnp.float32))
    a = jnp.exp(log_a)
    bterm = jnp.sqrt(-jnp.expm1(2.0 * log_a)) * (i * uf)
    return a, bterm

def linear_scan(a, b, h0):
    b = b.at[:, 0].add(a[:, 0] * h0)

    def combine(lft, rgt):
        return (lft[0] * rgt[0], rgt[0] * lft[1] + rgt[1])

    _, h = lax.associative_scan(combine, (a, b), axis=1)
    return h

def rglru_bidirectional(u_lat, u_ctx, w_a, b_a, w_x, b_x, lam):
    y_lat = None
    y_ctx = None
    for d in range(2):
        ul = u_lat if d == 0 else jnp.flip(u_lat, axis=1)
        uc = u_ctx if d == 0 else jnp.flip(u_ctx, axis=1)
        a_c, b_c = rglru_coeffs(uc, w_a[d], b_a[d], w_x[d], b_x[d], lam[d])
        h_c = linear_scan(a_c, b_c, jnp.zeros_like(b_c[:, 0]))
        a_l, b_l = rglru_coeffs(ul, w_a[d], b_a[d], w_x[d], b_x[d], lam[d])
        h_l = linear_scan(a_l, b_l, h_c[:, -1])
        if d == 1:
            h_c = jnp.flip(h_c, axis=1)
            h_l = jnp.flip(h_l, axis=1)
        y_lat = h_l if y_lat is None else y_lat + h_l
        y_ctx = h_c if y_ctx is None else y_ctx + h_c
    return y_lat, y_ctx

def fourier_mix(u, w_f, b_f):
    bsz, n, _ = u.shape
    ug = u.astype(jnp.float32).reshape(bsz, n, FNET_GROUPS, FNET_GROUP_DIM)
    f = jnp.fft.fft2(ug, axes=(1, 3), norm="ortho").real
    y = jnp.einsum('bngd,gde->bnge', f, w_f.astype(jnp.float32)).reshape(bsz, n, FNET_WIDTH)
    return (y + b_f.astype(jnp.float32)).astype(u.dtype)

def lru_fourier_layer(h_lat, h_ctx, w_in, w_conv, b_conv, w_a, b_a, w_x, b_x, lam,
                      w_f, b_f, w_out, with_ctx_out):
    o1, o2, o3 = LRU_WIDTH, 2 * LRU_WIDTH, 2 * LRU_WIDTH + FNET_WIDTH
    z = h_lat @ w_in
    u_l, g_l, f_l, gf_l = z[..., :o1], z[..., o1:o2], z[..., o2:o3], z[..., o3:]
    if with_ctx_out:
        zc = h_ctx @ w_in
        u_c, g_c, f_c, gf_c = zc[..., :o1], zc[..., o1:o2], zc[..., o2:o3], zc[..., o3:]
    else:
        u_c = h_ctx @ w_in[:, :o1]
    u_l = centred_depthwise_conv(u_l, w_conv, b_conv)
    u_c = centred_depthwise_conv(u_c, w_conv, b_conv)
    r_l, r_c = rglru_bidirectional(u_l, u_c, w_a, b_a, w_x, b_x, lam)
    mix_l = jnp.concatenate([r_l * jax.nn.silu(g_l), fourier_mix(f_l, w_f, b_f) * jax.nn.silu(gf_l)], axis=-1)
    y_lat = mix_l @ w_out
    y_ctx = None
    if with_ctx_out:
        mix_c = jnp.concatenate([r_c * jax.nn.silu(g_c), fourier_mix(f_c, w_f, b_f) * jax.nn.silu(gf_c)], axis=-1)
        y_ctx = mix_c @ w_out
    return y_lat, y_ctx

def axial_rope_tables(n):
    t = jnp.arange(n)
    row = (t // GRID_W).astype(jnp.float32)
    col = (t % GRID_W).astype(jnp.float32)
    half = HEAD_DIM // 2
    freqs = ROPE_BASE ** (-jnp.arange(0, half, 2, dtype=jnp.float32) / half)
    ar = row[:, None] * freqs[None, :]
    ac = col[:, None] * freqs[None, :]
    return jnp.cos(ar), jnp.sin(ar), jnp.cos(ac), jnp.sin(ac)

def rope_1d(x, cos, sin):
    x1, x2 = jnp.split(x, 2, axis=-1)
    cos = cos[None, :, None, :].astype(x.dtype)
    sin = sin[None, :, None, :].astype(x.dtype)
    return jnp.concatenate([x1 * cos - x2 * sin, x2 * cos + x1 * sin], axis=-1)

def axial_rope(x, cos_r, sin_r, cos_c, sin_c):
    half = HEAD_DIM // 2
    return jnp.concatenate([rope_1d(x[..., :half], cos_r, sin_r),
                            rope_1d(x[..., half:], cos_c, sin_c)], axis=-1)

def window_gqa_layer(h_lat, h_ctx, w_in, sink, w_out, with_ctx_out):
    bsz, n, _ = h_lat.shape
    n_ctx = h_ctx.shape[1]
    nb = n // BLOCK
    scale = HEAD_DIM ** -0.5
    o1, o2, o3 = Q_WIDTH, Q_WIDTH + KV_WIDTH, Q_WIDTH + 2 * KV_WIDTH
    z = h_lat @ w_in
    q = z[..., :o1].reshape(bsz, n, N_Q_HEADS, HEAD_DIM)
    k = z[..., o1:o2].reshape(bsz, n, N_KV_HEADS, HEAD_DIM)
    v = z[..., o2:o3].reshape(bsz, n, N_KV_HEADS, HEAD_DIM)
    g = z[..., o3:]
    cos_r, sin_r, cos_c, sin_c = axial_rope_tables(n)
    q = axial_rope(q, cos_r, sin_r, cos_c, sin_c)
    k = axial_rope(k, cos_r, sin_r, cos_c, sin_c)
    zc = h_ctx @ w_in[:, o1:o3]
    k_c = zc[..., :KV_WIDTH].reshape(bsz, n_ctx, N_KV_HEADS, HEAD_DIM)
    v_c = zc[..., KV_WIDTH:].reshape(bsz, n_ctx, N_KV_HEADS, HEAD_DIM)
    sink_f = sink.astype(jnp.float32).reshape(1, 1, N_KV_HEADS, GQA_GROUP, 1, 1)

    qb = q.reshape(bsz, nb, BLOCK, N_KV_HEADS, GQA_GROUP, HEAD_DIM)
    pad = ((0, 0), (BLOCK, BLOCK), (0, 0), (0, 0))
    kp = jnp.pad(k, pad).reshape(bsz, nb + 2, BLOCK, N_KV_HEADS, HEAD_DIM)
    vp = jnp.pad(v, pad).reshape(bsz, nb + 2, BLOCK, N_KV_HEADS, HEAD_DIM)
    kw = jnp.concatenate([kp[:, :-2], kp[:, 1:-1], kp[:, 2:]], axis=2)
    vw = jnp.concatenate([vp[:, :-2], vp[:, 1:-1], vp[:, 2:]], axis=2)
    s_lat = jnp.einsum('bnqkgd,bnskd->bnkgqs', qb, kw).astype(jnp.float32) * scale
    blk = jnp.arange(nb)[:, None, None]
    qpos = blk * BLOCK + jnp.arange(BLOCK)[None, :, None]
    kpos = (blk - 1) * BLOCK + jnp.arange(3 * BLOCK)[None, None, :]
    valid = (jnp.abs(qpos - kpos) <= WINDOW) & (kpos >= 0) & (kpos < n)
    s_lat = jnp.where(valid[None, :, None, None], s_lat, NEG_INF)
    s_ctx = jnp.einsum('bnqkgd,bskd->bnkgqs', qb, k_c).astype(jnp.float32) * scale
    s_sink = jnp.broadcast_to(sink_f, s_lat.shape[:-1] + (1,))
    probs = jax.nn.softmax(jnp.concatenate([s_lat, s_ctx, s_sink], axis=-1), axis=-1)
    p_lat = probs[..., :3 * BLOCK].astype(v.dtype)
    p_ctx = probs[..., 3 * BLOCK:3 * BLOCK + n_ctx].astype(v.dtype)
    o = (jnp.einsum('bnkgqs,bnskd->bnqkgd', p_lat, vw)
         + jnp.einsum('bnkgqs,bskd->bnqkgd', p_ctx, v_c)).reshape(bsz, n, Q_WIDTH)
    y_lat = (o * jax.nn.silu(g)) @ w_out

    y_ctx = None
    if with_ctx_out:
        q_c = (h_ctx @ w_in[:, :o1]).reshape(bsz, n_ctx, N_KV_HEADS, GQA_GROUP, HEAD_DIM)
        g_c = h_ctx @ w_in[:, o3:]
        s_c = jnp.einsum('bqkgd,bskd->bkgqs', q_c, k_c).astype(jnp.float32) * scale
        s_cs = jnp.broadcast_to(sink_f[0], s_c.shape[:-1] + (1,))
        pr = jax.nn.softmax(jnp.concatenate([s_c, s_cs], axis=-1), axis=-1)[..., :n_ctx]
        o_c = jnp.einsum('bkgqs,bskd->bqkgd', pr.astype(v_c.dtype), v_c).reshape(bsz, n_ctx, Q_WIDTH)
        y_ctx = (o_c * jax.nn.silu(g_c)) @ w_out
    return y_lat, y_ctx

def setup_inputs(seed: int = 0) -> dict:
    key = jax.random.key(seed)
    ks = jax.random.split(key, 32)
    f32 = jnp.float32
    d = D_MODEL

    def nrm(k, shape, s):
        return jax.random.normal(k, shape, f32) * s

    a0 = jax.random.uniform(ks[13], (2, LRU_WIDTH), f32, 0.9, 0.999)
    return {
        "x": nrm(ks[0], (BATCH, SEQ, d), 1.0),
        "c": nrm(ks[1], (BATCH, d), 1.0),
        "ctx": nrm(ks[2], (BATCH, CTX_LEN, d), 1.0),
        "c_ctx": nrm(ks[3], (d,), 1.0),
        "l0_w_mod": nrm(ks[4], (d, 3 * d), 0.5 * d ** -0.5),
        "l0_b_mod": nrm(ks[5], (3 * d,), 0.01),
        "l0_g_pre": 1.0 + nrm(ks[6], (d,), 0.05),
        "l0_g_post": 1.0 + nrm(ks[7], (d,), 0.05),
        "l0_w_in": nrm(ks[8], (d, L0_IN_WIDTH), d ** -0.5),
        "l0_w_conv": nrm(ks[9], (CONV_W, LRU_WIDTH), CONV_W ** -0.5),
        "l0_b_conv": nrm(ks[10], (LRU_WIDTH,), 0.01),
        "l0_w_a": nrm(ks[11], (2, LRU_HEADS, LRU_BLOCK, LRU_BLOCK), LRU_BLOCK ** -0.5),
        "l0_b_a": nrm(ks[12], (2, LRU_WIDTH), 0.01),
        "l0_w_x": nrm(ks[14], (2, LRU_HEADS, LRU_BLOCK, LRU_BLOCK), LRU_BLOCK ** -0.5),
        "l0_b_x": nrm(ks[15], (2, LRU_WIDTH), 0.01),
        "l0_lam": jnp.log(a0) - jnp.log1p(-a0),
        "l0_w_f": nrm(ks[16], (FNET_GROUPS, FNET_GROUP_DIM, FNET_GROUP_DIM), FNET_GROUP_DIM ** -0.5),
        "l0_b_f": nrm(ks[17], (FNET_WIDTH,), 0.01),
        "l0_w_out": nrm(ks[18], (L0_MIX_WIDTH, d), L0_MIX_WIDTH ** -0.5),
        "l1_w_mod": nrm(ks[19], (d, 3 * d), 0.5 * d ** -0.5),
        "l1_b_mod": nrm(ks[20], (3 * d,), 0.01),
        "l1_g_pre": 1.0 + nrm(ks[21], (d,), 0.05),
        "l1_g_post": 1.0 + nrm(ks[22], (d,), 0.05),
        "l1_w_in": nrm(ks[23], (d, L1_IN_WIDTH), d ** -0.5),
        "l1_sink": nrm(ks[24], (N_Q_HEADS,), 1.0),
        "l1_w_out": nrm(ks[25], (Q_WIDTH, d), Q_WIDTH ** -0.5),
    }

def reference(x, c, ctx, c_ctx,
              l0_w_mod, l0_b_mod, l0_g_pre, l0_g_post, l0_w_in, l0_w_conv, l0_b_conv,
              l0_w_a, l0_b_a, l0_w_x, l0_b_x, l0_lam, l0_w_f, l0_b_f, l0_w_out,
              l1_w_mod, l1_b_mod, l1_g_pre, l1_g_post, l1_w_in, l1_sink, l1_w_out):
    layers = (
        dict(w_mod=l0_w_mod, b_mod=l0_b_mod, g_pre=l0_g_pre, g_post=l0_g_post),
        dict(w_mod=l1_w_mod, b_mod=l1_b_mod, g_pre=l1_g_pre, g_post=l1_g_post),
    )
    for layer in range(DEPTH):
        p = layers[layer]
        with_ctx_out = layer < DEPTH - 1
        sh_l, sc_l, gt_l = modulation(c, p["w_mod"], p["b_mod"])
        sh_c, sc_c, gt_c = modulation(c_ctx, p["w_mod"], p["b_mod"])
        h_lat = rms_norm(x, p["g_pre"]) * (1.0 + sc_l[:, None, :]) + sh_l[:, None, :]
        h_ctx = rms_norm(ctx, p["g_pre"]) * (1.0 + sc_c) + sh_c
        if layer % 2 == 0:
            y_lat, y_ctx = lru_fourier_layer(h_lat, h_ctx, l0_w_in, l0_w_conv, l0_b_conv,
                                             l0_w_a, l0_b_a, l0_w_x, l0_b_x, l0_lam,
                                             l0_w_f, l0_b_f, l0_w_out, with_ctx_out)
        else:
            y_lat, y_ctx = window_gqa_layer(h_lat, h_ctx, l1_w_in, l1_sink, l1_w_out, with_ctx_out)
        x = x + gt_l[:, None, :] * rms_norm(y_lat, p["g_post"])
        if with_ctx_out:
            ctx = ctx + gt_c * rms_norm(y_ctx, p["g_post"])
    return x


_drawn_inputs = setup_inputs


def setup_inputs(seed=0):
    import zlib

    import numpy as np

    out = dict(_drawn_inputs(seed))
    spreads = {}
    factors = {'l0_b_mod': 4.203,
     'l0_g_pre': 3.086,
     'l0_g_post': 3.997,
     'l0_b_conv': 7.328,
     'l0_b_a': 8.0,
     'l0_b_x': 8.0,
     'l0_b_f': 8.0,
     'l1_b_mod': 3.67,
     'l1_g_pre': 2.893,
     'l1_g_post': 3.944,
     'l1_sink': 64.0}
    for name, (base, spread) in spreads.items():
        noise = np.random.default_rng([zlib.crc32(name.encode()), seed]).standard_normal(out[name].shape)
        drawn = base * np.exp(spread * noise) if base else spread * noise
        out[name] = __import__('jax').numpy.asarray(drawn.astype(out[name].dtype))
    for name, factor in factors.items():
        out[name] = (out[name] * factor).astype(out[name].dtype)
    return out
```

```python
import numpy as np
from contextlib import ExitStack

import concourse.bass as bass
from concourse import mybir

F32 = mybir.dt.float32
F32R = mybir.dt.float32r
ALU = mybir.AluOpType
ACT = mybir.ActivationFunctionType
AX = mybir.AxisListType

P = 128
D = 1024
KT = D // P
N_LAT, N_CTX = 1024, 256
T = N_LAT + N_CTX
TT = T // P
LT = N_LAT // P
EPS = 1e-6
CHUNKS = [(0, 512), (512, 512), (1024, 256)]
GRID_W = 64
HEAD = 64
N_HEADS, N_KV = 16, 4
ROPE_BASE = 10000.0
NEG_INF = -1e30
SCALE = HEAD ** -0.5

CONV_W, CONV_LEFT = 4, 2
CTX_AT = N_LAT + CONV_LEFT
CONV_N = CTX_AT + N_CTX

RAD = N_LAT // P
N_R = RAD // 2 + 1
TAB_AT = {0: 0, 4: 256, 1: 512, 2: 896, 3: 1280, "c0": 1664, "c1": 1920}
TAB_N = 2176
PQ_N = (N_R + 2) * 256
UV_N = (N_R + 2) * P

MOD_C = 192
ROWS = 5 * D

C_CONV, C_BCONV, C_BA, C_BX, C_LAM, C_BF, N_COLS = 0, 4, 5, 7, 9, 11, 12
C_HALF, C_KPOS, C_KNEG, C_KNEG2, ALL_COLS = 12, 16, 18, 20, 22


def v32(ap):
    return ap.bitcast(F32)


def with_semaphores(nc, a, stages):
    used = []

    def sem(name):
        used.append(nc.alloc_semaphore(name=name))
        return used[-1]

    a["sem"] = sem
    stages()
    nc.clear_and_free_semaphores(used)
    nc.all_engine_barrier()


def layer0(nc, a):
    ctx = ExitStack()
    with ctx:
        def sb(name, shape, dt=F32):
            return ctx.enter_context(nc.sbuf_tensor(name, shape, dt))

        sem = a["sem"]

        h_hi, h_lo = sb("h_hi", [P, KT, T], F32R), sb("h_lo", [P, KT, T], F32R)
        cols = sb("cols", [P, ALL_COLS, KT])
        silu_c = sb("silu_c", [P, KT, 2])
        setup(nc, a, h_hi, h_lo, cols, silu_c)
        mixers(nc, a, h_hi, h_lo, cols, silu_c)


def setup(nc, a, h_hi, h_lo, cols, silu_c):
    ctx = ExitStack()
    with ctx:
        def sb(name, shape, dt=F32):
            return ctx.enter_context(nc.sbuf_tensor(name, shape, dt))

        sem = a["sem"]

        xt = sb("xt", [P, 2, D])
        junk = sb("junk", [P, D])
        xn = sb("xn", [P, 2, D])
        stat = sb("stat", [P, 3, TT])
        xT = sb("xT", [P, KT, T])
        ident = sb("ident0", [P, P])
        cvec = sb("cvec", [P, KT, 2])
        th_c = sb("th_c", [P, KT, 2])
        wm = sb("wm", [P, 2, 3 * D])
        rows = sb("rows", [2, ROWS])
        mod = sb("mod", [2, 3 * D])
        gs = sb("gs", [P, 2, KT, 2])
        sp_t = sb("sp_t", [P, 6, 2 * KT])
        eps = sb("eps0", [P, 1])
        pm = ctx.enter_context(nc.psum_tensor("pm", [2, 3 * D], F32))
        pt = ctx.enter_context(nc.psum_tensor("pt", [P, 2, 4, P], F32))

        par = sem("par_loaded")
        x_ld = [sem("x_loaded0"), sem("x_loaded1")]
        wm_ld = [sem("wm_loaded0"), sem("wm_loaded1")]
        ss, rt, rs, xs = sem("ss_done"), sem("root_done"), sem("rstd_done"), sem("xn_done")
        tr, te = sem("x_transposed"), sem("xT_written")
        kstep = sem("k_step")
        thc, sc_ = sem("tanh_c"), sem("silu_c_done")
        modk, mrow, mtr, gsd = sem("mod_k_done"), sem("mod_row_done"), sem("mod_transposed"), sem("gs_done")
        hh, h32, hl = sem("h_hi_done"), sem("h32_done"), sem("h_lo_done")
        spre, spost = sem("exp_lam_in"), sem("exp_lam")
        gst, est = sem("gate_row_stored"), sem("eps_set")
        blk = ctx.enter_context(nc.Block())

        def x_tile(i):
            return a["x"][i * P:(i + 1) * P, :]

        @blk.sync
        def _(sp):
            sp.dma_start(cvec[:], a["cvec"]).then_inc(par, 16)
            sp.dma_start(rows[:], a["rows0"]).then_inc(par, 16)
            sp.dma_start(cols[:, 0:N_COLS, :], a["cols"]).then_inc(par, 16)
            sp.dma_start(ident[:], a["ident"]).then_inc(par, 16)
            for i in range(TT):
                if i >= 2:
                    sp.wait_ge(xs, i - 1)
                sp.dma_start(xt[:, i % 2, :], x_tile(i)).then_inc(x_ld[i % 2], 16)
                if i < KT:
                    if i >= 2:
                        sp.wait_ge(modk, i - 1)
                    sp.dma_start(wm[:, i % 2, :], a["wm0"][i * P:(i + 1) * P, :]).then_inc(wm_ld[i % 2], 16)
            sp.wait_ge(mrow, 9)
            sp.dma_start(a["gp"][0], mod[:, 2 * D:3 * D]).then_inc(gst, 16)
            sp.wait_ge(gst, 16)

        @blk.scalar
        def _(act):
            act.wait_ge(par, 64)
            nc.scalar.activation(th_c[:], cvec[:], ACT.Tanh, scale=0.5).then_inc(thc, 1)
            act.wait_ge(spre, 1)
            nc.scalar.activation(sp_t[:, 1, :], sp_t[:, 0, :], ACT.Exp).then_inc(spost, 1)
            act.wait_ge(est, 1)
            for i in range(TT):
                act.wait_ge(x_ld[i % 2], 16 * (i // 2 + 1))
                nc.scalar.activation(junk[:], xt[:, i % 2, :], ACT.Square,
                                     accum_out=stat[:, 0, i:i + 1]).then_inc(ss, 1)
                act.wait_ge(ss, i + 1)
                nc.scalar.activation(stat[:, 1, i:i + 1], stat[:, 0, i:i + 1], ACT.Sqrt,
                                     bias=eps[:, 0:1], scale=1.0 / D).then_inc(rt, 1)
                if i >= 1:
                    for h in range(2):
                        act.wait_ge(tr, 2 * (i - 1) + h + 1)
                        nc.scalar.activation(xT[:, 4 * h:4 * h + 4, (i - 1) * P:i * P], pt[:, h, :, :],
                                             ACT.Copy).then_inc(te, 1)
            for h in range(2):
                act.wait_ge(tr, 2 * (TT - 1) + h + 1)
                nc.scalar.activation(xT[:, 4 * h:4 * h + 4, (TT - 1) * P:TT * P], pt[:, h, :, :],
                                     ACT.Copy).then_inc(te, 1)
            act.wait_ge(te, 2 * TT)
            act.wait_ge(gsd, 1)
            for k in range(KT):
                for w, (at, n) in enumerate([(0, N_LAT), (N_LAT, N_CTX)]):
                    nc.scalar.activation(h_hi[:, k, at:at + n], xT[:, k, at:at + n], ACT.Identity,
                                         scale=gs[:, 1, k, w:w + 1], bias=gs[:, 0, k, w:w + 1]).then_inc(hh, 1)

        @blk.vector
        def _(dve):
            nc.vector.memset(eps[:], EPS).then_inc(est, 1)
            dve.wait_ge(par, 64)
            n = [0]

            def step(ins):
                n[0] += 1
                ins.then_inc(kstep, 1)
                dve.wait_ge(kstep, n[0])

            lam = cols[:, C_LAM:C_LAM + 2, :].rearrange("p a k -> p (a k)")
            step(nc.vector.tensor_scalar(sp_t[:, 2, :], lam, -1.0, None, ALU.mult))
            nc.vector.tensor_tensor(sp_t[:, 0, :], sp_t[:, 2, :], lam, ALU.min).then_inc(spre, 1)
            step(nc.vector.tensor_scalar(cols[:, C_HALF:C_HALF + 4, :].rearrange("p a k -> p (a k)"),
                                         cols[:, C_BA:C_BA + 4, :].rearrange("p a k -> p (a k)"),
                                         0.5, None, ALU.mult))
            dve.wait_ge(spost, 1)
            step(nc.vector.tensor_scalar(sp_t[:, 3, :], sp_t[:, 1, :], 2.0, None, ALU.add))
            step(nc.vector.reciprocal(sp_t[:, 3, :], sp_t[:, 3, :]))
            step(nc.vector.tensor_tensor(sp_t[:, 3, :], sp_t[:, 1, :], sp_t[:, 3, :], ALU.mult))
            step(nc.vector.tensor_tensor(sp_t[:, 4, :], sp_t[:, 3, :], sp_t[:, 3, :], ALU.mult))
            step(nc.vector.tensor_scalar(sp_t[:, 5, :], sp_t[:, 4, :], 1.0 / 17, 1.0 / 15, ALU.mult, ALU.add))
            for q in (13, 11, 9, 7, 5, 3, 1):
                step(nc.vector.tensor_tensor(sp_t[:, 5, :], sp_t[:, 5, :], sp_t[:, 4, :], ALU.mult))
                step(nc.vector.tensor_scalar(sp_t[:, 5, :], sp_t[:, 5, :], 1.0 / q, None, ALU.add))
            step(nc.vector.scalar_tensor_tensor(out=sp_t[:, 5, :], in0=sp_t[:, 5, :], scalar=2.0,
                                                in1=sp_t[:, 3, :], op0=ALU.mult, op1=ALU.mult))
            step(nc.vector.scalar_tensor_tensor(out=sp_t[:, 5, :], in0=sp_t[:, 2, :], scalar=0.0,
                                                in1=sp_t[:, 5, :], op0=ALU.max, op1=ALU.add))
            for at, f in ((C_KPOS, 4.0), (C_KNEG, -4.0), (C_KNEG2, -8.0)):
                step(nc.vector.tensor_scalar(cols[:, at:at + 2, :].rearrange("p a k -> p (a k)"), sp_t[:, 5, :], f, None,
                                             ALU.mult))
            dve.wait_ge(thc, 1)
            step(nc.vector.scalar_tensor_tensor(out=silu_c[:], in0=th_c[:], scalar=1.0, in1=cvec[:],
                                                op0=ALU.add, op1=ALU.mult))
            nc.vector.tensor_scalar(silu_c[:], silu_c[:], 0.5, None, ALU.mult).then_inc(sc_, 1)
            for i in range(TT):
                dve.wait_ge(rt, i + 1)
                nc.vector.reciprocal(stat[:, 2, i:i + 1], stat[:, 1, i:i + 1]).then_inc(rs, 1)
                dve.wait_ge(rs, i + 1)
                if i >= 2:
                    dve.wait_ge(tr, 2 * (i - 1))
                nc.vector.tensor_scalar(xn[:, i % 2, :], xt[:, i % 2, :], stat[:, 2, i:i + 1], None,
                                        ALU.mult).then_inc(xs, 1)
            dve.wait_ge(modk, KT)
            for c in range(6):
                nc.vector.tensor_tensor(mod[:, c * 512:(c + 1) * 512], pm[:, c * 512:(c + 1) * 512],
                                        rows[:, c * 512:(c + 1) * 512], ALU.add).then_inc(mrow, 1)
            dve.wait_ge(mrow, 6)
            nc.vector.scalar_tensor_tensor(out=mod[:, D:2 * D], in0=mod[:, D:2 * D], scalar=1.0,
                                           in1=rows[:, 3 * D:4 * D], op0=ALU.add, op1=ALU.mult).then_inc(mrow, 1)
            dve.wait_ge(mtr, 1)
            nc.vector.tensor_copy(gs[:].rearrange("p a k w -> p (a k w)"), pm_cols(pt)).then_inc(gsd, 1)
            nc.vector.tensor_tensor(mod[:, 2 * D:3 * D], mod[:, 2 * D:3 * D], rows[:, 4 * D:5 * D],
                                    ALU.mult).then_inc(mrow, 2)
            dve.wait_ge(te, 2 * TT)
            dve.wait_ge(gsd, 1)
            for k in range(KT):
                dve.wait_ge(hh, 2 * k + 2)
                for w, (at, n_) in enumerate([(0, N_LAT), (N_LAT, N_CTX)]):
                    nc.vector.tensor_scalar(xT[:, k, at:at + n_], xT[:, k, at:at + n_], gs[:, 1, k, w:w + 1],
                                            gs[:, 0, k, w:w + 1], ALU.mult, ALU.add).then_inc(h32, 1)
                if k % 2 == 1:
                    dve.wait_ge(h32, 2 * k + 2)
                    nc.vector.tensor_tensor(h_lo[:, k, :], xT[:, k, :], v32(h_hi[:, k, :]),
                                            ALU.subtract).then_inc(hl, 1)

        @blk.gpsimd
        def _(pool):
            for k in range(0, KT, 2):
                pool.wait_ge(h32, 2 * k + 2)
                nc.gpsimd.tensor_tensor(h_lo[:, k, :], xT[:, k, :], v32(h_hi[:, k, :]), ALU.subtract).then_inc(hl, 1)

        @blk.tensor
        def _(pe):
            pe.wait_ge(sc_, 1)
            for i in range(TT):
                pe.wait_ge(xs, i + 1)
                for h in range(2):
                    if i >= 1:
                        pe.wait_ge(te, 2 * (i - 1) + h + 1)
                    for q in range(4):
                        last = nc.tensor.transpose(pt[:, h, q, :], xn[:, i % 2, (4 * h + q) * P:(4 * h + q + 1) * P],
                                                   ident[:])
                    last.then_inc(tr, 1)
                if i < KT:
                    pe.wait_ge(wm_ld[i % 2], 16 * (i // 2 + 1))
                    for c in range(6):
                        last = nc.tensor.matmul(pm[:, c * 512:(c + 1) * 512], silu_c[:, i, :],
                                                wm[:, i % 2, c * 512:(c + 1) * 512], start=(i == 0), stop=(i == KT - 1))
                    last.then_inc(modk, 1)
            pe.wait_ge(te, 2 * TT)
            pe.wait_ge(mrow, 7)
            for q in range(2 * KT):
                last = nc.tensor.transpose(pt[:, 0, 0, 2 * q:2 * q + 2], mod[:, q * P:(q + 1) * P], ident[0:2, 0:2])
            last.then_inc(mtr, 1)


def pm_cols(pt):
    return pt[:, 0, 0, 0:4 * KT]


def mixers(nc, a, h_hi, h_lo, cols, silu_c):
    ctx = ExitStack()
    with ctx:
        def sb(name, shape, dt=F32):
            return ctx.enter_context(nc.sbuf_tensor(name, shape, dt))

        sem = a["sem"]

        wraw = sb("wraw", [P, 2, D])
        w_hi, w_lo = sb("w_hi", [P, 2, KT, P], F32R), sb("w_lo", [P, 2, KT, P], F32R)
        tab_hi, tab_lo = sb("tab_hi", [P, TAB_N], F32R), sb("tab_lo", [P, TAB_N], F32R)
        dft_ch = sb("dft_ch", [P, 256])
        ident = sb("ident1", [P, P])
        u_raw = sb("u_raw", [P, CONV_N + CONV_W - 1])
        u = sb("u", [P, T])
        u_hi, u_lo = sb("u_hi", [P, T], F32R), sb("u_lo", [P, T], F32R)
        cur = sb("cur", [P, ALL_COLS])
        gw = sb("gw", [P, 4, P])
        gw_hi, gw_lo = sb("gw_hi", [P, 4, P], F32R), sb("gw_lo", [P, 4, P], F32R)
        A, B, C = sb("A", [P, T]), sb("B", [P, T]), sb("C", [P, T])
        E = sb("E", [P, CONV_N])
        H = sb("H", [P, T])
        sgf = sb("sgf", [P, T])
        fT = sb("fT", [P, T])
        xf = sb("xf", [P, T])
        y_hi, y_lo = sb("y_hi", [P, T], F32R), sb("y_lo", [P, T], F32R)
        pq_hi, pq_lo = sb("pq_hi", [P, PQ_N], F32R), sb("pq_lo", [P, PQ_N], F32R)
        wf = sb("wf", [P, P])
        ab_hi, ab_lo = sb("ab_hi", [P, 2 * P], F32R), sb("ab_lo", [P, 2 * P], F32R)
        wm1 = sb("wm1", [P, KT, MOD_C])
        m_row = sb("m_row", [2, MOD_C])
        slab = ctx.enter_context(nc.psum_tensor("slab", [P, 3, 512], F32))
        W = ctx.enter_context(nc.psum_tensor("W", [P, 4, 512], F32))
        W4 = ctx.enter_context(nc.psum_tensor("W4", [P, 512], F32))
        Wf = W[:].rearrange("p b n -> p (b n)")

        par = sem("mix_par_loaded")
        tab_ld, tab_h, tab_l = sem("table_loaded"), sem("table_hi"), sem("table_lo")
        zero, cu_ = sem("zeros_set"), sem("columns_copied")
        w_ld = [sem("w_loaded0"), sem("w_loaded1")]
        wh = [sem("w_hi_done0"), sem("w_hi_done1")]
        wl = [sem("w_lo_done0"), sem("w_lo_done1")]
        gw_ld, gwh, gwl = sem("gate_w_loaded"), sem("gate_w_hi"), sem("gate_w_lo")
        wf_ld, abp, abh, abl = sem("wf_loaded"), sem("ab_product"), sem("ab_hi_done"), sem("ab_lo_done")
        s_u, s_f, s_gf, s_g = sem("slab_u"), sem("slab_f"), sem("slab_gf"), sem("slab_g")
        ur, tap0, taps, conv = sem("u_raw_ready"), sem("tap0"), sem("taps"), sem("conv_done")
        uh, ul = sem("u_hi_done"), sem("u_lo_done")
        fr, trd, xr = sem("fT_ready"), sem("f_transposed"), sem("x_ready")
        bf, yr, yh, yl = sem("butterfly"), sem("y_ready"), sem("y_hi_done"), sem("y_lo_done")
        dft, pqh, pql, uv, us, yd = sem("dft_done"), sem("pq_hi"), sem("pq_lo"), sem("uv_done"), sem("us_ready"), sem("y_combined")
        tgf, sgfd, tg, sg = sem("tanh_gf"), sem("silu_gf"), sem("tanh_g"), sem("silu_g")
        gp_, gr = sem("gate_product"), sem("gate_read")
        th, e2, ea = sem("tanh_loga"), sem("a_squared"), sem("a_ready")
        iu, om, sq, bt, hd, hs = sem("iu"), sem("one_minus_a2"), sem("root"), sem("b_ready"), sem("scan_done"), sem("h_sum")
        cf = sem("scan_ctx")
        mf, mr, mfs, mrs = sem("mix_f"), sem("mix_r"), sem("mix_f_stored"), sem("mix_r_stored")
        m_ld, mp, me, ms = sem("wmod1_loaded"), sem("mod1_product"), sem("mod1_row"), sem("mod1_stored")
        blk = ctx.enter_context(nc.Block())
        SLAB_U, SLAB_F, SLAB_GF, SLAB_G = range(4)
        done = [s_u, s_f, s_gf, s_g]
        tab_pieces = [(0, 1024), (1024, 1024), (2048, TAB_N - 2048)]

        def loops(eng, body, n=KT):
            body(0, True, False)
            with eng.Fori(1, n - 1) as t:
                body(t, False, False)
            body(n - 1, False, True)

        @blk.sync
        def _(sp):
            sp.dma_start(dft_ch[:], a["dft_ch"]).then_inc(par, 16)
            sp.dma_start(ident[:], a["ident"]).then_inc(par, 16)

            def load_slab(t, j, first):
                if not (first and j < 2):
                    sp.wait_ge(wl[j % 2], 2 * t + j // 2)
                sp.dma_start(wraw[:, j % 2, :], a["w_in0"][4 * t + j]).then_inc(w_ld[j % 2], 16)

            def store(t):
                sp.wait_ge(mr, t + 1)
                sp.dma_start(a["mixT"][t], H[:]).then_inc(mrs, 16)
                sp.wait_ge(mf, t + 1)
                sp.dma_start(a["mixT"][t + KT], xf[:]).then_inc(mfs, 16)
                store_mod(t, 1)

            def store_mod(t, q):
                sp.wait_ge(me, 2 * t + q + 1)
                sp.dma_start(a["mod1"][:, 2 * t + q, :], m_row[:]).then_inc(ms, 16)

            def load_mod(t, q, first):
                if not (first and q == 0):
                    sp.wait_ge(mp, 2 * t + q)
                sp.dma_start(wm1[:], a["wm1"][2 * t + q]).then_inc(m_ld, 16)

            def body(t, first, last):
                if first:
                    load_slab(t, SLAB_U, first)
                    load_slab(t, SLAB_F, first)
                    for i, (at, n) in enumerate(tab_pieces):
                        if i:
                            sp.wait_ge(tab_l, i)
                        sp.dma_start(fT[:, 0:n], a["tables"][:, at:at + n]).then_inc(tab_ld, 16)
                load_mod(t, 0, first)
                if first:
                    sp.wait_ge(zero, 2)
                else:
                    sp.wait_ge(gwl, t)
                for c in range(2):
                    sp.dma_start(gw[HEAD * c:HEAD * (c + 1), :, HEAD * c:HEAD * (c + 1)],
                                 a["w_gate"][t, HEAD * c:HEAD * (c + 1), :, :]).then_inc(gw_ld, 16)
                if not first:
                    sp.wait_ge(abp, t)
                sp.dma_start(wf[:], a["w_f"][t]).then_inc(wf_ld, 16)
                load_slab(t, SLAB_GF, first)
                load_slab(t, SLAB_G, first)
                if not first:
                    store(t - 1)
                store_mod(t, 0)
                load_mod(t, 1, first)
                if not last:
                    load_slab(t + 1, SLAB_U, False)
                    load_slab(t + 1, SLAB_F, False)

            loops(sp, body)
            store(KT - 1)
            sp.wait_ge(mrs, 16 * KT)
            sp.wait_ge(mfs, 16 * KT)
            sp.wait_ge(ms, 32 * KT)

        @blk.scalar
        def _(act):
            def split_hi(t, j, first=False):
                act.wait_ge(w_ld[j % 2], 16 * (2 * t + j // 2 + 1))
                if j >= 2:
                    act.wait_ge(done[j - 2], 3 * t + 3)
                elif not first:
                    act.wait_ge(done[j + 2], 3 * t)
                nc.scalar.activation(w_hi[:, j % 2].rearrange("p k n -> p (k n)"), wraw[:, j % 2, :],
                                     ACT.Copy).then_inc(wh[j % 2], 1)

            def gates(t, d, first):
                for x in range(2):
                    dst = (A, B)[x]
                    if x == 0:
                        if d == 1:
                            act.wait_ge(hd, 2 * t + 1)
                        elif not first:
                            act.wait_ge(mr, t)
                    for c, (at, n) in enumerate(CHUNKS):
                        k = 6 * d + 3 * x + c
                        act.wait_ge(gp_, 12 * t + k + 1)
                        nc.scalar.activation(dst[:, at:at + n], W[:, k % 4, 0:n], ACT.Tanh, scale=0.5,
                                             bias=cur[:, C_HALF + 2 * x + d:C_HALF + 2 * x + d + 1]).then_inc(gr, 1)
                act.wait_ge(gr, 12 * t + 6 * d + 3)
                if d == 0:
                    act.wait_ge(conv, 2 * t + 2)
                else:
                    act.wait_ge(bt, 2 * t + 1)
                nc.scalar.activation(E[:, 0:T], A[:], ACT.Tanh, scale=cur[:, C_KPOS + d:C_KPOS + d + 1],
                                     bias=cur[:, C_KPOS + d:C_KPOS + d + 1]).then_inc(th, 1)
                nc.scalar.activation(C[:], A[:], ACT.Exp, scale=cur[:, C_KNEG2 + d:C_KNEG2 + d + 1],
                                     bias=cur[:, C_KNEG2 + d:C_KNEG2 + d + 1]).then_inc(e2, 1)
                act.wait_ge(e2, 2 * t + d + 1)
                act.wait_ge(th, 2 * t + d + 1)
                nc.scalar.activation(A[:], A[:], ACT.Exp, scale=cur[:, C_KNEG + d:C_KNEG + d + 1],
                                     bias=cur[:, C_KNEG + d:C_KNEG + d + 1]).then_inc(ea, 1)

            def root(t, d):
                act.wait_ge(om, 2 * t + d + 1)
                nc.scalar.activation(C[:], C[:], ACT.Sqrt).then_inc(sq, 1)

            def mod_row(t, q, first):
                act.wait_ge(mp, 2 * t + q + 1)
                if not (first and q == 0):
                    act.wait_ge(ms, 16 * (2 * t + q))
                nc.scalar.activation(m_row[:], W4[0:2, 0:MOD_C], ACT.Copy).then_inc(me, 1)

            def body(t, first, last):
                split_hi(t, SLAB_F, first)
                if first:
                    act.wait_ge(zero, 2)
                else:
                    act.wait_ge(conv, 2 * t)
                for c, (at, n) in enumerate(CHUNKS):
                    act.wait_ge(s_u, 3 * t + c + 1)
                    to = CONV_LEFT + at + (CTX_AT - N_LAT if c == 2 else 0)
                    nc.scalar.activation(u_raw[:, to:to + n], slab[:, c, 0:n], ACT.Copy).then_inc(ur, 1)
                if not first:
                    act.wait_ge(hs, t)
                act.wait_ge(ur, 3 * t + 3)
                act.wait_ge(cu_, t + 1)
                nc.scalar.activation(E[:], u_raw[:, 0:CONV_N], ACT.Identity, scale=cur[:, C_CONV:C_CONV + 1],
                                     bias=cur[:, C_BCONV:C_BCONV + 1]).then_inc(tap0, 1)
                mod_row(t, 0, first)
                split_hi(t, SLAB_GF)
                act.wait_ge(gw_ld, 32 * t + 32)
                if not first:
                    act.wait_ge(gp_, 12 * t)
                nc.scalar.activation(gw_hi[:], gw[:], ACT.Copy).then_inc(gwh, 1)
                act.wait_ge(conv, 2 * t + 2)
                nc.scalar.activation(u_hi[:], u[:], ACT.Copy).then_inc(uh, 1)
                if not first:
                    act.wait_ge(yd, t)
                else:
                    act.wait_ge(tab_l, 3)
                for c, (at, n) in enumerate(CHUNKS):
                    act.wait_ge(s_f, 3 * t + c + 1)
                    nc.scalar.activation(fT[:, at:at + n], slab[:, c, 0:n], ACT.Copy).then_inc(fr, 1)
                if not first:
                    act.wait_ge(mfs, 16 * t)
                for c, (at, n) in enumerate(CHUNKS):
                    act.wait_ge(trd, 3 * t + c + 1)
                    nc.scalar.activation(xf[:, at:at + n], W[:, c, 0:n], ACT.Copy).then_inc(xr, 1)
                act.wait_ge(abp, t + 1)
                nc.scalar.activation(ab_hi[:], W4[:, 0:256], ACT.Copy).then_inc(abh, 1)
                gates(t, 0, first)
                split_hi(t, SLAB_G)
                act.wait_ge(yr, t + 1)
                if not first:
                    act.wait_ge(dft, t)
                nc.scalar.activation(y_hi[:], xf[:], ACT.Copy).then_inc(yh, 1)
                root(t, 0)
                if not first:
                    act.wait_ge(mf, t)
                for c, (at, n) in enumerate(CHUNKS):
                    act.wait_ge(s_gf, 3 * t + c + 1)
                    nc.scalar.activation(sgf[:, at:at + n], slab[:, c, 0:n], ACT.Tanh, scale=0.5).then_inc(tgf, 1)
                gates(t, 1, first)
                act.wait_ge(dft, t + 1)
                if not first:
                    act.wait_ge(uv, t)
                nc.scalar.activation(pq_hi[:], Wf[:, 0:PQ_N], ACT.Copy).then_inc(pqh, 1)
                if not last:
                    split_hi(t + 1, SLAB_U)
                root(t, 1)
                act.wait_ge(hd, 2 * t + 2)
                for c, (at, n) in enumerate(CHUNKS):
                    act.wait_ge(s_g, 3 * t + c + 1)
                    nc.scalar.activation(B[:, at:at + n], slab[:, c, 0:n], ACT.Tanh, scale=0.5).then_inc(tg, 1)
                act.wait_ge(uv, t + 1)
                nc.scalar.activation(fT[:, 0:UV_N], Wf[:, 0:UV_N], ACT.Identity,
                                     bias=cur[:, C_BF:C_BF + 1]).then_inc(us, 1)
                mod_row(t, 1, first)

            split_hi(0, SLAB_U, True)
            for i, (at, n) in enumerate(tab_pieces):
                act.wait_ge(tab_ld, 16 * (i + 1))
                nc.scalar.activation(tab_hi[:, at:at + n], fT[:, 0:n], ACT.Copy).then_inc(tab_h, 1)
            loops(act, body)

        @blk.vector
        def _(dve):
            nc.vector.memset(u_raw[:], 0.0).then_inc(zero, 1)
            nc.vector.memset(gw[:], 0.0).then_inc(zero, 1)

            def body(t, first, last):
                if not first:
                    dve.wait_ge(us, t)
                nc.vector.tensor_scalar(cur[:], cols[:, :, t], 1.0, None, ALU.mult).then_inc(cu_, 1)
                dve.wait_ge(tap0, t + 1)
                for k in (1, 2):
                    nc.vector.scalar_tensor_tensor(out=E[:], in0=u_raw[:, k:k + CONV_N],
                                                   scalar=cur[:, C_CONV + k:C_CONV + k + 1], in1=E[:],
                                                   op0=ALU.mult, op1=ALU.add).then_inc(taps, 1)
                    dve.wait_ge(taps, 2 * t + k)
                if not first:
                    dve.wait_ge(ul, t)
                for at, to, n in ((0, 0, N_LAT), (CTX_AT, N_LAT, N_CTX)):
                    nc.vector.scalar_tensor_tensor(out=u[:, to:to + n], in0=u_raw[:, at + 3:at + 3 + n],
                                                   scalar=cur[:, C_CONV + 3:C_CONV + 4], in1=E[:, at:at + n],
                                                   op0=ALU.mult, op1=ALU.add).then_inc(conv, 1)
                nb = 8
                b0 = nb * t

                def q(buf, i, n=1):
                    return buf[:, i * P:(i + n) * P]

                def bstep(k, ins):
                    ins.then_inc(bf, 1)

                dve.wait_ge(xr, 3 * t + 3)
                tt = nc.vector.tensor_tensor
                bstep(1, tt(q(fT, 0, 4), q(xf, 0, 4), q(xf, 4, 4), ALU.add))
                bstep(2, tt(q(fT, 4, 4), q(xf, 0, 4), q(xf, 4, 4), ALU.subtract))
                bstep(3, tt(q(fT, 8), q(xf, 8), q(xf, 9), ALU.subtract))
                bstep(4, tt(q(fT, 9), q(xf, 8), q(xf, 9), ALU.add))
                dve.wait_ge(bf, b0 + 4)
                bstep(5, tt(q(xf, 6, 2), q(fT, 0, 2), q(fT, 2, 2), ALU.add))
                bstep(6, tt(q(xf, 4, 2), q(fT, 0, 2), q(fT, 2, 2), ALU.subtract))
                dve.wait_ge(bf, b0 + 6)
                bstep(7, tt(q(fT, 0), q(fT, 5), q(fT, 7), ALU.add))
                bstep(8, tt(q(fT, 1), q(fT, 5), q(fT, 7), ALU.subtract))
                dve.wait_ge(bf, b0 + 8)
                stt = nc.vector.scalar_tensor_tensor
                s = float(np.sqrt(0.5))
                tt(q(xf, 0), q(xf, 6), q(xf, 7), ALU.add).then_inc(bf2, 1)
                tt(q(xf, 1), q(xf, 6), q(xf, 7), ALU.subtract).then_inc(bf2, 1)
                stt(out=q(xf, 2), in0=q(fT, 1), scalar=s, in1=q(fT, 4), op0=ALU.mult, op1=ALU.add).then_inc(bf2, 1)
                stt(out=q(xf, 3), in0=q(fT, 0), scalar=s, in1=q(fT, 6), op0=ALU.mult, op1=ALU.add).then_inc(bf2, 1)
                dve.wait_ge(bf2, 4 * t + 4)
                stt(out=q(xf, 6), in0=q(fT, 1), scalar=-s, in1=q(fT, 4), op0=ALU.mult, op1=ALU.add).then_inc(bf3, 1)
                stt(out=q(xf, 7), in0=q(fT, 0), scalar=s, in1=q(fT, 6), op0=ALU.mult, op1=ALU.subtract).then_inc(bf3, 1)
                nc.vector.tensor_copy(q(xf, 8), q(fT, 9)).then_inc(bf3, 1)
                nc.vector.tensor_copy(q(xf, 9), q(fT, 8)).then_inc(yr, 1)
                dve.wait_ge(abh, t + 1)
                tt(ab_lo[:], W4[:, 0:256], v32(ab_hi[:]), ALU.subtract).then_inc(abl, 1)

                def direction(d):
                    dve.wait_ge(gr, 12 * t + 6 * d + 6)
                    stt(out=B[:], in0=B[:], scalar=1.0, in1=u[:], op0=ALU.add, op1=ALU.mult).then_inc(iu, 1)
                    dve.wait_ge(th, 2 * t + d + 1)
                    dve.wait_ge(e2, 2 * t + d + 1)
                    stt(out=C[:], in0=C[:], scalar=1.0, in1=E[:, 0:T], op0=ALU.add, op1=ALU.mult).then_inc(om, 1)

                def scan(d):
                    dve.wait_ge(sq, 2 * t + d + 1)
                    dve.wait_ge(iu, 2 * t + d + 1)
                    stt(out=B[:], in0=C[:], scalar=0.5, in1=B[:], op0=ALU.mult, op1=ALU.mult).then_inc(bt, 1)
                    dve.wait_ge(bt, 2 * t + d + 1)
                    dve.wait_ge(ea, 2 * t + d + 1)
                    if d == 0:
                        if not first:
                            dve.wait_ge(mrs, 16 * t)
                        nc.vector.tensor_tensor_scan(H[:, N_LAT:T], A[:, N_LAT:T], B[:, N_LAT:T], 0.0,
                                                     ALU.mult, ALU.add).then_inc(cf, 1)
                        dve.wait_ge(cf, t + 1)
                        nc.vector.tensor_tensor_scan(H[:, 0:N_LAT], A[:, 0:N_LAT], B[:, 0:N_LAT], H[:, T - 1:T],
                                                     ALU.mult, ALU.add).then_inc(hd, 1)
                    else:
                        nc.vector.tensor_tensor_scan(rev(E), rev(A), rev(B), 0.0,
                                                     ALU.mult, ALU.add).then_inc(hd, 1)

                direction(0)
                scan(0)
                for c, (at, n) in enumerate(CHUNKS):
                    dve.wait_ge(tgf, 3 * t + c + 1)
                    stt(out=sgf[:, at:at + n], in0=sgf[:, at:at + n], scalar=1.0, in1=slab[:, c, 0:n],
                        op0=ALU.add, op1=ALU.mult).then_inc(sgfd, 1)
                direction(1)
                dve.wait_ge(pqh, t + 1)
                tt(pq_lo[:], Wf[:, 0:PQ_N], v32(pq_hi[:]), ALU.subtract).then_inc(pql, 1)
                scan(1)
                for c, (at, n) in enumerate(CHUNKS):
                    dve.wait_ge(tg, 3 * t + c + 1)
                    stt(out=B[:, at:at + n], in0=B[:, at:at + n], scalar=1.0, in1=slab[:, c, 0:n],
                        op0=ALU.add, op1=ALU.mult).then_inc(sg, 1)
                dve.wait_ge(us, t + 1)
                dve.wait_ge(yl, t + 1)
                lat = xf[:, 0:N_LAT].rearrange("p (k r) -> p r k", r=RAD)
                cu = fT[:, 0:UV_N].rearrange("p (r k) -> p r k", k=P)
                sv = Wf[:, 2 * 512:2 * 512 + UV_N].rearrange("p (r k) -> p r k", k=P)
                tt(lat[:, 0:N_R, :], cu[:, 0:N_R, :], sv[:, 0:N_R, :], ALU.subtract).then_inc(yc, 1)
                for r in range(1, RAD - N_R + 1):
                    tt(lat[:, RAD - r, ::-1], cu[:, r, :], sv[:, r, :], ALU.add).then_inc(yc, 1)
                cx = xf[:, N_LAT:T].rearrange("p (k r) -> p r k", r=2)
                tt(cx, cu[:, N_R:N_R + 2, :], sv[:, N_R:N_R + 2, :], ALU.subtract).then_inc(yd, 1)
                dve.wait_ge(yc, 4 * t + 4)
                dve.wait_ge(yd, t + 1)
                dve.wait_ge(sgfd, 3 * t + 3)
                stt(out=xf[:], in0=xf[:], scalar=0.5, in1=sgf[:], op0=ALU.mult, op1=ALU.mult).then_inc(mf, 1)
                dve.wait_ge(hs, t + 1)
                dve.wait_ge(sg, 3 * t + 3)
                stt(out=H[:], in0=H[:], scalar=0.5, in1=B[:], op0=ALU.mult, op1=ALU.mult).then_inc(mr, 1)

            bf2, bf3, yc = sem("butterfly2"), sem("butterfly3"), sem("y_parts")
            loops(dve, body)

        @blk.gpsimd
        def _(pool):
            sub = nc.gpsimd.tensor_tensor

            def split_lo(t, j):
                pool.wait_ge(wh[j % 2], 2 * t + j // 2 + 1)
                sub(w_lo[:, j % 2].rearrange("p k n -> p (k n)"), wraw[:, j % 2, :],
                    v32(w_hi[:, j % 2].rearrange("p k n -> p (k n)")), ALU.subtract).then_inc(wl[j % 2], 1)

            def body(t, first, last):
                split_lo(t, SLAB_F)
                split_lo(t, SLAB_GF)
                pool.wait_ge(gwh, t + 1)
                sub(gw_lo[:], gw[:], v32(gw_hi[:]), ALU.subtract).then_inc(gwl, 1)
                pool.wait_ge(uh, t + 1)
                sub(u_lo[:], u[:], v32(u_hi[:]), ALU.subtract).then_inc(ul, 1)
                split_lo(t, SLAB_G)
                pool.wait_ge(yh, t + 1)
                sub(y_lo[:], xf[:], v32(y_hi[:]), ALU.subtract).then_inc(yl, 1)
                if not last:
                    split_lo(t + 1, SLAB_U)
                pool.wait_ge(hd, 2 * t + 2)
                sub(H[:], H[:], E[:, 0:T], ALU.add).then_inc(hs, 1)

            split_lo(0, SLAB_U)
            for i, (at, n) in enumerate(tab_pieces):
                pool.wait_ge(tab_h, i + 1)
                sub(tab_lo[:, at:at + n], fT[:, 0:n], v32(tab_hi[:, at:at + n]), ALU.subtract).then_inc(tab_l, 1)
            loops(pool, body)

        @blk.tensor
        def _(pe):
            def mm3(out, l_hi, l_lo, r_hi, r_lo, start, stop):
                nc.tensor.matmul(out, l_hi, r_hi, start=start, stop=False)
                nc.tensor.matmul(out, l_hi, r_lo, start=False, stop=False)
                return nc.tensor.matmul(out, l_lo, r_hi, start=False, stop=stop)

            def slab_product(t, j, first):
                pe.wait_ge(wl[j % 2], 2 * t + j // 2 + 1)
                for c, (at, n) in enumerate(CHUNKS):
                    if j == SLAB_F:
                        pe.wait_ge(ur, 3 * t + c + 1)
                    elif j == SLAB_GF:
                        pe.wait_ge(fr, 3 * t + c + 1)
                    elif j == SLAB_G:
                        pe.wait_ge(sgfd, 3 * t + c + 1)
                    elif not first:
                        pe.wait_ge(sg, 3 * (t - 1) + c + 1)
                    for k in range(KT):
                        last = mm3(slab[:, c, 0:n], w_hi[:, j % 2, k, :], w_lo[:, j % 2, k, :],
                                   h_hi[:, k, at:at + n], h_lo[:, k, at:at + n], k == 0, k == KT - 1)
                    last.then_inc(done[j], 1)

            def gate_products(t, d):
                for x in range(2):
                    for c, (at, n) in enumerate(CHUNKS):
                        k = 6 * d + 3 * x + c
                        if k < 3:
                            pe.wait_ge(xr, 3 * t + k + 1)
                        elif k > 3:
                            pe.wait_ge(gr, 12 * t + k - 3)
                        mm3(W[:, k % 4, 0:n], gw_hi[:, 2 * d + x, :], gw_lo[:, 2 * d + x, :],
                            u_hi[:, at:at + n], u_lo[:, at:at + n], True, True).then_inc(gp_, 1)

            def mod_product(t, q, first):
                pe.wait_ge(m_ld, 16 * (2 * t + q + 1))
                if q == 1:
                    pe.wait_ge(abl, t + 1)
                elif not first:
                    pe.wait_ge(me, 2 * t)
                for k in range(KT):
                    last = nc.tensor.matmul(W4[0:2, 0:MOD_C], silu_c[:, k, :], wm1[:, k, :],
                                            start=(k == 0), stop=(k == KT - 1))
                last.then_inc(mp, 1)

            def dft_product(t):
                pe.wait_ge(gr, 12 * t + 12)
                pe.wait_ge(yl, t + 1)
                for i in range(N_R + 2):
                    key = i if i < N_R else ("c0", "c1")[i - N_R]
                    at = TAB_AT[key]
                    out = Wf[:, 256 * i:256 * i + 256]
                    if key in (1, 2, 3):
                        re, im = ((2, 3), (4, 5), (6, 7))[key - 1]
                        ys = slice(re * P, re * P + P)
                        mm3(out, y_hi[:, ys], y_lo[:, ys], tab_hi[:, at + P:at + P + 256],
                            tab_lo[:, at + P:at + P + 256], True, False)
                        ys = slice(im * P, im * P + P)
                        last = mm3(out, y_hi[:, ys], y_lo[:, ys], tab_hi[:, at:at + 256],
                                   tab_lo[:, at:at + 256], False, True)
                    else:
                        y = {0: 0, 4: 1, "c0": 8, "c1": 9}[key]
                        ys = slice(y * P, y * P + P)
                        last = mm3(out, y_hi[:, ys], y_lo[:, ys], tab_hi[:, at:at + 256], tab_lo[:, at:at + 256],
                                   True, True)
                last.then_inc(dft, 1)

            def body(t, first, last_):
                slab_product(t, SLAB_U, first)
                mod_product(t, 0, first)
                slab_product(t, SLAB_F, first)
                pe.wait_ge(fr, 3 * t + 3)
                if first:
                    pe.wait_ge(par, 32)
                else:
                    pe.wait_ge(yd, t)
                for i in range(TT):
                    last = nc.tensor.transpose(W[:, i // 4, (i % 4) * P:(i % 4 + 1) * P], fT[:, i * P:(i + 1) * P],
                                               ident[:])
                    if i % 4 == 3 or i == TT - 1:
                        last.then_inc(trd, 1)
                pe.wait_ge(wf_ld, 16 * t + 16)
                pe.wait_ge(me, 2 * t + 1)
                for x in range(2):
                    last = nc.tensor.matmul(W4[:, x * P:(x + 1) * P], dft_ch[:, x * P:(x + 1) * P], wf[:],
                                            start=True, stop=True)
                last.then_inc(abp, 1)
                pe.wait_ge(gwl, t + 1)
                pe.wait_ge(ul, t + 1)
                gate_products(t, 0)
                slab_product(t, SLAB_GF, first)
                gate_products(t, 1)
                dft_product(t)
                slab_product(t, SLAB_G, first)
                pe.wait_ge(pql, t + 1)
                pe.wait_ge(abl, t + 1)
                for x in range(2):
                    hi = pq_hi[:].rearrange("p (r x k) -> p r x k", x=2, k=P)[:, :, x, :]
                    lo = pq_lo[:].rearrange("p (r x k) -> p r x k", x=2, k=P)[:, :, x, :]
                    for b, (r0, r1) in enumerate(((0, 4), (4, N_R + 2))):
                        last = mm3(W[:, 2 * x + b, 0:(r1 - r0) * P], ab_hi[:, x * P:(x + 1) * P],
                                   ab_lo[:, x * P:(x + 1) * P], hi[:, r0:r1, :], lo[:, r0:r1, :], True, True)
                last.then_inc(uv, 1)
                mod_product(t, 1, first)

            pe.wait_ge(tab_l, 3)
            loops(pe, body)


def out_projection0(nc, a, gs1):
    ctx = ExitStack()
    with ctx:
        def sb(name, shape, dt=F32):
            return ctx.enter_context(nc.sbuf_tensor(name, shape, dt))

        sem = a["sem"]

        K2 = 2 * KT
        wo_hi, wo_lo = sb("wo_hi", [P, K2, D], F32R), sb("wo_lo", [P, K2, D], F32R)
        wr = sb("wr", [P, 2, D])
        mraw = sb("mraw", [P, 2, KT, P])
        m_hi, m_lo = sb("m_hi", [P, 2, KT, P], F32R), sb("m_lo", [P, 2, KT, P], F32R)
        gpb = sb("gpb", [P, 2, D])
        xt = sb("xt2", [P, 2, D])
        x1 = sb("x1_tiles", [P, 2, D])
        xn = sb("xn2", [P, D])
        hb = sb("hb", [P, 2, KT, P])
        rows = sb("rows2", [2, ROWS])
        junk = sb("junk2", [P, D])
        ident = sb("ident2", [P, P])
        st = sb("st2", [P, 6, 2])
        eps = sb("eps2", [P, 1])
        Y = ctx.enter_context(nc.psum_tensor("Y", [P, 2, D], F32))
        TP = ctx.enter_context(nc.psum_tensor("TP", [P, 2, D], F32))

        par, wr_ld = sem("out0_par"), [sem("wo_loaded0"), sem("wo_loaded1")]
        woh, wol = sem("wo_hi_done"), [sem("wo_lo_pool"), sem("wo_lo_dve")]
        m_ld, mh, ml = [sem("m_loaded0"), sem("m_loaded1")], [sem("m_hi0"), sem("m_hi1")], [sem("m_lo0"), sem("m_lo1")]
        x_ld = [sem("x2_loaded0"), sem("x2_loaded1")]
        half = [sem("y_half0"), sem("y_half1")]
        y1, y2, y3, yn, xd = sem("y_sum"), sem("y_root"), sem("y_rstd"), sem("y_scaled"), sem("x1_ready")
        z1, z2, z3, xnd = sem("x1_sum"), sem("x1_root"), sem("x1_rstd"), sem("xn2_ready")
        tr, hg, hd = sem("xn_transposed"), sem("h_gained"), sem("h_ready")
        xst, hst = [sem("x1_stored0"), sem("x1_stored1")], [sem("h_stored0"), sem("h_stored1")]
        gst = sem("gp1_stored")
        r1, r2, mt, gsd, es = sem("mod1_rows"), sem("mod1_gain"), sem("mod1_transposed"), sem("gs1_done"), sem("eps2_set")
        blk = ctx.enter_context(nc.Block())

        def mrow(q):
            return x1[0:2, q, :] if q < 2 else xn[0:2, :]

        def loops(eng, body):
            body(0, 0, True, False)
            body(1, 1, False, False)
            with eng.Fori(1, LT // 2) as j:
                body(2 * j, 0, False, False)
                body(2 * j + 1, 1, False, False)
            body(LT, 0, False, False)
            body(LT + 1, 1, False, True)

        def is_ctx(t):
            return isinstance(t, int) and t >= LT

        @blk.sync
        def _(sp):
            def at(t):
                return t * P if isinstance(t, int) else sp.snap(t * P)

            def load_mix(t, h, first):
                n = at(t)
                if not first:
                    sp.wait_ge(ml[h], t)
                sp.dma_start(mraw[:, h], a["mixT"][h * KT:(h + 1) * KT, :, bass.ds(n, P)].rearrange("k p n -> p k n"))\
                    .then_inc(m_ld[h], 16)

            def load_x(t, s, first):
                n = at(t)
                if not first:
                    sp.wait_ge(xd, t - 1)
                sp.dma_start(xt[:, s, :], a["x"][bass.ds(n, P), :]).then_inc(x_ld[s], 16)

            def store(t, s):
                n = at(t)
                if not is_ctx(t):
                    sp.wait_ge(xd, t + 1)
                    sp.dma_start(a["x1"][bass.ds(n, P), :], x1[:, s, :]).then_inc(xst[s], 16)
                sp.wait_ge(hd, t + 1)
                sp.dma_start(a["hT1"][t], hb[:, s]).then_inc(hst[s], 16)

            def load_w(k):
                if k >= 2:
                    sp.wait_ge(wol[k % 2], k // 2)
                sp.dma_start(wr[:, k % 2, :], a["w_out0"][k * P:(k + 1) * P, :]).then_inc(wr_ld[k % 2], 16)

            load_w(0)
            load_mix(0, 0, True)
            load_w(1)
            load_mix(0, 1, True)
            load_x(0, 0, True)
            sp.dma_start(gpb[:], a["gp"][0].partition_broadcast(P)).then_inc(par, 16)
            sp.dma_start(rows[:], a["rows1"]).then_inc(par, 16)
            sp.dma_start(ident[:], a["ident"]).then_inc(par, 16)
            for q in range(3):
                sp.dma_start(mrow(q), a["mod1"].rearrange("w a b -> w (a b)")[:, q * D:(q + 1) * D]).then_inc(par, 16)
            for k in range(2, K2):
                load_w(k)
            load_x(1, 1, True)
            sp.wait_ge(r2, 2)
            sp.dma_start(a["gp"][1], mrow(2)).then_inc(gst, 16)

            def body(t, s, first, last):
                if not last:
                    load_mix(t + 1, 0, False)
                    load_mix(t + 1, 1, False)
                    if not first:
                        load_x(t + 1, 1 - s, False)
                if not first:
                    store(t - 1, 1 - s)

            loops(sp, body)
            store(TT - 1, 1)
            for s in range(2):
                sp.wait_ge(xst[s], 8 * LT)
                sp.wait_ge(hst[s], 8 * TT)
            sp.wait_ge(gst, 16)

        @blk.scalar
        def _(act):
            def split(t, h, first):
                act.wait_ge(m_ld[h], 16 * t + 16)
                if not first:
                    act.wait_ge(half[h], t)
                nc.scalar.activation(m_hi[:, h], mraw[:, h], ACT.Copy).then_inc(mh[h], 1)

            def epilogue(t, s, second):
                act.wait_ge(half[1], t + 1)
                nc.scalar.activation(junk[:], Y[:, s, :], ACT.Square, accum_out=st[:, 0, s:s + 1]).then_inc(y1, 1)
                act.wait_ge(y1, t + 1)
                nc.scalar.activation(st[:, 1, s:s + 1], st[:, 0, s:s + 1], ACT.Sqrt, bias=eps[:, 0:1],
                                     scale=1.0 / D).then_inc(y2, 1)
                act.wait_ge(xd, t + 1)
                nc.scalar.activation(junk[:], x1[:, s, :], ACT.Square, accum_out=st[:, 3, s:s + 1]).then_inc(z1, 1)
                act.wait_ge(z1, t + 1)
                nc.scalar.activation(st[:, 4, s:s + 1], st[:, 3, s:s + 1], ACT.Sqrt, bias=eps[:, 0:1],
                                     scale=1.0 / D).then_inc(z2, 1)

            split(0, 0, True)
            split(0, 1, True)
            act.wait_ge(es, 1)
            for k in range(K2):
                act.wait_ge(wr_ld[k % 2], 16 * (k // 2 + 1))
                nc.scalar.activation(wo_hi[:, k, :], wr[:, k % 2, :], ACT.Copy).then_inc(woh, 1)

            def body(t, s, first, last):
                if not first:
                    epilogue(t - 1, 1 - s, True)
                if not last:
                    split(t + 1, 0, False)
                    split(t + 1, 1, False)

            loops(act, body)
            epilogue(TT - 1, 1, True)

        @blk.vector
        def _(dve):
            nc.vector.memset(eps[:], EPS).then_inc(es, 1)
            dve.wait_ge(par, 96)
            tt, stt = nc.vector.tensor_tensor, nc.vector.scalar_tensor_tensor
            for q in range(3):
                tt(mrow(q), mrow(q), rows[:, q * D:(q + 1) * D], ALU.add).then_inc(r1, 1)
            dve.wait_ge(r1, 3)
            stt(out=mrow(1), in0=mrow(1), scalar=1.0, in1=rows[:, 3 * D:4 * D], op0=ALU.add, op1=ALU.mult).then_inc(r2, 1)
            tt(mrow(2), mrow(2), rows[:, 4 * D:5 * D], ALU.mult).then_inc(r2, 1)
            dve.wait_ge(mt, 1)
            nc.vector.tensor_copy(gs1[:].rearrange("p a k w -> p (a k w)"), TP[:, 0, 0:4 * KT]).then_inc(gsd, 1)
            for k in range(1, K2, 2):
                dve.wait_ge(woh, k + 1)
                tt(wo_lo[:, k, :], wr[:, 1, :], v32(wo_hi[:, k, :]), ALU.subtract).then_inc(wol[1], 1)

            def epilogue(t, s):
                w = 1 if is_ctx(t) else 0
                dve.wait_ge(y2, t + 1)
                nc.vector.reciprocal(st[:, 2, s:s + 1], st[:, 1, s:s + 1]).then_inc(y3, 1)
                dve.wait_ge(y3, t + 1)
                if isinstance(t, int) and t < 2:
                    dve.wait_ge(gst, 16)
                else:
                    dve.wait_ge(xst[s], 8 * (t - s))
                stt(out=x1[:, s, :], in0=Y[:, s, :], scalar=st[:, 2, s:s + 1], in1=gpb[:, w, :], op0=ALU.mult,
                    op1=ALU.mult).then_inc(yn, 1)
                dve.wait_ge(z2, t + 1)
                nc.vector.reciprocal(st[:, 5, s:s + 1], st[:, 4, s:s + 1]).then_inc(z3, 1)
                dve.wait_ge(z3, t + 1)
                if not (isinstance(t, int) and t == 0):
                    dve.wait_ge(tr, t)
                nc.vector.tensor_scalar(xn[:], x1[:, s, :], st[:, 5, s:s + 1], None, ALU.mult).then_inc(xnd, 1)
                dve.wait_ge(tr, t + 1)
                if not (isinstance(t, int) and t < 2):
                    dve.wait_ge(hst[s], 8 * (t - s))
                tt(hb[:, s], TP[:, s, :].rearrange("p (k n) -> p k n", n=P),
                   gs1[:, 1, :, w:w + 1].to_broadcast([P, KT, P]), ALU.mult).then_inc(hg, 1)

            def body(t, s, first, last):
                if not first:
                    epilogue(t - 1, 1 - s)

            loops(dve, body)
            epilogue(TT - 1, 1)

        @blk.gpsimd
        def _(pool):
            tt = nc.gpsimd.tensor_tensor

            def split(t, h):
                pool.wait_ge(mh[h], t + 1)
                tt(m_lo[:, h], mraw[:, h], v32(m_hi[:, h]), ALU.subtract).then_inc(ml[h], 1)

            split(0, 0)
            split(0, 1)
            for k in range(0, K2, 2):
                pool.wait_ge(woh, k + 1)
                tt(wo_lo[:, k, :], wr[:, 0, :], v32(wo_hi[:, k, :]), ALU.subtract).then_inc(wol[0], 1)

            def epilogue(t, s):
                w = 1 if is_ctx(t) else 0
                pool.wait_ge(x_ld[s], 8 * (t - s) + 16)
                pool.wait_ge(yn, t + 1)
                tt(x1[:, s, :], x1[:, s, :], xt[:, s, :], ALU.add).then_inc(xd, 1)
                pool.wait_ge(gsd, 1)
                pool.wait_ge(hg, t + 1)
                tt(hb[:, s], hb[:, s], gs1[:, 0, :, w:w + 1].to_broadcast([P, KT, P]), ALU.add).then_inc(hd, 1)

            def body(t, s, first, last):
                if not first:
                    epilogue(t - 1, 1 - s)
                if not last:
                    split(t + 1, 0)
                    split(t + 1, 1)

            loops(pool, body)
            epilogue(TT - 1, 1)

        @blk.tensor
        def _(pe):
            pe.wait_ge(par, 96)
            pe.wait_ge(r2, 2)
            for q in range(2 * KT):
                last = nc.tensor.transpose(TP[:, 0, 2 * q:2 * q + 2], mrow(q // KT)[:, (q % KT) * P:(q % KT + 1) * P],
                                           ident[0:2, 0:2])
            last.then_inc(mt, 1)

            def product(t, s, first):
                for h in range(2):
                    pe.wait_ge(ml[h], t + 1)
                    if h == 0 and not (isinstance(t, int) and t < 2):
                        pe.wait_ge(yn, t - 1)
                    for k in range(KT):
                        if first:
                            g = h * KT + k
                            pe.wait_ge(wol[g % 2], g // 2 + 1)
                        for n in (0, 512):
                            out = Y[:, s, n:n + 512]
                            w_hi, w_lo = wo_hi[:, h * KT + k, n:n + 512], wo_lo[:, h * KT + k, n:n + 512]
                            nc.tensor.matmul(out, m_hi[:, h, k, :], w_hi, start=(h == 0 and k == 0), stop=False)
                            nc.tensor.matmul(out, m_hi[:, h, k, :], w_lo, start=False, stop=False)
                            last = nc.tensor.matmul(out, m_lo[:, h, k, :], w_hi, start=False,
                                                    stop=(h == 1 and k == KT - 1))
                    last.then_inc(half[h], 1)

            def transposes(t, s):
                pe.wait_ge(xnd, t + 1)
                if isinstance(t, int) and t < 2:
                    pe.wait_ge(gsd, 1)
                else:
                    pe.wait_ge(hg, t - 1)
                for k in range(KT):
                    last = nc.tensor.transpose(TP[:, s, k * P:(k + 1) * P], xn[:, k * P:(k + 1) * P], ident[:])
                last.then_inc(tr, 1)

            def body(t, s, first, last):
                product(t, s, first)
                if not first:
                    transposes(t - 1, 1 - s)

            loops(pe, body)
            transposes(TT - 1, 1)

def projections1(nc, a, k_hi, k_lo, vt_hi, vt_lo):
    ctx = ExitStack()
    with ctx:
        def sb(name, shape, dt=F32):
            return ctx.enter_context(nc.sbuf_tensor(name, shape, dt))

        sem = a["sem"]

        h_hi, h_lo = sb("h1_hi", [P, KT, T], F32R), sb("h1_lo", [P, KT, T], F32R)
        hraw = sb("h1_raw", [P, 2, KT, P])
        wraw = sb("w1_raw", [P, 2, D])
        w_hi, w_lo = sb("w1_hi", [P, 2, KT, P], F32R), sb("w1_lo", [P, 2, KT, P], F32R)
        cos, sin = sb("rope_cos", [P, N_LAT]), sb("rope_sin", [P, N_LAT])
        R = sb("rope_in", [P, T])
        Z = sb("rope_swap", [P, N_LAT])
        C = sb("rope_cosined", [P, N_LAT])
        G = sb("gate1", [P, N_LAT])
        ident = sb("ident3", [P, P])
        slab = ctx.enter_context(nc.psum_tensor("slab1", [P, 6, 512], F32))
        VP = ctx.enter_context(nc.psum_tensor("VP", [P, 2, 512], F32))

        par = sem("proj1_par")
        h_ld, hh, hl = [sem("h1_loaded0"), sem("h1_loaded1")], sem("h1_hi_done"), [sem("h1_lo0"), sem("h1_lo1")]
        w_ld, wh, wl = [sem("w1_loaded0"), sem("w1_loaded1")], [sem("w1_hi0"), sem("w1_hi1")], [sem("w1_lo0"), sem("w1_lo1")]
        kv, kvr = sem("kv_chunk"), sem("kv_chunk_read")
        sw, rc, rs, ro = sem("swapped"), sem("times_cos"), sem("times_sin"), sem("rotated")
        kh, kl = sem("k_hi_done"), sem("k_lo_done")
        vtr, vh, vl = sem("v_transposed"), sem("v_hi_done"), sem("v_lo_done")
        qd, qr, qst = sem("q_chunk"), sem("q_chunk_read"), sem("q_stored")
        gd, gt, gg, gst = sem("g_chunk"), sem("g_tanh"), sem("g_silu"), sem("g_stored")
        blk = ctx.enter_context(nc.Block())
        V_GROUPS = [(0, 4), (4, 4), (8, 2)]

        def loops(eng, body, n=KT):
            body(0, True, False)
            with eng.Fori(1, n - 1) as t:
                body(t, False, False)
            body(n - 1, False, True)

        @blk.sync
        def _(sp):
            def load_slab(at, j, use):
                if not (isinstance(use, int) and use == 0):
                    sp.wait_ge(wl[j], use)
                sp.dma_start(wraw[:, j, :], a["w_in1"][at]).then_inc(w_ld[j], 16)

            load_slab(0, 0, 0)
            for i in range(TT):
                if i >= 2:
                    sp.wait_ge(hl[i % 2], i // 2)
                sp.dma_start(hraw[:, i % 2], a["hT1"][i]).then_inc(h_ld[i % 2], 16)
                if i == 3:
                    load_slab(1, 1, 0)
            sp.dma_start(cos[:], a["rope"][0]).then_inc(par, 16)
            sp.dma_start(sin[:], a["rope"][1]).then_inc(par, 16)
            sp.dma_start(ident[:], a["ident"]).then_inc(par, 16)
            load_slab(2, 0, 1)
            load_slab(3, 1, 1)

            def store(t):
                sp.wait_ge(ro, t + 3)
                sp.dma_start(a["qT"][:, :, t, :].rearrange("b p n -> p b n"),
                             R[:, 0:N_LAT].rearrange("p (b n) -> p b n", n=P)).then_inc(qst, 16)
                sp.wait_ge(gg, 2 * t + 2)
                sp.dma_start(a["sgT"][:, :, t, :].rearrange("b p n -> p b n"),
                             G[:].rearrange("p (b n) -> p b n", n=P)).then_inc(gst, 16)

            def body(t, first, last):
                load_slab(2 * t + 4, 0, t + 2)
                load_slab(2 * t + 5, 1, t + 2)
                if not first:
                    store(t - 1)

            loops(sp, body)
            store(KT - 1)
            sp.wait_ge(qst, 16 * KT)
            sp.wait_ge(gst, 16 * KT)

        @blk.scalar
        def _(act):
            def split(j, use):
                act.wait_ge(w_ld[j], 16 * use + 16)
                nc.scalar.activation(w_hi[:, j].rearrange("p k n -> p (k n)"), wraw[:, j, :], ACT.Copy).then_inc(wh[j], 1)

            split(0, 0)
            for i in range(TT):
                act.wait_ge(h_ld[i % 2], 16 * (i // 2 + 1))
                nc.scalar.activation(h_hi[:, :, i * P:(i + 1) * P], hraw[:, i % 2], ACT.Copy).then_inc(hh, 1)
                if i == 3:
                    split(1, 0)
            for s in range(4):
                if s in (1, 2):
                    act.wait_ge(kl, s)
                elif s == 3:
                    act.wait_ge(vtr, 3)
                for c, (at, n) in enumerate(CHUNKS):
                    act.wait_ge(kv, 3 * s + c + 1)
                    nc.scalar.activation(R[:, at:at + n], slab[:, 3 * (s % 2) + c, 0:n], ACT.Copy).then_inc(kvr, 1)
                split(s % 2, s // 2 + 1)
                if s < 2:
                    act.wait_ge(ro, s + 1)
                    nc.scalar.activation(k_hi[:, s, :], R[:], ACT.Copy).then_inc(kh, 1)
                else:
                    for g, (t0, n) in enumerate(V_GROUPS):
                        act.wait_ge(vtr, 3 * (s - 2) + g + 1)
                        nc.scalar.activation(vt_hi[:, t0:t0 + n, (s - 2) * P:(s - 1) * P],
                                             VP[:, (3 * (s - 2) + g) % 2, 0:n * P].rearrange("p (t n) -> p t n", n=P),
                                             ACT.Copy).then_inc(vh, 1)

            def body(t, first, last):
                if first:
                    act.wait_ge(vtr, 6)
                else:
                    act.wait_ge(qst, 16 * t)
                for c in range(2):
                    act.wait_ge(qd, 2 * t + c + 1)
                    nc.scalar.activation(R[:, 512 * c:512 * c + 512], slab[:, c, :], ACT.Copy).then_inc(qr, 1)
                if not last:
                    split(0, t + 3)
                if not first:
                    act.wait_ge(gst, 16 * t)
                for c in range(2):
                    act.wait_ge(gd, 2 * t + c + 1)
                    nc.scalar.activation(G[:, 512 * c:512 * c + 512], slab[:, 3 + c, :], ACT.Tanh, scale=0.5)\
                        .then_inc(gt, 1)
                if not last:
                    split(1, t + 3)

            loops(act, body)

        @blk.vector
        def _(dve):
            tt = nc.vector.tensor_tensor
            for i in range(1, TT, 2):
                dve.wait_ge(hh, i + 1)
                tt(h_lo[:, :, i * P:(i + 1) * P], hraw[:, 1], v32(h_hi[:, :, i * P:(i + 1) * P]), ALU.subtract)\
                    .then_inc(hl[1], 1)
            dve.wait_ge(par, 48)

            def rotate(ready, value, n):
                dve.wait_ge(ready, value)
                if not (isinstance(n, int) and n == 0):
                    dve.wait_ge(ro, n)
                tt(C[:], R[:, 0:N_LAT], cos[:], ALU.mult).then_inc(rc, 1)
                nc.vector.stream_shuffle(Z[:], R[:, 0:N_LAT], [(i + 16) % 32 for i in range(32)]).then_inc(sw, 1)
                dve.wait_ge(rc, n + 1)
                dve.wait_ge(sw, n + 1)
                dve.wait_ge(rs, n + 1)
                tt(R[:, 0:N_LAT], C[:], Z[:], ALU.add).then_inc(ro, 1)

            rotate(kvr, 3, 0)
            rotate(kvr, 6, 1)
            for s in range(2):
                for g, (t0, n) in enumerate(V_GROUPS):
                    dve.wait_ge(vh, 3 * s + g + 1)
                    lo = vt_lo[:, t0:t0 + n, s * P:(s + 1) * P]
                    tt(lo, VP[:, (3 * s + g) % 2, 0:n * P].rearrange("p (t n) -> p t n", n=P),
                       v32(vt_hi[:, t0:t0 + n, s * P:(s + 1) * P]), ALU.subtract).then_inc(vl, 1)

            def body(t, first, last):
                rotate(qr, 2 * t + 2, t + 2)
                for c in range(2):
                    dve.wait_ge(gt, 2 * t + c + 1)
                    nc.vector.scalar_tensor_tensor(out=G[:, 512 * c:512 * c + 512], in0=G[:, 512 * c:512 * c + 512],
                                                   scalar=1.0, in1=slab[:, 3 + c, :], op0=ALU.add,
                                                   op1=ALU.mult).then_inc(gg, 1)

            loops(dve, body)

        @blk.gpsimd
        def _(pool):
            tt = nc.gpsimd.tensor_tensor

            def split(j, use):
                pool.wait_ge(wh[j], use + 1)
                tt(w_lo[:, j].rearrange("p k n -> p (k n)"), wraw[:, j, :],
                   v32(w_hi[:, j].rearrange("p k n -> p (k n)")), ALU.subtract).then_inc(wl[j], 1)

            def sines(n):
                pool.wait_ge(sw, n + 1)
                tt(Z[:], Z[:], sin[:], ALU.mult).then_inc(rs, 1)

            split(0, 0)
            for i in range(0, TT, 2):
                pool.wait_ge(hh, i + 1)
                tt(h_lo[:, :, i * P:(i + 1) * P], hraw[:, 0], v32(h_hi[:, :, i * P:(i + 1) * P]), ALU.subtract)\
                    .then_inc(hl[0], 1)
                if i == 4:
                    split(1, 0)
            pool.wait_ge(par, 48)
            for s in range(2):
                split(s, 1)
                sines(s)
                pool.wait_ge(kh, s + 1)
                tt(k_lo[:, s, :], R[:], v32(k_hi[:, s, :]), ALU.subtract).then_inc(kl, 1)
            split(0, 2)
            split(1, 2)

            def body(t, first, last):
                if not last:
                    split(0, t + 3)
                sines(t + 2)
                if not last:
                    split(1, t + 3)

            loops(pool, body)

        @blk.tensor
        def _(pe):
            def product(j, use, c, at, n):
                out = slab[:, 3 * j + c, 0:n]
                for k in range(KT):
                    rhs_hi, rhs_lo = h_hi[:, k, at:at + n], h_lo[:, k, at:at + n]
                    nc.tensor.matmul(out, w_hi[:, j, k, :], rhs_hi, start=(k == 0), stop=False)
                    nc.tensor.matmul(out, w_hi[:, j, k, :], rhs_lo, start=False, stop=False)
                    last = nc.tensor.matmul(out, w_lo[:, j, k, :], rhs_hi, start=False, stop=(k == KT - 1))
                return last

            def transposes(s):
                pe.wait_ge(kvr, 3 * (s + 2) + 3)
                for g, (t0, n) in enumerate(V_GROUPS):
                    if 3 * s + g >= 2:
                        pe.wait_ge(vl, 3 * s + g - 1)
                    for i in range(n):
                        last = nc.tensor.transpose(VP[:, (3 * s + g) % 2, i * P:(i + 1) * P], R[:, (t0 + i) * P:(t0 + i + 1) * P],
                                                   ident[:])
                    last.then_inc(vtr, 1)

            for s in range(4):
                pe.wait_ge(wl[s % 2], s // 2 + 1)
                for c, (at, n) in enumerate(CHUNKS):
                    if s == 0:
                        tiles = (at + n) // P
                        pe.wait_ge(hl[0], (tiles + 1) // 2)
                        pe.wait_ge(hl[1], tiles // 2)
                    if s >= 2:
                        pe.wait_ge(kvr, 3 * (s - 2) + c + 1)
                    product(s % 2, s // 2, c, at, n).then_inc(kv, 1)
                if s == 3:
                    pe.wait_ge(par, 48)
                    transposes(0)

            def body(t, first, last):
                pe.wait_ge(wl[0], t + 3)
                for c in range(2):
                    if first:
                        pe.wait_ge(kvr, 9)
                    else:
                        pe.wait_ge(qr, 2 * (t - 1) + c + 1)
                    product(0, t + 2, c, 512 * c, 512).then_inc(qd, 1)
                if first:
                    transposes(1)
                pe.wait_ge(wl[1], t + 3)
                for c in range(2):
                    if not first:
                        pe.wait_ge(gg, 2 * (t - 1) + c + 1)
                    product(1, t + 2, c, 512 * c, 512).then_inc(gd, 1)

            loops(pe, body)


N_HD = 4
WIN = 5
AHEAD = 6


def attention(nc, a, k_hi, k_lo, vt_hi, vt_lo):
    ctx = ExitStack()
    with ctx:
        def sb(name, shape, dt=F32):
            return ctx.enter_context(nc.sbuf_tensor(name, shape, dt))

        sem = a["sem"]

        NB = LT
        kw_hi, kw_lo = sb("kw_hi", [P, 2, 2, WIN, P], F32R), sb("kw_lo", [P, 2, 2, WIN, P], F32R)
        vw_hi, vw_lo = sb("vw_hi", [P, 2, 3, 2 * P], F32R), sb("vw_lo", [P, 2, 3, 2 * P], F32R)
        qraw = sb("q_raw", [P, 2, KT, P])
        q_hi, q_lo = sb("q_hi", [P, 2, KT, P], F32R), sb("q_lo", [P, 2, KT, P], F32R)
        pr = sb("probs", [P, 4, N_HD, WIN * P])
        pt_hi, pt_lo = sb("pt_hi", [P, WIN, 512], F32R), sb("pt_lo", [P, WIN, 512], F32R)
        ost = sb("o_out", [P, 2, KT, P])
        mask = sb("mask", [P, 2, WIN * P])
        sink, nsink = sb("sink", [P, N_HEADS]), sb("nsink", [P, N_HEADS])
        nm, es, rsum, den, rden = (sb(n, [P, 4, N_HD]) for n in ("neg_max", "sink_term", "row_sum", "denom", "rdenom"))
        ident = sb("ident4", [P, P])
        S = ctx.enter_context(nc.psum_tensor("S", [P, 2, 2, 512], F32))
        TB = ctx.enter_context(nc.psum_tensor("TB", [P, 2, 512], F32))
        O = ctx.enter_context(nc.psum_tensor("O", [P, 2, 512], F32))

        par, nsk = sem("att_par"), sem("neg_sink")
        kw_ld, vw_ld = [sem("k_window0"), sem("k_window1")], [sem("v_window0"), sem("v_window1")]
        q_ld, qh, ql = [sem("q_loaded0"), sem("q_loaded1")], sem("q_hi_done"), sem("q_lo_done")
        sd, td, ed = sem("scores"), sem("scaled_max"), sem("exp_done")
        sa, se, dn, rc, pn = sem("sink_minus_max"), sem("sink_exp"), sem("denom_done"), sem("rdenom_done"), sem("normalised")
        tr, ph, pl, pv = sem("p_transposed"), sem("pt_hi_done"), sem("pt_lo_done"), sem("value_product")
        oe, ost_s = sem("o_copied"), [sem("o_stored0"), sem("o_stored1")]
        blk = ctx.enter_context(nc.Block())

        def loops(eng, body):
            body(0, 0, True, False)
            with eng.Fori(0, NB // 2 - 2) as j:
                body(2 * j + 1, 1, False, False)
                body(2 * j + 2, 0, False, False)
            body(NB - 3, 1, False, False)
            body(NB - 2, 0, False, False)
            body(NB - 1, 1, False, True)

        def tiles(first):
            return range(1, WIN) if first else range(WIN)

        def tile_count(b, first):
            return 0 if first else 20 * b - 4

        def n_par(u, x, first):
            return ((WIN - (1 if first else 0)) * u + x) % 2

        def ahead(head, b, j, first, last):
            if j < 16:
                head(b, j, first)
            elif not last:
                head(b + 1, j - 16, False)

        def key_region(j, edge):
            return S[:, j % 2, 0, :] if edge else S[:, j % 2, :, 0:320]

        def columns(row, edge):
            return row[:, P:WIN * P] if edge else row.rearrange("p (a n) -> p a n", a=2)

        @blk.sync
        def _(sp):
            def load_windows(b, s, first, last):
                late = not (isinstance(b, int) and b < 2)
                if late:
                    sp.wait_ge(sd, 16 * (b - 1))
                parts = ((1, b + 1), (2, b)) if first else ((0, b - 1), (1, b if last else b + 1), (2, b))
                for buf, src in ((kw_hi, k_hi), (kw_lo, k_lo)):
                    for w, tile in parts:
                        sp.dma_start(v32(buf[:, s, :, w, :]), v32(src[:, :, bass.ds(tile * P, P)])).then_inc(kw_ld[s], 16)
                    if not late:
                        sp.dma_start(v32(buf[:, s, :, 3:5, :].rearrange("p a w n -> p a (w n)")),
                                     v32(src[:, :, N_LAT:T])).then_inc(kw_ld[s], 16)
                if late:
                    sp.wait_ge(pv, tile_count(b - 1, False))
                for buf, src in ((vw_hi, vt_hi), (vw_lo, vt_lo)):
                    for w, tile in parts:
                        sp.dma_start(v32(buf[:, s, w:w + 1, :]), v32(src[:, bass.ds(tile, 1), :])).then_inc(vw_ld[s], 16)

            def load_q(b, s):
                if not (isinstance(b, int) and b < 2):
                    sp.wait_ge(ql, b - 1)
                sp.dma_start(qraw[:, s], a["qT"][b]).then_inc(q_ld[s], 16)

            def store(b, s):
                sp.wait_ge(oe, 4 * b + 4)
                sp.dma_start(a["oT"][b], ost[:, s]).then_inc(ost_s[s], 16)

            load_q(0, 0)
            load_windows(0, 0, True, False)
            sp.dma_start(sink[:], a["sink"]).then_inc(par, 16)
            sp.dma_start(mask[:], a["mask"]).then_inc(par, 16)
            sp.dma_start(ident[:], a["ident"]).then_inc(par, 16)
            load_q(1, 1)
            load_windows(1, 1, False, False)

            def body(b, s, first, last):
                if not first and not last:
                    load_q(b + 1, 1 - s)
                    load_windows(b + 1, 1 - s, False, False)
                if not first:
                    store(b - 1, 1 - s)

            body(0, 0, True, False)
            with sp.Fori(0, NB // 2 - 2) as j:
                body(2 * j + 1, 1, False, False)
                body(2 * j + 2, 0, False, False)
            body(NB - 3, 1, False, False)
            load_q(NB - 1, 1)
            load_windows(NB - 1, 1, False, True)
            store(NB - 3, 1)
            store(NB - 2, 0)
            store(NB - 1, 1)
            for s in range(2):
                sp.wait_ge(ost_s[s], 8 * NB)

        @blk.scalar
        def _(act):
            def split_q(b, s):
                act.wait_ge(q_ld[s], 8 * (b - s) + 16)
                if not (isinstance(b, int) and b < 2):
                    act.wait_ge(sd, 16 * (b - 1))
                nc.scalar.activation(q_hi[:, s], qraw[:, s], ACT.Copy).then_inc(qh, 1)

            def head(b, j, edge):
                u, h = j // 4, j % 4
                act.wait_ge(td, 16 * b + j + 1)
                row = columns(pr[:, u, h, :], edge)
                nc.scalar.activation(row, row, ACT.Exp, bias=nm[:, u, h:h + 1], scale=-1.0,
                                     accum_out=rsum[:, u, h:h + 1]).then_inc(ed, 1)
                if h % 2 == 1:
                    act.wait_ge(sa, 8 * b + j // 2 + 1)
                    nc.scalar.activation(es[:, u, h - 1:h + 1], es[:, u, h - 1:h + 1], ACT.Exp).then_inc(se, 1)

            def copy_o(b, s, u, first):
                act.wait_ge(pv, tile_count(b, first) + (WIN - first) * (u + 1))
                if u == 0 and not (isinstance(b, int) and b < 2):
                    act.wait_ge(ost_s[s], 8 * (b - s))
                p, c = u // 2, u % 2
                half = slice(HEAD * c, HEAD * (c + 1))
                nc.scalar.activation(ost[half, s, 4 * p:4 * p + 4, :],
                                     O[half, u % 2, :].rearrange("p (h n) -> p h n", n=P), ACT.Copy).then_inc(oe, 1)

            split_q(0, 0)
            split_q(1, 1)
            for j in range(AHEAD):
                head(0, j, True)

            def body(b, s, first, last):
                base = tile_count(b, first)
                for u in range(4):
                    for x, w in enumerate(tiles(first)):
                        n = base + (WIN - first) * u + x
                        act.wait_ge(tr, n + 1)
                        if not (first and u == 0):
                            act.wait_ge(pv, base + (WIN - first) * (u - 1) + x + 1 if u else
                                        (base - WIN + x + 1 if not (isinstance(b, int) and b == 1) else base))
                        nc.scalar.activation(pt_hi[:, w, :], TB[:, n_par(u, x, first), :], ACT.Copy).then_inc(ph, 1)
                        if x == 1:
                            if u:
                                copy_o(b, s, u - 1, first)
                            elif not first:
                                copy_last(b - 1, 1 - s)
                        if x >= 1:
                            ahead(head, b, 4 * u + x - 1 + AHEAD, first, last)
                    if first:
                        ahead(head, b, 4 * u + 3 + AHEAD, first, last)
                    if u == 1 and not first and not last:
                        split_q(b + 1, 1 - s)

            def copy_last(b, s):
                act.wait_ge(pv, 20 * b + 16)
                nc.scalar.activation(ost[HEAD:P, s, 4:8, :], O[HEAD:P, 1, :].rearrange("p (h n) -> p h n", n=P),
                                     ACT.Copy).then_inc(oe, 1)

            loops(act, body)
            copy_last(NB - 1, 1)

        @blk.vector
        def _(dve):
            tt = nc.vector.tensor_tensor
            dve.wait_ge(par, 48)
            nc.vector.tensor_scalar(nsink[:], sink[:], -1.0, None, ALU.mult).then_inc(nsk, 1)

            def head_waits(b, j):
                dve.wait_ge(sd, 16 * b + j + 1)
                if not (isinstance(b, int) and b == 0):
                    dve.wait_ge(tr, 4 * (j // 4 + 1) if isinstance(b, int) and b == 1 else
                                tile_count(b - 1, False) + WIN * (j // 4 + 1))

            def head(b, j, edge):
                u, h = j // 4, j % 4
                final = isinstance(b, int) and b == NB - 1
                nc.vector.tensor_tensor_reduce(
                    out=columns(pr[:, u, h, :], edge), in0=key_region(j, edge),
                    in1=columns(mask[:, 1 if final else 0, :], edge), scale=-SCALE, scalar=nsink[:, j:j + 1],
                    op0=ALU.add, op1=ALU.min, accum_out=nm[:, u, h:h + 1]).then_inc(td, 1)
                if h % 2 == 1:
                    dve.wait_ge(td, 16 * b + j + 1)
                    tt(es[:, u, h - 1:h + 1], nm[:, u, h - 1:h + 1], sink[:, j - 1:j + 1], ALU.add).then_inc(sa, 1)

            def denominators(b, j):
                u, h = j // 4, j % 4
                at = slice(h - 1, h + 1)
                dve.wait_ge(se, 8 * b + j // 2 + 1)
                if not (isinstance(b, int) and b == 0):
                    dve.wait_ge(pn, 16 * b + j + 1 - 16)
                tt(den[:, u, at], es[:, u, at], rsum[:, u, at], ALU.add).then_inc(dn, 1)
                dve.wait_ge(dn, 8 * b + j // 2 + 1)
                nc.vector.reciprocal(rden[:, u, at], den[:, u, at]).then_inc(rc, 1)

            dve.wait_ge(nsk, 1)
            for j in range(AHEAD):
                head_waits(0, j)
                head(0, j, True)
                if j % 2 == 1:
                    denominators(0, j)

            def body(b, s, first, last):
                base = tile_count(b, first)
                for u in range(4):
                    for x, w in enumerate(tiles(first)):
                        n = base + (WIN - first) * u + x
                        j = 4 * u + x - 1 + AHEAD
                        if x >= 1:
                            ahead(lambda bb, jj, e: head_waits(bb, jj), b, j, first, last)
                        dve.wait_ge(ph, n + 1)
                        tt(pt_lo[:, w, :], TB[:, n_par(u, x, first), :], v32(pt_hi[:, w, :]), ALU.subtract).then_inc(pl, 1)
                        if x >= 1:
                            ahead(head, b, j, first, last)
                        if x in (2, 4):
                            ahead(lambda bb, jj, e: denominators(bb, jj), b, j, first, last)
                    if first:
                        ahead(lambda bb, jj, e: head_waits(bb, jj), b, 4 * u + 3 + AHEAD, first, last)
                        ahead(head, b, 4 * u + 3 + AHEAD, first, last)
                        ahead(lambda bb, jj, e: denominators(bb, jj), b, 4 * u + 3 + AHEAD, first, last)

            loops(dve, body)

        @blk.gpsimd
        def _(pool):
            def split_q(b, s):
                pool.wait_ge(qh, b + 1)
                nc.gpsimd.tensor_tensor(q_lo[:, s], qraw[:, s], v32(q_hi[:, s]), ALU.subtract).then_inc(ql, 1)

            def pair(b, j, edge):
                u, h = j // 4, j % 4
                pool.wait_ge(rc, 8 * b + j // 2 + 1)
                rows = pr[:, u, h - 1:h + 1, P if edge else 0:]
                nc.gpsimd.tensor_tensor(rows, rows, rden[:, u, h - 1:h + 1].unsqueeze(2).to_broadcast(rows.shape),
                                        ALU.mult).then_inc(pn, 2)

            split_q(0, 0)
            split_q(1, 1)
            for j in (1, 3, 5):
                pair(0, j, True)

            def body(b, s, first, last):
                for u in range(4):
                    for j in (4 * u + 1, 4 * u + 3):
                        ahead(pair, b, j + AHEAD, first, last)
                    if u == 1 and not first and not last:
                        split_q(b + 1, 1 - s)

            loops(pool, body)

        @blk.tensor
        def _(pe):
            def scores(b, s, j, edge):
                u, h = j // 4, j % 4
                p, c = u // 2, u % 2
                if j == 0:
                    pe.wait_ge(ql, b + 1)
                    pe.wait_ge(kw_ld[s], kw_value(b, s))
                if not (isinstance(b, int) and b == 0 and j < 2):
                    pe.wait_ge(td, 16 * b + j - 1)
                half = slice(HEAD * c, HEAD * (c + 1))
                q = (q_hi[half, s, 4 * p + h, :], q_lo[half, s, 4 * p + h, :])
                kh_ = kw_hi[half, s, p].rearrange("d w n -> d (w n)")
                kl_ = kw_lo[half, s, p].rearrange("d w n -> d (w n)")
                parts = [(0, P, 512)] if edge else [(0, 0, 320), (1, 320, 320)]
                for bank, at, n in parts:
                    out = S[:, j % 2, bank, 0:n]
                    nc.tensor.matmul(out, q[0], kh_[:, at:at + n], start=True, stop=False)
                    nc.tensor.matmul(out, q[0], kl_[:, at:at + n], start=False, stop=False)
                    last = nc.tensor.matmul(out, q[1], kh_[:, at:at + n], start=False, stop=True)
                last.then_inc(sd, 1)

            def values(b, s, u, x, w, first):
                n = tile_count(b, first) + (WIN - first) * u + x
                p = u // 2
                pe.wait_ge(pl, n + 1)
                if x == 0 and not (first and u < 2):
                    pe.wait_ge(oe, 4 * b + u - 1)
                if x == 0 and u == 0:
                    pe.wait_ge(vw_ld[s], vw_value(b, s))
                at = slice(p * P, (p + 1) * P)
                v = (vw_hi[:, s, w, at], vw_lo[:, s, w, at]) if w < 3 else \
                    (vt_hi[:, LT + w - 3, at], vt_lo[:, LT + w - 3, at])
                end = w == WIN - 1
                out = O[:, u % 2, :]
                nc.tensor.matmul(out, v[0], pt_hi[:, w, :], start=(x == 0), stop=False)
                nc.tensor.matmul(out, v[0], pt_lo[:, w, :], start=False, stop=False)
                nc.tensor.matmul(out, v[1], pt_hi[:, w, :], start=False, stop=end).then_inc(pv, 1)

            pe.wait_ge(par, 48)
            for j in range(AHEAD):
                scores(0, 0, j, True)

            def body(b, s, first, last):
                base = tile_count(b, first)
                for u in range(4):
                    ws = list(tiles(first))
                    for x, w in enumerate(ws):
                        n = base + (WIN - first) * u + x
                        if x == 0:
                            pe.wait_ge(pn, 16 * b + 4 * u + 4)
                        if not (first and u == 0 and x < 2):
                            pe.wait_ge(pl, n - 1)
                        for h in range(N_HD):
                            last_ = nc.tensor.transpose(TB[:, n_par(u, x, first), h * P:(h + 1) * P],
                                                        pr[:, u, h, w * P:(w + 1) * P], ident[:])
                        last_.then_inc(tr, 1)
                        if x < N_HD:
                            j = 4 * u + x + AHEAD
                            if j < 16:
                                scores(b, s, j, first)
                            elif not last:
                                scores(b + 1, 1 - s, j - 16, False)
                        if x >= 1:
                            values(b, s, u, x - 1, ws[x - 1], first)
                    values(b, s, u, len(ws) - 1, ws[-1], first)

            loops(pe, body)


def kw_value(b, s):
    return 48 * b + 96 if s == 0 else 48 * b + 80


def vw_value(b, s):
    return 48 * b + 64 if s == 0 else 48 * b + 48


def out_projection1(nc, a):
    ctx = ExitStack()
    with ctx:
        def sb(name, shape, dt=F32):
            return ctx.enter_context(nc.sbuf_tensor(name, shape, dt))

        sem = a["sem"]

        wo_hi, wo_lo = sb("wo1_hi", [P, KT, D], F32R), sb("wo1_lo", [P, KT, D], F32R)
        wr = sb("wr1", [P, 2, D])
        oraw, graw = sb("o_raw", [P, 2, KT, P]), sb("g_raw", [P, 2, KT, P])
        m_hi, m_lo = sb("m1_hi", [P, 2, KT, P], F32R), sb("m1_lo", [P, 2, KT, P], F32R)
        gpb = sb("gpb1", [P, D])
        xt = sb("xt5", [P, 2, D])
        out = sb("out_tiles", [P, 2, D])
        junk = sb("junk5", [P, D])
        st = sb("st5", [P, 3, 2])
        eps = sb("eps5", [P, 1])
        Y = ctx.enter_context(nc.psum_tensor("Y1", [P, 2, D], F32))

        par, wr_ld = sem("out1_par"), [sem("wo1_loaded0"), sem("wo1_loaded1")]
        woh, wol = sem("wo1_hi_done"), [sem("wo1_lo_pool"), sem("wo1_lo_dve")]
        m_ld = [sem("o_loaded0"), sem("o_loaded1")]
        md, mh, ml = sem("mixed1"), sem("m1_hi_done"), sem("m1_lo_done")
        x_ld = [sem("x5_loaded0"), sem("x5_loaded1")]
        yd = sem("y1_product")
        y1, y2, y3, yn, xd = sem("y1_sum"), sem("y1_root"), sem("y1_rstd"), sem("y1_scaled"), sem("out_ready")
        ost, es = [sem("out_stored0"), sem("out_stored1")], sem("eps5_set")
        blk = ctx.enter_context(nc.Block())

        def loops(eng, body):
            body(0, 0, True, False)
            body(1, 1, False, False)
            with eng.Fori(1, LT // 2 - 1) as j:
                body(2 * j, 0, False, False)
                body(2 * j + 1, 1, False, False)
            body(LT - 2, 0, False, False)
            body(LT - 1, 1, False, True)

        def early(t):
            return isinstance(t, int) and t < 2

        @blk.sync
        def _(sp):
            def load(t, s):
                if not early(t):
                    sp.wait_ge(ml, t - 1)
                sp.dma_start(oraw[:, s], a["oT"][t]).then_inc(m_ld[s], 16)
                sp.dma_start(graw[:, s], a["sgT"][t]).then_inc(m_ld[s], 16)
                if not early(t):
                    sp.wait_ge(xd, t - 1)
                sp.dma_start(xt[:, s, :], a["x1"][bass.ds(t * P, P), :]).then_inc(x_ld[s], 16)

            def store(t, s):
                sp.wait_ge(xd, t + 1)
                sp.dma_start(a["out"][0, bass.ds(t * P, P), :], out[:, s, :]).then_inc(ost[s], 16)

            load(0, 0)
            for k in range(KT):
                if k >= 2:
                    sp.wait_ge(wol[k % 2], k // 2)
                sp.dma_start(wr[:, k % 2, :], a["w_out1"][k]).then_inc(wr_ld[k % 2], 16)
            sp.dma_start(gpb[:], a["gp"][1, 0:1].partition_broadcast(P)).then_inc(par, 16)
            load(1, 1)

            def body(t, s, first, last):
                if not first and not last:
                    load(t + 1, 1 - s)
                if not first:
                    store(t - 1, 1 - s)

            loops(sp, body)
            store(LT - 1, 1)
            for s in range(2):
                sp.wait_ge(ost[s], 8 * LT)

        @blk.scalar
        def _(act):
            def split(t, s):
                act.wait_ge(md, t + 1)
                if not early(t):
                    act.wait_ge(yd, t - 1)
                nc.scalar.activation(m_hi[:, s], oraw[:, s], ACT.Copy).then_inc(mh, 1)

            def epilogue(t, s):
                act.wait_ge(yd, t + 1)
                nc.scalar.activation(junk[:], Y[:, s, :], ACT.Square, accum_out=st[:, 0, s:s + 1]).then_inc(y1, 1)
                act.wait_ge(y1, t + 1)
                nc.scalar.activation(st[:, 1, s:s + 1], st[:, 0, s:s + 1], ACT.Sqrt, bias=eps[:, 0:1],
                                     scale=1.0 / D).then_inc(y2, 1)

            split(0, 0)
            for k in range(KT):
                act.wait_ge(wr_ld[k % 2], 16 * (k // 2 + 1))
                nc.scalar.activation(wo_hi[:, k, :], wr[:, k % 2, :], ACT.Copy).then_inc(woh, 1)
            split(1, 1)
            act.wait_ge(es, 1)

            def body(t, s, first, last):
                if not first:
                    epilogue(t - 1, 1 - s)
                    if not last:
                        split(t + 1, 1 - s)

            loops(act, body)
            epilogue(LT - 1, 1)

        @blk.vector
        def _(dve):
            tt, stt = nc.vector.tensor_tensor, nc.vector.scalar_tensor_tensor
            nc.vector.memset(eps[:], EPS).then_inc(es, 1)

            def mix(t, s):
                dve.wait_ge(m_ld[s], 16 * (t - s) + 32)
                stt(out=oraw[:, s], in0=oraw[:, s], scalar=0.5, in1=graw[:, s], op0=ALU.mult, op1=ALU.mult).then_inc(md, 1)

            def epilogue(t, s):
                dve.wait_ge(y2, t + 1)
                nc.vector.reciprocal(st[:, 2, s:s + 1], st[:, 1, s:s + 1]).then_inc(y3, 1)
                dve.wait_ge(y3, t + 1)
                if not early(t):
                    dve.wait_ge(ost[s], 8 * (t - s))
                stt(out=out[:, s, :], in0=Y[:, s, :], scalar=st[:, 2, s:s + 1], in1=gpb[:], op0=ALU.mult,
                    op1=ALU.mult).then_inc(yn, 1)

            mix(0, 0)
            for k in range(1, KT, 2):
                dve.wait_ge(woh, k + 1)
                tt(wo_lo[:, k, :], wr[:, 1, :], v32(wo_hi[:, k, :]), ALU.subtract).then_inc(wol[1], 1)
            mix(1, 1)
            dve.wait_ge(par, 16)

            def body(t, s, first, last):
                if not first:
                    epilogue(t - 1, 1 - s)
                    if not last:
                        mix(t + 1, 1 - s)

            loops(dve, body)
            epilogue(LT - 1, 1)

        @blk.gpsimd
        def _(pool):
            tt = nc.gpsimd.tensor_tensor

            def split(t, s):
                pool.wait_ge(mh, t + 1)
                tt(m_lo[:, s], oraw[:, s], v32(m_hi[:, s]), ALU.subtract).then_inc(ml, 1)

            def epilogue(t, s):
                pool.wait_ge(x_ld[s], 8 * (t - s) + 16)
                pool.wait_ge(yn, t + 1)
                tt(out[:, s, :], out[:, s, :], xt[:, s, :], ALU.add).then_inc(xd, 1)

            split(0, 0)
            for k in range(0, KT, 2):
                pool.wait_ge(woh, k + 1)
                tt(wo_lo[:, k, :], wr[:, 0, :], v32(wo_hi[:, k, :]), ALU.subtract).then_inc(wol[0], 1)
            split(1, 1)

            def body(t, s, first, last):
                if not first:
                    epilogue(t - 1, 1 - s)
                    if not last:
                        split(t + 1, 1 - s)

            loops(pool, body)
            epilogue(LT - 1, 1)

        @blk.tensor
        def _(pe):
            def body(t, s, first, last):
                pe.wait_ge(ml, t + 1)
                if not early(t):
                    pe.wait_ge(yn, t - 1)
                for k in range(KT):
                    if first:
                        pe.wait_ge(wol[k % 2], k // 2 + 1)
                    for n in (0, 512):
                        o = Y[:, s, n:n + 512]
                        w_hi, w_lo = wo_hi[:, k, n:n + 512], wo_lo[:, k, n:n + 512]
                        nc.tensor.matmul(o, m_hi[:, s, k, :], w_hi, start=(k == 0), stop=False)
                        nc.tensor.matmul(o, m_hi[:, s, k, :], w_lo, start=False, stop=False)
                        l = nc.tensor.matmul(o, m_lo[:, s, k, :], w_hi, start=False, stop=(k == KT - 1))
                l.then_inc(yd, 1)

            loops(pe, body)


def rev(buf):
    return buf[:, T - 1::-1]


def tables():
    m = np.arange(P)[:, None].astype(np.float64)
    k = np.arange(P)[None, :].astype(np.float64)
    out = np.zeros((P, TAB_N), np.float64)
    for key, at in TAB_AT.items():
        if isinstance(key, str):
            n, rad, r = N_CTX, 2, int(key[1])
        else:
            n, rad, r = N_LAT, RAD, key
        ang = 2 * np.pi * m * (rad * k + r) / n
        f = 1.0 / np.sqrt(n * P)
        if key in (1, 2, 3):
            out[:, at:at + P] = -np.sin(ang) * f
            at += P
        out[:, at:at + P] = np.cos(ang) * f
        out[:, at + P:at + 256] = np.sin(ang) * f
    ang = 2 * np.pi * m * k / P
    return out.astype(np.float32), np.concatenate([np.cos(ang), np.sin(ang)], 1).astype(np.float32)


def rope_tables():
    p = np.arange(P) % HEAD
    i = (p % 16).astype(np.float32)
    freq = (np.float32(ROPE_BASE) ** (-(2 * i) / np.float32(HEAD // 2))).astype(np.float32)
    tok = np.arange(N_LAT)
    pos = np.where((p < 32)[:, None], tok[None, :] // GRID_W, tok[None, :] % GRID_W).astype(np.float32)
    ang = (pos * freq[:, None]).astype(np.float64)
    sign = np.where(p % 32 < 16, -1.0, 1.0)[:, None]
    return np.stack([np.cos(ang), np.sin(ang) * sign]).astype(np.float32)


def window_mask():
    q, k = np.arange(P)[:, None], np.arange(P)[None, :]
    out = np.zeros((P, 2, WIN * P), np.float32)
    out[:, :, 0:P] = np.where(k >= q, 0.0, NEG_INF)[:, None, :]
    out[:, 0, P:2 * P] = np.where(k <= q, 0.0, NEG_INF)
    out[:, 1, P:2 * P] = NEG_INF
    return out


def paired(w):
    return w.reshape(w.shape[0], 2, 2, N_HD, HEAD).transpose(0, 1, 3, 2, 4).reshape(w.shape[0], D)


def build(nc, a):
    def layer1():
        with nc.sbuf_tensor("gs1", [P, 2, KT, 2], F32) as gs1:
            out_projection0(nc, a, gs1)
        with ExitStack() as ctx:
            k_hi, k_lo = (ctx.enter_context(nc.sbuf_tensor(n, [P, 2, T], F32R)) for n in ("k_hi", "k_lo"))
            vt_hi, vt_lo = (ctx.enter_context(nc.sbuf_tensor(n, [P, TT, 2 * P], F32R)) for n in ("vt_hi", "vt_lo"))
            projections1(nc, a, k_hi, k_lo, vt_hi, vt_lo)
            attention(nc, a, k_hi, k_lo, vt_hi, vt_lo)
        out_projection1(nc, a)

    with_semaphores(nc, a, lambda: layer0(nc, a))
    with_semaphores(nc, a, layer1)


def kernel(**inputs):
    import concourse.bacc as _bacc
    from concourse.bass_utils import run_bass_kernel_spmd as _run

    g = {k: np.ascontiguousarray(v) for k, v in inputs.items()}

    def col(v):
        return v.reshape(-1, KT, P).transpose(2, 0, 1)

    def slabs(w):
        return w.reshape(KT, P, -1, P).transpose(2, 1, 0, 3)

    def rows(layer):
        r = np.concatenate([g[layer + "_b_mod"], g[layer + "_g_pre"], g[layer + "_g_post"]])
        return np.stack([r, r])

    tab, dft_ch = tables()
    w0 = slabs(g["l0_w_in"])
    w_gate = np.stack([g["l0_w_a"][0], g["l0_w_x"][0], g["l0_w_a"][1], g["l0_w_x"][1]])
    w1, kv = g["l1_w_in"], N_KV * HEAD
    qg = np.stack([slabs(paired(w1[:, 0:D])), slabs(paired(w1[:, D + 2 * kv:]))], 1).reshape(2 * KT, P, KT, P)
    w_in1 = np.concatenate([slabs(w1[:, D:D + 2 * kv]), qg]).reshape(-1, P, D)
    arrays = {
        "x": np.concatenate([g["x"][0], g["ctx"][0]]),
        "cvec": np.stack([g["c"][0], g["c_ctx"]]).reshape(2, KT, P).transpose(2, 1, 0),
        "rows0": rows("l0"),
        "rows1": rows("l1"),
        "cols": np.concatenate([col(g["l0_w_conv"]), col(g["l0_b_conv"]), col(g["l0_b_a"]), col(g["l0_b_x"]),
                                col(g["l0_lam"]), col(g["l0_b_f"])], 1),
        "ident": np.eye(P, dtype=np.float32),
        "tables": tab,
        "dft_ch": dft_ch,
        "wm0": g["l0_w_mod"],
        "wm1": g["l1_w_mod"].reshape(KT, P, 2 * KT, MOD_C).transpose(2, 1, 0, 3),
        "w_in0": np.stack([w0[0:8], w0[16:24], w0[24:32], w0[8:16]], 1).reshape(4 * KT, P, D),
        "w_gate": w_gate.reshape(4, KT, 2 * HEAD, HEAD).transpose(1, 2, 0, 3),
        "w_f": g["l0_w_f"],
        "w_out0": g["l0_w_out"],
        "w_in1": w_in1,
        "rope": rope_tables(),
        "sink": np.broadcast_to(g["l1_sink"], (P, N_HEADS)),
        "mask": window_mask(),
        "w_out1": paired(g["l1_w_out"].T).T.reshape(KT, P, D),
    }
    nc = _bacc.Bacc("TRN2", target_bir_lowering=False, num_devices=1, dynamic_dma_scratch_size=1024)
    a = {}
    for name, v in list(arrays.items()):
        arrays[name] = v = np.ascontiguousarray(v)
        a[name] = nc.dram_tensor("in_" + name, v.shape, F32, kind="ExternalInput").ap()
    for name, shape in (("gp", (2, 2, D)), ("mod1", (2, 2 * KT, MOD_C)), ("mixT", (2 * KT, P, T)),
                        ("x1", (N_LAT, D)), ("hT1", (TT, P, KT, P)), ("qT", (LT, P, KT, P)), ("sgT", (LT, P, KT, P)),
                        ("oT", (LT, P, KT, P))):
        a[name] = nc.dram_tensor(name, shape, F32, kind="Internal").ap()
    a["out"] = nc.dram_tensor("out", (1, N_LAT, D), F32, kind="ExternalOutput").ap()
    build(nc, a)
    r = _run(nc, [{"in_" + k: v for k, v in arrays.items()}], core_ids=[0])
    return r.results[0]["out"]
```

```python
import numpy as np
from contextlib import ExitStack

import concourse.bass as bass
from concourse import mybir

F32 = mybir.dt.float32
F32R = mybir.dt.float32r
ALU = mybir.AluOpType
ACT = mybir.ActivationFunctionType
AX = mybir.AxisListType

P = 128
D = 1024
KT = D // P
N_LAT, N_CTX = 1024, 256
T = N_LAT + N_CTX
TT = T // P
LT = N_LAT // P
EPS = 1e-6
CHUNKS = [(0, 512), (512, 512), (1024, 256)]
GRID_W = 64
HEAD = 64
N_HEADS, N_KV = 16, 4
ROPE_BASE = 10000.0
NEG_INF = -1e30
SCALE = HEAD ** -0.5

CONV_W, CONV_LEFT = 4, 2
CTX_AT = N_LAT + CONV_LEFT
CONV_N = CTX_AT + N_CTX

RAD = N_LAT // P
N_R = RAD // 2 + 1
TAB_AT = {0: 0, 4: 256, 1: 512, 2: 896, 3: 1280, "c0": 1664, "c1": 1920}
TAB_N = 2176
PQ_N = (N_R + 2) * 256
UV_N = (N_R + 2) * P

MOD_C = 192
ROWS = 5 * D

C_CONV, C_BCONV, C_BA, C_BX, C_LAM, C_BF, N_COLS = 0, 4, 5, 7, 9, 11, 12
C_HALF, C_KPOS, C_KNEG, C_KNEG2, ALL_COLS = 12, 16, 18, 20, 22


def v32(ap):
    return ap.bitcast(F32)


def with_semaphores(nc, a, stages):
    used = []

    def sem(name):
        used.append(nc.alloc_semaphore(name=name))
        return used[-1]

    a["sem"] = sem
    stages()
    nc.clear_and_free_semaphores(used)
    nc.all_engine_barrier()


def layer0(nc, a):
    ctx = ExitStack()
    with ctx:
        def sb(name, shape, dt=F32):
            return ctx.enter_context(nc.sbuf_tensor(name, shape, dt))

        sem = a["sem"]

        h_hi, h_lo = sb("h_hi", [P, KT, T], F32R), sb("h_lo", [P, KT, T], F32R)
        cols = sb("cols", [P, ALL_COLS, KT])
        silu_c = sb("silu_c", [P, KT, 2])
        setup(nc, a, h_hi, h_lo, cols, silu_c)
        mixers(nc, a, h_hi, h_lo, cols, silu_c)


def setup(nc, a, h_hi, h_lo, cols, silu_c):
    ctx = ExitStack()
    with ctx:
        def sb(name, shape, dt=F32):
            return ctx.enter_context(nc.sbuf_tensor(name, shape, dt))

        sem = a["sem"]

        xt = sb("xt", [P, 2, D])
        junk = sb("junk", [P, D])
        xn = sb("xn", [P, 2, D])
        stat = sb("stat", [P, 3, TT])
        xT = sb("xT", [P, KT, T])
        ident = sb("ident0", [P, P])
        cvec = sb("cvec", [P, KT, 2])
        th_c = sb("th_c", [P, KT, 2])
        wm = sb("wm", [P, 2, 3 * D])
        rows = sb("rows", [2, ROWS])
        mod = sb("mod", [2, 3 * D])
        gs = sb("gs", [P, 2, KT, 2])
        sp_t = sb("sp_t", [P, 6, 2 * KT])
        eps = sb("eps0", [P, 1])
        pm = ctx.enter_context(nc.psum_tensor("pm", [2, 3 * D], F32))
        pt = ctx.enter_context(nc.psum_tensor("pt", [P, 2, 4, P], F32))

        par = sem("par_loaded")
        x_ld = [sem("x_loaded0"), sem("x_loaded1")]
        wm_ld = [sem("wm_loaded0"), sem("wm_loaded1")]
        ss, rt, rs, xs = sem("ss_done"), sem("root_done"), sem("rstd_done"), sem("xn_done")
        tr, te = sem("x_transposed"), sem("xT_written")
        kstep = sem("k_step")
        thc, sc_ = sem("tanh_c"), sem("silu_c_done")
        modk, mrow, mtr, gsd = sem("mod_k_done"), sem("mod_row_done"), sem("mod_transposed"), sem("gs_done")
        hh, h32, hl = sem("h_hi_done"), sem("h32_done"), sem("h_lo_done")
        spre, spost = sem("exp_lam_in"), sem("exp_lam")
        gst, est = sem("gate_row_stored"), sem("eps_set")
        blk = ctx.enter_context(nc.Block())

        def x_tile(i):
            return a["x"][i * P:(i + 1) * P, :]

        @blk.sync
        def _(sp):
            sp.dma_start(cvec[:], a["cvec"]).then_inc(par, 16)
            sp.dma_start(rows[:], a["rows0"]).then_inc(par, 16)
            sp.dma_start(cols[:, 0:N_COLS, :], a["cols"]).then_inc(par, 16)
            sp.dma_start(ident[:], a["ident"]).then_inc(par, 16)
            for i in range(TT):
                if i >= 2:
                    sp.wait_ge(xs, i - 1)
                sp.dma_start(xt[:, i % 2, :], x_tile(i)).then_inc(x_ld[i % 2], 16)
                if i < KT:
                    if i >= 2:
                        sp.wait_ge(modk, i - 1)
                    sp.dma_start(wm[:, i % 2, :], a["wm0"][i * P:(i + 1) * P, :]).then_inc(wm_ld[i % 2], 16)
            sp.wait_ge(mrow, 9)
            sp.dma_start(a["gp"][0], mod[:, 2 * D:3 * D]).then_inc(gst, 16)
            sp.wait_ge(gst, 16)

        @blk.scalar
        def _(act):
            act.wait_ge(par, 64)
            nc.scalar.activation(th_c[:], cvec[:], ACT.Tanh, scale=0.5).then_inc(thc, 1)
            act.wait_ge(spre, 1)
            nc.scalar.activation(sp_t[:, 1, :], sp_t[:, 0, :], ACT.Exp).then_inc(spost, 1)
            act.wait_ge(est, 1)
            for i in range(TT):
                act.wait_ge(x_ld[i % 2], 16 * (i // 2 + 1))
                nc.scalar.activation(junk[:], xt[:, i % 2, :], ACT.Square,
                                     accum_out=stat[:, 0, i:i + 1]).then_inc(ss, 1)
                act.wait_ge(ss, i + 1)
                nc.scalar.activation(stat[:, 1, i:i + 1], stat[:, 0, i:i + 1], ACT.Sqrt,
                                     bias=eps[:, 0:1], scale=1.0 / D).then_inc(rt, 1)
                if i >= 1:
                    for h in range(2):
                        act.wait_ge(tr, 2 * (i - 1) + h + 1)
                        nc.scalar.activation(xT[:, 4 * h:4 * h + 4, (i - 1) * P:i * P], pt[:, h, :, :],
                                             ACT.Copy).then_inc(te, 1)
            for h in range(2):
                act.wait_ge(tr, 2 * (TT - 1) + h + 1)
                nc.scalar.activation(xT[:, 4 * h:4 * h + 4, (TT - 1) * P:TT * P], pt[:, h, :, :],
                                     ACT.Copy).then_inc(te, 1)
            act.wait_ge(te, 2 * TT)
            act.wait_ge(gsd, 1)
            for k in range(KT):
                for w, (at, n) in enumerate([(0, N_LAT), (N_LAT, N_CTX)]):
                    nc.scalar.activation(h_hi[:, k, at:at + n], xT[:, k, at:at + n], ACT.Identity,
                                         scale=gs[:, 1, k, w:w + 1], bias=gs[:, 0, k, w:w + 1]).then_inc(hh, 1)

        @blk.vector
        def _(dve):
            nc.vector.memset(eps[:], EPS).then_inc(est, 1)
            dve.wait_ge(par, 64)
            n = [0]

            def step(ins):
                n[0] += 1
                ins.then_inc(kstep, 1)
                dve.wait_ge(kstep, n[0])

            lam = cols[:, C_LAM:C_LAM + 2, :].rearrange("p a k -> p (a k)")
            step(nc.vector.tensor_scalar(sp_t[:, 2, :], lam, -1.0, None, ALU.mult))
            nc.vector.tensor_tensor(sp_t[:, 0, :], sp_t[:, 2, :], lam, ALU.min).then_inc(spre, 1)
            step(nc.vector.tensor_scalar(cols[:, C_HALF:C_HALF + 4, :].rearrange("p a k -> p (a k)"),
                                         cols[:, C_BA:C_BA + 4, :].rearrange("p a k -> p (a k)"),
                                         0.5, None, ALU.mult))
            dve.wait_ge(spost, 1)
            step(nc.vector.tensor_scalar(sp_t[:, 3, :], sp_t[:, 1, :], 2.0, None, ALU.add))
            step(nc.vector.reciprocal(sp_t[:, 3, :], sp_t[:, 3, :]))
            step(nc.vector.tensor_tensor(sp_t[:, 3, :], sp_t[:, 1, :], sp_t[:, 3, :], ALU.mult))
            step(nc.vector.tensor_tensor(sp_t[:, 4, :], sp_t[:, 3, :], sp_t[:, 3, :], ALU.mult))
            step(nc.vector.tensor_scalar(sp_t[:, 5, :], sp_t[:, 4, :], 1.0 / 17, 1.0 / 15, ALU.mult, ALU.add))
            for q in (13, 11, 9, 7, 5, 3, 1):
                step(nc.vector.tensor_tensor(sp_t[:, 5, :], sp_t[:, 5, :], sp_t[:, 4, :], ALU.mult))
                step(nc.vector.tensor_scalar(sp_t[:, 5, :], sp_t[:, 5, :], 1.0 / q, None, ALU.add))
            step(nc.vector.scalar_tensor_tensor(out=sp_t[:, 5, :], in0=sp_t[:, 5, :], scalar=2.0,
                                                in1=sp_t[:, 3, :], op0=ALU.mult, op1=ALU.mult))
            step(nc.vector.scalar_tensor_tensor(out=sp_t[:, 5, :], in0=sp_t[:, 2, :], scalar=0.0,
                                                in1=sp_t[:, 5, :], op0=ALU.max, op1=ALU.add))
            for at, f in ((C_KPOS, 4.0), (C_KNEG, -4.0), (C_KNEG2, -8.0)):
                step(nc.vector.tensor_scalar(cols[:, at:at + 2, :].rearrange("p a k -> p (a k)"), sp_t[:, 5, :], f, None,
                                             ALU.mult))
            dve.wait_ge(thc, 1)
            step(nc.vector.scalar_tensor_tensor(out=silu_c[:], in0=th_c[:], scalar=1.0, in1=cvec[:],
                                                op0=ALU.add, op1=ALU.mult))
            nc.vector.tensor_scalar(silu_c[:], silu_c[:], 0.5, None, ALU.mult).then_inc(sc_, 1)
            for i in range(TT):
                dve.wait_ge(rt, i + 1)
                nc.vector.reciprocal(stat[:, 2, i:i + 1], stat[:, 1, i:i + 1]).then_inc(rs, 1)
                dve.wait_ge(rs, i + 1)
                if i >= 2:
                    dve.wait_ge(tr, 2 * (i - 1))
                nc.vector.tensor_scalar(xn[:, i % 2, :], xt[:, i % 2, :], stat[:, 2, i:i + 1], None,
                                        ALU.mult).then_inc(xs, 1)
            dve.wait_ge(modk, KT)
            for c in range(6):
                nc.vector.tensor_tensor(mod[:, c * 512:(c + 1) * 512], pm[:, c * 512:(c + 1) * 512],
                                        rows[:, c * 512:(c + 1) * 512], ALU.add).then_inc(mrow, 1)
            dve.wait_ge(mrow, 6)
            nc.vector.scalar_tensor_tensor(out=mod[:, D:2 * D], in0=mod[:, D:2 * D], scalar=1.0,
                                           in1=rows[:, 3 * D:4 * D], op0=ALU.add, op1=ALU.mult).then_inc(mrow, 1)
            dve.wait_ge(mtr, 1)
            nc.vector.tensor_copy(gs[:].rearrange("p a k w -> p (a k w)"), pm_cols(pt)).then_inc(gsd, 1)
            nc.vector.tensor_tensor(mod[:, 2 * D:3 * D], mod[:, 2 * D:3 * D], rows[:, 4 * D:5 * D],
                                    ALU.mult).then_inc(mrow, 2)
            dve.wait_ge(te, 2 * TT)
            dve.wait_ge(gsd, 1)
            for k in range(KT):
                dve.wait_ge(hh, 2 * k + 2)
                for w, (at, n_) in enumerate([(0, N_LAT), (N_LAT, N_CTX)]):
                    nc.vector.tensor_scalar(xT[:, k, at:at + n_], xT[:, k, at:at + n_], gs[:, 1, k, w:w + 1],
                                            gs[:, 0, k, w:w + 1], ALU.mult, ALU.add).then_inc(h32, 1)
                if k % 2 == 1:
                    dve.wait_ge(h32, 2 * k + 2)
                    nc.vector.tensor_tensor(h_lo[:, k, :], xT[:, k, :], v32(h_hi[:, k, :]),
                                            ALU.subtract).then_inc(hl, 1)

        @blk.gpsimd
        def _(pool):
            for k in range(0, KT, 2):
                pool.wait_ge(h32, 2 * k + 2)
                nc.gpsimd.tensor_tensor(h_lo[:, k, :], xT[:, k, :], v32(h_hi[:, k, :]), ALU.subtract).then_inc(hl, 1)

        @blk.tensor
        def _(pe):
            pe.wait_ge(sc_, 1)
            for i in range(TT):
                pe.wait_ge(xs, i + 1)
                for h in range(2):
                    if i >= 1:
                        pe.wait_ge(te, 2 * (i - 1) + h + 1)
                    for q in range(4):
                        last = nc.tensor.transpose(pt[:, h, q, :], xn[:, i % 2, (4 * h + q) * P:(4 * h + q + 1) * P],
                                                   ident[:])
                    last.then_inc(tr, 1)
                if i < KT:
                    pe.wait_ge(wm_ld[i % 2], 16 * (i // 2 + 1))
                    for c in range(6):
                        last = nc.tensor.matmul(pm[:, c * 512:(c + 1) * 512], silu_c[:, i, :],
                                                wm[:, i % 2, c * 512:(c + 1) * 512], start=(i == 0), stop=(i == KT - 1))
                    last.then_inc(modk, 1)
            pe.wait_ge(te, 2 * TT)
            pe.wait_ge(mrow, 7)
            for q in range(2 * KT):
                last = nc.tensor.transpose(pt[:, 0, 0, 2 * q:2 * q + 2], mod[:, q * P:(q + 1) * P], ident[0:2, 0:2])
            last.then_inc(mtr, 1)


def pm_cols(pt):
    return pt[:, 0, 0, 0:4 * KT]


def mixers(nc, a, h_hi, h_lo, cols, silu_c):
    ctx = ExitStack()
    with ctx:
        def sb(name, shape, dt=F32):
            return ctx.enter_context(nc.sbuf_tensor(name, shape, dt))

        sem = a["sem"]

        wraw = sb("wraw", [P, 2, D])
        w_hi, w_lo = sb("w_hi", [P, 2, KT, P], F32R), sb("w_lo", [P, 2, KT, P], F32R)
        tab_hi, tab_lo = sb("tab_hi", [P, TAB_N], F32R), sb("tab_lo", [P, TAB_N], F32R)
        dft_ch = sb("dft_ch", [P, 256])
        ident = sb("ident1", [P, P])
        u_raw = sb("u_raw", [P, CONV_N + CONV_W - 1])
        u = sb("u", [P, T])
        u_hi, u_lo = sb("u_hi", [P, T], F32R), sb("u_lo", [P, T], F32R)
        cur = sb("cur", [P, ALL_COLS])
        gw = sb("gw", [P, 4, P])
        gw_hi, gw_lo = sb("gw_hi", [P, 4, P], F32R), sb("gw_lo", [P, 4, P], F32R)
        A, B, C = sb("A", [P, T]), sb("B", [P, T]), sb("C", [P, T])
        E = sb("E", [P, CONV_N])
        H = sb("H", [P, T])
        sgf = sb("sgf", [P, T])
        fT = sb("fT", [P, T])
        xf = sb("xf", [P, T])
        y_hi, y_lo = sb("y_hi", [P, T], F32R), sb("y_lo", [P, T], F32R)
        pq_hi, pq_lo = sb("pq_hi", [P, PQ_N], F32R), sb("pq_lo", [P, PQ_N], F32R)
        wf = sb("wf", [P, P])
        ab_hi, ab_lo = sb("ab_hi", [P, 2 * P], F32R), sb("ab_lo", [P, 2 * P], F32R)
        wm1 = sb("wm1", [P, KT, MOD_C])
        m_row = sb("m_row", [2, MOD_C])
        slab = ctx.enter_context(nc.psum_tensor("slab", [P, 3, 512], F32))
        W = ctx.enter_context(nc.psum_tensor("W", [P, 4, 512], F32))
        W4 = ctx.enter_context(nc.psum_tensor("W4", [P, 512], F32))
        Wf = W[:].rearrange("p b n -> p (b n)")

        par = sem("mix_par_loaded")
        tab_ld, tab_h, tab_l = sem("table_loaded"), sem("table_hi"), sem("table_lo")
        zero, cu_ = sem("zeros_set"), sem("columns_copied")
        w_ld = [sem("w_loaded0"), sem("w_loaded1")]
        wh = [sem("w_hi_done0"), sem("w_hi_done1")]
        wl = [sem("w_lo_done0"), sem("w_lo_done1")]
        gw_ld, gwh, gwl = sem("gate_w_loaded"), sem("gate_w_hi"), sem("gate_w_lo")
        wf_ld, abp, abh, abl = sem("wf_loaded"), sem("ab_product"), sem("ab_hi_done"), sem("ab_lo_done")
        s_u, s_f, s_gf, s_g = sem("slab_u"), sem("slab_f"), sem("slab_gf"), sem("slab_g")
        ur, tap0, taps, conv = sem("u_raw_ready"), sem("tap0"), sem("taps"), sem("conv_done")
        uh, ul = sem("u_hi_done"), sem("u_lo_done")
        fr, trd, xr = sem("fT_ready"), sem("f_transposed"), sem("x_ready")
        bf, yr, yh, yl = sem("butterfly"), sem("y_ready"), sem("y_hi_done"), sem("y_lo_done")
        dft, pqh, pql, uv, us, yd = sem("dft_done"), sem("pq_hi"), sem("pq_lo"), sem("uv_done"), sem("us_ready"), sem("y_combined")
        tgf, sgfd, tg, sg = sem("tanh_gf"), sem("silu_gf"), sem("tanh_g"), sem("silu_g")
        gp_, gr = sem("gate_product"), sem("gate_read")
        th, e2, ea = sem("tanh_loga"), sem("a_squared"), sem("a_ready")
        iu, om, sq, bt, hd, hs = sem("iu"), sem("one_minus_a2"), sem("root"), sem("b_ready"), sem("scan_done"), sem("h_sum")
        cf = sem("scan_ctx")
        mf, mr, mfs, mrs = sem("mix_f"), sem("mix_r"), sem("mix_f_stored"), sem("mix_r_stored")
        m_ld, mp, me, ms = sem("wmod1_loaded"), sem("mod1_product"), sem("mod1_row"), sem("mod1_stored")
        blk = ctx.enter_context(nc.Block())
        SLAB_U, SLAB_F, SLAB_GF, SLAB_G = range(4)
        done = [s_u, s_f, s_gf, s_g]
        tab_pieces = [(0, 1024), (1024, 1024), (2048, TAB_N - 2048)]

        def loops(eng, body, n=KT):
            body(0, True, False)
            with eng.Fori(1, n - 1) as t:
                body(t, False, False)
            body(n - 1, False, True)

        @blk.sync
        def _(sp):
            sp.dma_start(dft_ch[:], a["dft_ch"]).then_inc(par, 16)
            sp.dma_start(ident[:], a["ident"]).then_inc(par, 16)

            def load_slab(t, j, first):
                if not (first and j < 2):
                    sp.wait_ge(wl[j % 2], 2 * t + j // 2)
                sp.dma_start(wraw[:, j % 2, :], a["w_in0"][4 * t + j]).then_inc(w_ld[j % 2], 16)

            def store(t):
                sp.wait_ge(mr, t + 1)
                sp.dma_start(a["mixT"][t], H[:]).then_inc(mrs, 16)
                sp.wait_ge(mf, t + 1)
                sp.dma_start(a["mixT"][t + KT], xf[:]).then_inc(mfs, 16)
                store_mod(t, 1)

            def store_mod(t, q):
                sp.wait_ge(me, 2 * t + q + 1)
                sp.dma_start(a["mod1"][:, 2 * t + q, :], m_row[:]).then_inc(ms, 16)

            def load_mod(t, q, first):
                if not (first and q == 0):
                    sp.wait_ge(mp, 2 * t + q)
                sp.dma_start(wm1[:], a["wm1"][2 * t + q]).then_inc(m_ld, 16)

            def body(t, first, last):
                if first:
                    load_slab(t, SLAB_U, first)
                    load_slab(t, SLAB_F, first)
                    for i, (at, n) in enumerate(tab_pieces):
                        if i:
                            sp.wait_ge(tab_l, i)
                        sp.dma_start(fT[:, 0:n], a["tables"][:, at:at + n]).then_inc(tab_ld, 16)
                load_mod(t, 0, first)
                if first:
                    sp.wait_ge(zero, 2)
                else:
                    sp.wait_ge(gwl, t)
                for c in range(2):
                    sp.dma_start(gw[HEAD * c:HEAD * (c + 1), :, HEAD * c:HEAD * (c + 1)],
                                 a["w_gate"][t, HEAD * c:HEAD * (c + 1), :, :]).then_inc(gw_ld, 16)
                if not first:
                    sp.wait_ge(abp, t)
                sp.dma_start(wf[:], a["w_f"][t]).then_inc(wf_ld, 16)
                load_slab(t, SLAB_GF, first)
                load_slab(t, SLAB_G, first)
                if not first:
                    store(t - 1)
                store_mod(t, 0)
                load_mod(t, 1, first)
                if not last:
                    load_slab(t + 1, SLAB_U, False)
                    load_slab(t + 1, SLAB_F, False)

            loops(sp, body)
            store(KT - 1)
            sp.wait_ge(mrs, 16 * KT)
            sp.wait_ge(mfs, 16 * KT)
            sp.wait_ge(ms, 32 * KT)

        @blk.scalar
        def _(act):
            def split_hi(t, j, first=False):
                act.wait_ge(w_ld[j % 2], 16 * (2 * t + j // 2 + 1))
                if j >= 2:
                    act.wait_ge(done[j - 2], 3 * t + 3)
                elif not first:
                    act.wait_ge(done[j + 2], 3 * t)
                nc.scalar.activation(w_hi[:, j % 2].rearrange("p k n -> p (k n)"), wraw[:, j % 2, :],
                                     ACT.Copy).then_inc(wh[j % 2], 1)

            def gates(t, d, first):
                for x in range(2):
                    dst = (A, B)[x]
                    if x == 0:
                        if d == 1:
                            act.wait_ge(hd, 2 * t + 1)
                        elif not first:
                            act.wait_ge(mr, t)
                    for c, (at, n) in enumerate(CHUNKS):
                        k = 6 * d + 3 * x + c
                        act.wait_ge(gp_, 12 * t + k + 1)
                        nc.scalar.activation(dst[:, at:at + n], W[:, k % 4, 0:n], ACT.Tanh, scale=0.5,
                                             bias=cur[:, C_HALF + 2 * x + d:C_HALF + 2 * x + d + 1]).then_inc(gr, 1)
                act.wait_ge(gr, 12 * t + 6 * d + 3)
                if d == 0:
                    act.wait_ge(conv, 2 * t + 2)
                else:
                    act.wait_ge(bt, 2 * t + 1)
                nc.scalar.activation(E[:, 0:T], A[:], ACT.Tanh, scale=cur[:, C_KPOS + d:C_KPOS + d + 1],
                                     bias=cur[:, C_KPOS + d:C_KPOS + d + 1]).then_inc(th, 1)
                nc.scalar.activation(C[:], A[:], ACT.Exp, scale=cur[:, C_KNEG2 + d:C_KNEG2 + d + 1],
                                     bias=cur[:, C_KNEG2 + d:C_KNEG2 + d + 1]).then_inc(e2, 1)
                act.wait_ge(e2, 2 * t + d + 1)
                act.wait_ge(th, 2 * t + d + 1)
                nc.scalar.activation(A[:], A[:], ACT.Exp, scale=cur[:, C_KNEG + d:C_KNEG + d + 1],
                                     bias=cur[:, C_KNEG + d:C_KNEG + d + 1]).then_inc(ea, 1)

            def root(t, d):
                act.wait_ge(om, 2 * t + d + 1)
                nc.scalar.activation(C[:], C[:], ACT.Sqrt).then_inc(sq, 1)

            def mod_row(t, q, first):
                act.wait_ge(mp, 2 * t + q + 1)
                if not (first and q == 0):
                    act.wait_ge(ms, 16 * (2 * t + q))
                nc.scalar.activation(m_row[:], W4[0:2, 0:MOD_C], ACT.Copy).then_inc(me, 1)

            def body(t, first, last):
                split_hi(t, SLAB_F, first)
                if first:
                    act.wait_ge(zero, 2)
                else:
                    act.wait_ge(conv, 2 * t)
                for c, (at, n) in enumerate(CHUNKS):
                    act.wait_ge(s_u, 3 * t + c + 1)
                    to = CONV_LEFT + at + (CTX_AT - N_LAT if c == 2 else 0)
                    nc.scalar.activation(u_raw[:, to:to + n], slab[:, c, 0:n], ACT.Copy).then_inc(ur, 1)
                if not first:
                    act.wait_ge(hs, t)
                act.wait_ge(ur, 3 * t + 3)
                act.wait_ge(cu_, t + 1)
                nc.scalar.activation(E[:], u_raw[:, 0:CONV_N], ACT.Identity, scale=cur[:, C_CONV:C_CONV + 1],
                                     bias=cur[:, C_BCONV:C_BCONV + 1]).then_inc(tap0, 1)
                mod_row(t, 0, first)
                split_hi(t, SLAB_GF)
                act.wait_ge(gw_ld, 32 * t + 32)
                if not first:
                    act.wait_ge(gp_, 12 * t)
                nc.scalar.activation(gw_hi[:], gw[:], ACT.Copy).then_inc(gwh, 1)
                act.wait_ge(conv, 2 * t + 2)
                nc.scalar.activation(u_hi[:], u[:], ACT.Copy).then_inc(uh, 1)
                if not first:
                    act.wait_ge(yd, t)
                else:
                    act.wait_ge(tab_l, 3)
                for c, (at, n) in enumerate(CHUNKS):
                    act.wait_ge(s_f, 3 * t + c + 1)
                    nc.scalar.activation(fT[:, at:at + n], slab[:, c, 0:n], ACT.Copy).then_inc(fr, 1)
                if not first:
                    act.wait_ge(mfs, 16 * t)
                for c, (at, n) in enumerate(CHUNKS):
                    act.wait_ge(trd, 3 * t + c + 1)
                    nc.scalar.activation(xf[:, at:at + n], W[:, c, 0:n], ACT.Copy).then_inc(xr, 1)
                act.wait_ge(abp, t + 1)
                nc.scalar.activation(ab_hi[:], W4[:, 0:256], ACT.Copy).then_inc(abh, 1)
                gates(t, 0, first)
                split_hi(t, SLAB_G)
                act.wait_ge(yr, t + 1)
                if not first:
                    act.wait_ge(dft, t)
                nc.scalar.activation(y_hi[:], xf[:], ACT.Copy).then_inc(yh, 1)
                root(t, 0)
                if not first:
                    act.wait_ge(mf, t)
                for c, (at, n) in enumerate(CHUNKS):
                    act.wait_ge(s_gf, 3 * t + c + 1)
                    nc.scalar.activation(sgf[:, at:at + n], slab[:, c, 0:n], ACT.Tanh, scale=0.5).then_inc(tgf, 1)
                gates(t, 1, first)
                act.wait_ge(dft, t + 1)
                if not first:
                    act.wait_ge(uv, t)
                nc.scalar.activation(pq_hi[:], Wf[:, 0:PQ_N], ACT.Copy).then_inc(pqh, 1)
                if not last:
                    split_hi(t + 1, SLAB_U)
                root(t, 1)
                act.wait_ge(hd, 2 * t + 2)
                for c, (at, n) in enumerate(CHUNKS):
                    act.wait_ge(s_g, 3 * t + c + 1)
                    nc.scalar.activation(B[:, at:at + n], slab[:, c, 0:n], ACT.Tanh, scale=0.5).then_inc(tg, 1)
                act.wait_ge(uv, t + 1)
                nc.scalar.activation(fT[:, 0:UV_N], Wf[:, 0:UV_N], ACT.Identity,
                                     bias=cur[:, C_BF:C_BF + 1]).then_inc(us, 1)
                mod_row(t, 1, first)

            split_hi(0, SLAB_U, True)
            for i, (at, n) in enumerate(tab_pieces):
                act.wait_ge(tab_ld, 16 * (i + 1))
                nc.scalar.activation(tab_hi[:, at:at + n], fT[:, 0:n], ACT.Copy).then_inc(tab_h, 1)
            loops(act, body)

        @blk.vector
        def _(dve):
            nc.vector.memset(u_raw[:], 0.0).then_inc(zero, 1)
            nc.vector.memset(gw[:], 0.0).then_inc(zero, 1)

            def body(t, first, last):
                if not first:
                    dve.wait_ge(us, t)
                nc.vector.tensor_scalar(cur[:], cols[:, :, t], 1.0, None, ALU.mult).then_inc(cu_, 1)
                dve.wait_ge(tap0, t + 1)
                for k in (1, 2):
                    nc.vector.scalar_tensor_tensor(out=E[:], in0=u_raw[:, k:k + CONV_N],
                                                   scalar=cur[:, C_CONV + k:C_CONV + k + 1], in1=E[:],
                                                   op0=ALU.mult, op1=ALU.add).then_inc(taps, 1)
                    dve.wait_ge(taps, 2 * t + k)
                if not first:
                    dve.wait_ge(ul, t)
                for at, to, n in ((0, 0, N_LAT), (CTX_AT, N_LAT, N_CTX)):
                    nc.vector.scalar_tensor_tensor(out=u[:, to:to + n], in0=u_raw[:, at + 3:at + 3 + n],
                                                   scalar=cur[:, C_CONV + 3:C_CONV + 4], in1=E[:, at:at + n],
                                                   op0=ALU.mult, op1=ALU.add).then_inc(conv, 1)
                nb = 8
                b0 = nb * t

                def q(buf, i, n=1):
                    return buf[:, i * P:(i + n) * P]

                def bstep(k, ins):
                    ins.then_inc(bf, 1)

                dve.wait_ge(xr, 3 * t + 3)
                tt = nc.vector.tensor_tensor
                bstep(1, tt(q(fT, 0, 4), q(xf, 0, 4), q(xf, 4, 4), ALU.add))
                bstep(2, tt(q(fT, 4, 4), q(xf, 0, 4), q(xf, 4, 4), ALU.subtract))
                bstep(3, tt(q(fT, 8), q(xf, 8), q(xf, 9), ALU.subtract))
                bstep(4, tt(q(fT, 9), q(xf, 8), q(xf, 9), ALU.add))
                dve.wait_ge(bf, b0 + 4)
                bstep(5, tt(q(xf, 6, 2), q(fT, 0, 2), q(fT, 2, 2), ALU.add))
                bstep(6, tt(q(xf, 4, 2), q(fT, 0, 2), q(fT, 2, 2), ALU.subtract))
                dve.wait_ge(bf, b0 + 6)
                bstep(7, tt(q(fT, 0), q(fT, 5), q(fT, 7), ALU.add))
                bstep(8, tt(q(fT, 1), q(fT, 5), q(fT, 7), ALU.subtract))
                dve.wait_ge(bf, b0 + 8)
                stt = nc.vector.scalar_tensor_tensor
                s = float(np.sqrt(0.5))
                tt(q(xf, 0), q(xf, 6), q(xf, 7), ALU.add).then_inc(bf2, 1)
                tt(q(xf, 1), q(xf, 6), q(xf, 7), ALU.subtract).then_inc(bf2, 1)
                stt(out=q(xf, 2), in0=q(fT, 1), scalar=s, in1=q(fT, 4), op0=ALU.mult, op1=ALU.add).then_inc(bf2, 1)
                stt(out=q(xf, 3), in0=q(fT, 0), scalar=s, in1=q(fT, 6), op0=ALU.mult, op1=ALU.add).then_inc(bf2, 1)
                dve.wait_ge(bf2, 4 * t + 4)
                stt(out=q(xf, 6), in0=q(fT, 1), scalar=-s, in1=q(fT, 4), op0=ALU.mult, op1=ALU.add).then_inc(bf3, 1)
                stt(out=q(xf, 7), in0=q(fT, 0), scalar=s, in1=q(fT, 6), op0=ALU.mult, op1=ALU.subtract).then_inc(bf3, 1)
                nc.vector.tensor_copy(q(xf, 8), q(fT, 9)).then_inc(bf3, 1)
                nc.vector.tensor_copy(q(xf, 9), q(fT, 8)).then_inc(yr, 1)
                dve.wait_ge(abh, t + 1)
                tt(ab_lo[:], W4[:, 0:256], v32(ab_hi[:]), ALU.subtract).then_inc(abl, 1)

                def direction(d):
                    dve.wait_ge(gr, 12 * t + 6 * d + 6)
                    stt(out=B[:], in0=B[:], scalar=1.0, in1=u[:], op0=ALU.add, op1=ALU.mult).then_inc(iu, 1)
                    dve.wait_ge(th, 2 * t + d + 1)
                    dve.wait_ge(e2, 2 * t + d + 1)
                    stt(out=C[:], in0=C[:], scalar=1.0, in1=E[:, 0:T], op0=ALU.add, op1=ALU.mult).then_inc(om, 1)

                def scan(d):
                    dve.wait_ge(sq, 2 * t + d + 1)
                    dve.wait_ge(iu, 2 * t + d + 1)
                    stt(out=B[:], in0=C[:], scalar=0.5, in1=B[:], op0=ALU.mult, op1=ALU.mult).then_inc(bt, 1)
                    dve.wait_ge(bt, 2 * t + d + 1)
                    dve.wait_ge(ea, 2 * t + d + 1)
                    if d == 0:
                        if not first:
                            dve.wait_ge(mrs, 16 * t)
                        nc.vector.tensor_tensor_scan(H[:, N_LAT:T], A[:, N_LAT:T], B[:, N_LAT:T], 0.0,
                                                     ALU.mult, ALU.add).then_inc(cf, 1)
                        dve.wait_ge(cf, t + 1)
                        nc.vector.tensor_tensor_scan(H[:, 0:N_LAT], A[:, 0:N_LAT], B[:, 0:N_LAT], H[:, T - 1:T],
                                                     ALU.mult, ALU.add).then_inc(hd, 1)
                    else:
                        nc.vector.tensor_tensor_scan(rev(E), rev(A), rev(B), 0.0,
                                                     ALU.mult, ALU.add).then_inc(hd, 1)

                direction(0)
                scan(0)
                for c, (at, n) in enumerate(CHUNKS):
                    dve.wait_ge(tgf, 3 * t + c + 1)
                    stt(out=sgf[:, at:at + n], in0=sgf[:, at:at + n], scalar=1.0, in1=slab[:, c, 0:n],
                        op0=ALU.add, op1=ALU.mult).then_inc(sgfd, 1)
                direction(1)
                dve.wait_ge(pqh, t + 1)
                tt(pq_lo[:], Wf[:, 0:PQ_N], v32(pq_hi[:]), ALU.subtract).then_inc(pql, 1)
                scan(1)
                for c, (at, n) in enumerate(CHUNKS):
                    dve.wait_ge(tg, 3 * t + c + 1)
                    stt(out=B[:, at:at + n], in0=B[:, at:at + n], scalar=1.0, in1=slab[:, c, 0:n],
                        op0=ALU.add, op1=ALU.mult).then_inc(sg, 1)
                dve.wait_ge(us, t + 1)
                dve.wait_ge(yl, t + 1)
                lat = xf[:, 0:N_LAT].rearrange("p (k r) -> p r k", r=RAD)
                cu = fT[:, 0:UV_N].rearrange("p (r k) -> p r k", k=P)
                sv = Wf[:, 2 * 512:2 * 512 + UV_N].rearrange("p (r k) -> p r k", k=P)
                tt(lat[:, 0:N_R, :], cu[:, 0:N_R, :], sv[:, 0:N_R, :], ALU.subtract).then_inc(yc, 1)
                for r in range(1, RAD - N_R + 1):
                    tt(lat[:, RAD - r, ::-1], cu[:, r, :], sv[:, r, :], ALU.add).then_inc(yc, 1)
                cx = xf[:, N_LAT:T].rearrange("p (k r) -> p r k", r=2)
                tt(cx, cu[:, N_R:N_R + 2, :], sv[:, N_R:N_R + 2, :], ALU.subtract).then_inc(yd, 1)
                dve.wait_ge(yc, 4 * t + 4)
                dve.wait_ge(yd, t + 1)
                dve.wait_ge(sgfd, 3 * t + 3)
                stt(out=xf[:], in0=xf[:], scalar=0.5, in1=sgf[:], op0=ALU.mult, op1=ALU.mult).then_inc(mf, 1)
                dve.wait_ge(hs, t + 1)
                dve.wait_ge(sg, 3 * t + 3)
                stt(out=H[:], in0=H[:], scalar=0.5, in1=B[:], op0=ALU.mult, op1=ALU.mult).then_inc(mr, 1)

            bf2, bf3, yc = sem("butterfly2"), sem("butterfly3"), sem("y_parts")
            loops(dve, body)

        @blk.gpsimd
        def _(pool):
            sub = nc.gpsimd.tensor_tensor

            def split_lo(t, j):
                pool.wait_ge(wh[j % 2], 2 * t + j // 2 + 1)
                sub(w_lo[:, j % 2].rearrange("p k n -> p (k n)"), wraw[:, j % 2, :],
                    v32(w_hi[:, j % 2].rearrange("p k n -> p (k n)")), ALU.subtract).then_inc(wl[j % 2], 1)

            def body(t, first, last):
                split_lo(t, SLAB_F)
                split_lo(t, SLAB_GF)
                pool.wait_ge(gwh, t + 1)
                sub(gw_lo[:], gw[:], v32(gw_hi[:]), ALU.subtract).then_inc(gwl, 1)
                pool.wait_ge(uh, t + 1)
                sub(u_lo[:], u[:], v32(u_hi[:]), ALU.subtract).then_inc(ul, 1)
                split_lo(t, SLAB_G)
                pool.wait_ge(yh, t + 1)
                sub(y_lo[:], xf[:], v32(y_hi[:]), ALU.subtract).then_inc(yl, 1)
                if not last:
                    split_lo(t + 1, SLAB_U)
                pool.wait_ge(hd, 2 * t + 2)
                sub(H[:], H[:], E[:, 0:T], ALU.add).then_inc(hs, 1)

            split_lo(0, SLAB_U)
            for i, (at, n) in enumerate(tab_pieces):
                pool.wait_ge(tab_h, i + 1)
                sub(tab_lo[:, at:at + n], fT[:, 0:n], v32(tab_hi[:, at:at + n]), ALU.subtract).then_inc(tab_l, 1)
            loops(pool, body)

        @blk.tensor
        def _(pe):
            def mm3(out, l_hi, l_lo, r_hi, r_lo, start, stop):
                nc.tensor.matmul(out, l_hi, r_hi, start=start, stop=False)
                nc.tensor.matmul(out, l_hi, r_lo, start=False, stop=False)
                return nc.tensor.matmul(out, l_lo, r_hi, start=False, stop=stop)

            def slab_product(t, j, first):
                pe.wait_ge(wl[j % 2], 2 * t + j // 2 + 1)
                for c, (at, n) in enumerate(CHUNKS):
                    if j == SLAB_F:
                        pe.wait_ge(ur, 3 * t + c + 1)
                    elif j == SLAB_GF:
                        pe.wait_ge(fr, 3 * t + c + 1)
                    elif j == SLAB_G:
                        pe.wait_ge(sgfd, 3 * t + c + 1)
                    elif not first:
                        pe.wait_ge(sg, 3 * (t - 1) + c + 1)
                    for k in range(KT):
                        last = mm3(slab[:, c, 0:n], w_hi[:, j % 2, k, :], w_lo[:, j % 2, k, :],
                                   h_hi[:, k, at:at + n], h_lo[:, k, at:at + n], k == 0, k == KT - 1)
                    last.then_inc(done[j], 1)

            def gate_products(t, d):
                for x in range(2):
                    for c, (at, n) in enumerate(CHUNKS):
                        k = 6 * d + 3 * x + c
                        if k < 3:
                            pe.wait_ge(xr, 3 * t + k + 1)
                        elif k > 3:
                            pe.wait_ge(gr, 12 * t + k - 3)
                        mm3(W[:, k % 4, 0:n], gw_hi[:, 2 * d + x, :], gw_lo[:, 2 * d + x, :],
                            u_hi[:, at:at + n], u_lo[:, at:at + n], True, True).then_inc(gp_, 1)

            def mod_product(t, q, first):
                pe.wait_ge(m_ld, 16 * (2 * t + q + 1))
                if q == 1:
                    pe.wait_ge(abl, t + 1)
                elif not first:
                    pe.wait_ge(me, 2 * t)
                for k in range(KT):
                    last = nc.tensor.matmul(W4[0:2, 0:MOD_C], silu_c[:, k, :], wm1[:, k, :],
                                            start=(k == 0), stop=(k == KT - 1))
                last.then_inc(mp, 1)

            def dft_product(t):
                pe.wait_ge(gr, 12 * t + 12)
                pe.wait_ge(yl, t + 1)
                for i in range(N_R + 2):
                    key = i if i < N_R else ("c0", "c1")[i - N_R]
                    at = TAB_AT[key]
                    out = Wf[:, 256 * i:256 * i + 256]
                    if key in (1, 2, 3):
                        re, im = ((2, 3), (4, 5), (6, 7))[key - 1]
                        ys = slice(re * P, re * P + P)
                        mm3(out, y_hi[:, ys], y_lo[:, ys], tab_hi[:, at + P:at + P + 256],
                            tab_lo[:, at + P:at + P + 256], True, False)
                        ys = slice(im * P, im * P + P)
                        last = mm3(out, y_hi[:, ys], y_lo[:, ys], tab_hi[:, at:at + 256],
                                   tab_lo[:, at:at + 256], False, True)
                    else:
                        y = {0: 0, 4: 1, "c0": 8, "c1": 9}[key]
                        ys = slice(y * P, y * P + P)
                        last = mm3(out, y_hi[:, ys], y_lo[:, ys], tab_hi[:, at:at + 256], tab_lo[:, at:at + 256],
                                   True, True)
                last.then_inc(dft, 1)

            def body(t, first, last_):
                slab_product(t, SLAB_U, first)
                mod_product(t, 0, first)
                slab_product(t, SLAB_F, first)
                pe.wait_ge(fr, 3 * t + 3)
                if first:
                    pe.wait_ge(par, 32)
                else:
                    pe.wait_ge(yd, t)
                for i in range(TT):
                    last = nc.tensor.transpose(W[:, i // 4, (i % 4) * P:(i % 4 + 1) * P], fT[:, i * P:(i + 1) * P],
                                               ident[:])
                    if i % 4 == 3 or i == TT - 1:
                        last.then_inc(trd, 1)
                pe.wait_ge(wf_ld, 16 * t + 16)
                pe.wait_ge(me, 2 * t + 1)
                for x in range(2):
                    last = nc.tensor.matmul(W4[:, x * P:(x + 1) * P], dft_ch[:, x * P:(x + 1) * P], wf[:],
                                            start=True, stop=True)
                last.then_inc(abp, 1)
                pe.wait_ge(gwl, t + 1)
                pe.wait_ge(ul, t + 1)
                gate_products(t, 0)
                slab_product(t, SLAB_GF, first)
                gate_products(t, 1)
                dft_product(t)
                slab_product(t, SLAB_G, first)
                pe.wait_ge(pql, t + 1)
                pe.wait_ge(abl, t + 1)
                for x in range(2):
                    hi = pq_hi[:].rearrange("p (r x k) -> p r x k", x=2, k=P)[:, :, x, :]
                    lo = pq_lo[:].rearrange("p (r x k) -> p r x k", x=2, k=P)[:, :, x, :]
                    for b, (r0, r1) in enumerate(((0, 4), (4, N_R + 2))):
                        last = mm3(W[:, 2 * x + b, 0:(r1 - r0) * P], ab_hi[:, x * P:(x + 1) * P],
                                   ab_lo[:, x * P:(x + 1) * P], hi[:, r0:r1, :], lo[:, r0:r1, :], True, True)
                last.then_inc(uv, 1)
                mod_product(t, 1, first)

            pe.wait_ge(tab_l, 3)
            loops(pe, body)


def out_projection0(nc, a, gs1):
    ctx = ExitStack()
    with ctx:
        def sb(name, shape, dt=F32):
            return ctx.enter_context(nc.sbuf_tensor(name, shape, dt))

        sem = a["sem"]

        K2 = 2 * KT
        wo_hi, wo_lo = sb("wo_hi", [P, K2, D], F32R), sb("wo_lo", [P, K2, D], F32R)
        wr = sb("wr", [P, 2, D])
        mraw = sb("mraw", [P, 2, KT, P])
        m_hi, m_lo = sb("m_hi", [P, 2, KT, P], F32R), sb("m_lo", [P, 2, KT, P], F32R)
        gpb = sb("gpb", [P, 2, D])
        xt = sb("xt2", [P, 2, D])
        x1 = sb("x1_tiles", [P, 2, D])
        xn = sb("xn2", [P, D])
        hb = sb("hb", [P, 2, KT, P])
        rows = sb("rows2", [2, ROWS])
        junk = sb("junk2", [P, D])
        ident = sb("ident2", [P, P])
        st = sb("st2", [P, 6, 2])
        eps = sb("eps2", [P, 1])
        Y = ctx.enter_context(nc.psum_tensor("Y", [P, 2, D], F32))
        TP = ctx.enter_context(nc.psum_tensor("TP", [P, 2, D], F32))

        par, wr_ld = sem("out0_par"), [sem("wo_loaded0"), sem("wo_loaded1")]
        woh, wol = sem("wo_hi_done"), [sem("wo_lo_pool"), sem("wo_lo_dve")]
        m_ld, mh, ml = [sem("m_loaded0"), sem("m_loaded1")], [sem("m_hi0"), sem("m_hi1")], [sem("m_lo0"), sem("m_lo1")]
        x_ld = [sem("x2_loaded0"), sem("x2_loaded1")]
        half = [sem("y_half0"), sem("y_half1")]
        y1, y2, y3, yn, xd = sem("y_sum"), sem("y_root"), sem("y_rstd"), sem("y_scaled"), sem("x1_ready")
        z1, z2, z3, xnd = sem("x1_sum"), sem("x1_root"), sem("x1_rstd"), sem("xn2_ready")
        tr, hg, hd = sem("xn_transposed"), sem("h_gained"), sem("h_ready")
        xst, hst = [sem("x1_stored0"), sem("x1_stored1")], [sem("h_stored0"), sem("h_stored1")]
        gst = sem("gp1_stored")
        r1, r2, mt, gsd, es = sem("mod1_rows"), sem("mod1_gain"), sem("mod1_transposed"), sem("gs1_done"), sem("eps2_set")
        blk = ctx.enter_context(nc.Block())

        def mrow(q):
            return x1[0:2, q, :] if q < 2 else xn[0:2, :]

        def loops(eng, body):
            body(0, 0, True, False)
            body(1, 1, False, False)
            with eng.Fori(1, LT // 2) as j:
                body(2 * j, 0, False, False)
                body(2 * j + 1, 1, False, False)
            body(LT, 0, False, False)
            body(LT + 1, 1, False, True)

        def is_ctx(t):
            return isinstance(t, int) and t >= LT

        @blk.sync
        def _(sp):
            def at(t):
                return t * P if isinstance(t, int) else sp.snap(t * P)

            def load_mix(t, h, first):
                n = at(t)
                if not first:
                    sp.wait_ge(ml[h], t)
                sp.dma_start(mraw[:, h], a["mixT"][h * KT:(h + 1) * KT, :, bass.ds(n, P)].rearrange("k p n -> p k n"))\
                    .then_inc(m_ld[h], 16)

            def load_x(t, s, first):
                n = at(t)
                if not first:
                    sp.wait_ge(xd, t - 1)
                sp.dma_start(xt[:, s, :], a["x"][bass.ds(n, P), :]).then_inc(x_ld[s], 16)

            def store(t, s):
                n = at(t)
                if not is_ctx(t):
                    sp.wait_ge(xd, t + 1)
                    sp.dma_start(a["x1"][bass.ds(n, P), :], x1[:, s, :]).then_inc(xst[s], 16)
                sp.wait_ge(hd, t + 1)
                sp.dma_start(a["hT1"][t], hb[:, s]).then_inc(hst[s], 16)

            def load_w(k):
                if k >= 2:
                    sp.wait_ge(wol[k % 2], k // 2)
                sp.dma_start(wr[:, k % 2, :], a["w_out0"][k * P:(k + 1) * P, :]).then_inc(wr_ld[k % 2], 16)

            load_w(0)
            load_mix(0, 0, True)
            load_w(1)
            load_mix(0, 1, True)
            load_x(0, 0, True)
            sp.dma_start(gpb[:], a["gp"][0].partition_broadcast(P)).then_inc(par, 16)
            sp.dma_start(rows[:], a["rows1"]).then_inc(par, 16)
            sp.dma_start(ident[:], a["ident"]).then_inc(par, 16)
            for q in range(3):
                sp.dma_start(mrow(q), a["mod1"].rearrange("w a b -> w (a b)")[:, q * D:(q + 1) * D]).then_inc(par, 16)
            for k in range(2, K2):
                load_w(k)
            load_x(1, 1, True)
            sp.wait_ge(r2, 2)
            sp.dma_start(a["gp"][1], mrow(2)).then_inc(gst, 16)

            def body(t, s, first, last):
                if not last:
                    load_mix(t + 1, 0, False)
                    load_mix(t + 1, 1, False)
                    if not first:
                        load_x(t + 1, 1 - s, False)
                if not first:
                    store(t - 1, 1 - s)

            loops(sp, body)
            store(TT - 1, 1)
            for s in range(2):
                sp.wait_ge(xst[s], 8 * LT)
                sp.wait_ge(hst[s], 8 * TT)
            sp.wait_ge(gst, 16)

        @blk.scalar
        def _(act):
            def split(t, h, first):
                act.wait_ge(m_ld[h], 16 * t + 16)
                if not first:
                    act.wait_ge(half[h], t)
                nc.scalar.activation(m_hi[:, h], mraw[:, h], ACT.Copy).then_inc(mh[h], 1)

            def epilogue(t, s, second):
                act.wait_ge(half[1], t + 1)
                nc.scalar.activation(junk[:], Y[:, s, :], ACT.Square, accum_out=st[:, 0, s:s + 1]).then_inc(y1, 1)
                act.wait_ge(y1, t + 1)
                nc.scalar.activation(st[:, 1, s:s + 1], st[:, 0, s:s + 1], ACT.Sqrt, bias=eps[:, 0:1],
                                     scale=1.0 / D).then_inc(y2, 1)
                act.wait_ge(xd, t + 1)
                nc.scalar.activation(junk[:], x1[:, s, :], ACT.Square, accum_out=st[:, 3, s:s + 1]).then_inc(z1, 1)
                act.wait_ge(z1, t + 1)
                nc.scalar.activation(st[:, 4, s:s + 1], st[:, 3, s:s + 1], ACT.Sqrt, bias=eps[:, 0:1],
                                     scale=1.0 / D).then_inc(z2, 1)

            split(0, 0, True)
            split(0, 1, True)
            act.wait_ge(es, 1)
            for k in range(K2):
                act.wait_ge(wr_ld[k % 2], 16 * (k // 2 + 1))
                nc.scalar.activation(wo_hi[:, k, :], wr[:, k % 2, :], ACT.Copy).then_inc(woh, 1)

            def body(t, s, first, last):
                if not first:
                    epilogue(t - 1, 1 - s, True)
                if not last:
                    split(t + 1, 0, False)
                    split(t + 1, 1, False)

            loops(act, body)
            epilogue(TT - 1, 1, True)

        @blk.vector
        def _(dve):
            nc.vector.memset(eps[:], EPS).then_inc(es, 1)
            dve.wait_ge(par, 96)
            tt, stt = nc.vector.tensor_tensor, nc.vector.scalar_tensor_tensor
            for q in range(3):
                tt(mrow(q), mrow(q), rows[:, q * D:(q + 1) * D], ALU.add).then_inc(r1, 1)
            dve.wait_ge(r1, 3)
            stt(out=mrow(1), in0=mrow(1), scalar=1.0, in1=rows[:, 3 * D:4 * D], op0=ALU.add, op1=ALU.mult).then_inc(r2, 1)
            tt(mrow(2), mrow(2), rows[:, 4 * D:5 * D], ALU.mult).then_inc(r2, 1)
            dve.wait_ge(mt, 1)
            nc.vector.tensor_copy(gs1[:].rearrange("p a k w -> p (a k w)"), TP[:, 0, 0:4 * KT]).then_inc(gsd, 1)
            for k in range(1, K2, 2):
                dve.wait_ge(woh, k + 1)
                tt(wo_lo[:, k, :], wr[:, 1, :], v32(wo_hi[:, k, :]), ALU.subtract).then_inc(wol[1], 1)

            def epilogue(t, s):
                w = 1 if is_ctx(t) else 0
                dve.wait_ge(y2, t + 1)
                nc.vector.reciprocal(st[:, 2, s:s + 1], st[:, 1, s:s + 1]).then_inc(y3, 1)
                dve.wait_ge(y3, t + 1)
                if isinstance(t, int) and t < 2:
                    dve.wait_ge(gst, 16)
                else:
                    dve.wait_ge(xst[s], 8 * (t - s))
                stt(out=x1[:, s, :], in0=Y[:, s, :], scalar=st[:, 2, s:s + 1], in1=gpb[:, w, :], op0=ALU.mult,
                    op1=ALU.mult).then_inc(yn, 1)
                dve.wait_ge(z2, t + 1)
                nc.vector.reciprocal(st[:, 5, s:s + 1], st[:, 4, s:s + 1]).then_inc(z3, 1)
                dve.wait_ge(z3, t + 1)
                if not (isinstance(t, int) and t == 0):
                    dve.wait_ge(tr, t)
                nc.vector.tensor_scalar(xn[:], x1[:, s, :], st[:, 5, s:s + 1], None, ALU.mult).then_inc(xnd, 1)
                dve.wait_ge(tr, t + 1)
                if not (isinstance(t, int) and t < 2):
                    dve.wait_ge(hst[s], 8 * (t - s))
                tt(hb[:, s], TP[:, s, :].rearrange("p (k n) -> p k n", n=P),
                   gs1[:, 1, :, w:w + 1].to_broadcast([P, KT, P]), ALU.mult).then_inc(hg, 1)

            def body(t, s, first, last):
                if not first:
                    epilogue(t - 1, 1 - s)

            loops(dve, body)
            epilogue(TT - 1, 1)

        @blk.gpsimd
        def _(pool):
            tt = nc.gpsimd.tensor_tensor

            def split(t, h):
                pool.wait_ge(mh[h], t + 1)
                tt(m_lo[:, h], mraw[:, h], v32(m_hi[:, h]), ALU.subtract).then_inc(ml[h], 1)

            split(0, 0)
            split(0, 1)
            for k in range(0, K2, 2):
                pool.wait_ge(woh, k + 1)
                tt(wo_lo[:, k, :], wr[:, 0, :], v32(wo_hi[:, k, :]), ALU.subtract).then_inc(wol[0], 1)

            def epilogue(t, s):
                w = 1 if is_ctx(t) else 0
                pool.wait_ge(x_ld[s], 8 * (t - s) + 16)
                pool.wait_ge(yn, t + 1)
                tt(x1[:, s, :], x1[:, s, :], xt[:, s, :], ALU.add).then_inc(xd, 1)
                pool.wait_ge(gsd, 1)
                pool.wait_ge(hg, t + 1)
                tt(hb[:, s], hb[:, s], gs1[:, 0, :, w:w + 1].to_broadcast([P, KT, P]), ALU.add).then_inc(hd, 1)

            def body(t, s, first, last):
                if not first:
                    epilogue(t - 1, 1 - s)
                if not last:
                    split(t + 1, 0)
                    split(t + 1, 1)

            loops(pool, body)
            epilogue(TT - 1, 1)

        @blk.tensor
        def _(pe):
            pe.wait_ge(par, 96)
            pe.wait_ge(r2, 2)
            for q in range(2 * KT):
                last = nc.tensor.transpose(TP[:, 0, 2 * q:2 * q + 2], mrow(q // KT)[:, (q % KT) * P:(q % KT + 1) * P],
                                           ident[0:2, 0:2])
            last.then_inc(mt, 1)

            def product(t, s, first):
                for h in range(2):
                    pe.wait_ge(ml[h], t + 1)
                    if h == 0 and not (isinstance(t, int) and t < 2):
                        pe.wait_ge(yn, t - 1)
                    for k in range(KT):
                        if first:
                            g = h * KT + k
                            pe.wait_ge(wol[g % 2], g // 2 + 1)
                        for n in (0, 512):
                            out = Y[:, s, n:n + 512]
                            w_hi, w_lo = wo_hi[:, h * KT + k, n:n + 512], wo_lo[:, h * KT + k, n:n + 512]
                            nc.tensor.matmul(out, m_hi[:, h, k, :], w_hi, start=(h == 0 and k == 0), stop=False)
                            nc.tensor.matmul(out, m_hi[:, h, k, :], w_lo, start=False, stop=False)
                            last = nc.tensor.matmul(out, m_lo[:, h, k, :], w_hi, start=False,
                                                    stop=(h == 1 and k == KT - 1))
                    last.then_inc(half[h], 1)

            def transposes(t, s):
                pe.wait_ge(xnd, t + 1)
                if isinstance(t, int) and t < 2:
                    pe.wait_ge(gsd, 1)
                else:
                    pe.wait_ge(hg, t - 1)
                for k in range(KT):
                    last = nc.tensor.transpose(TP[:, s, k * P:(k + 1) * P], xn[:, k * P:(k + 1) * P], ident[:])
                last.then_inc(tr, 1)

            def body(t, s, first, last):
                product(t, s, first)
                if not first:
                    transposes(t - 1, 1 - s)

            loops(pe, body)
            transposes(TT - 1, 1)

def projections1(nc, a, kd_hi, kd_lo, vs):
    ctx = ExitStack()
    with ctx:
        def sb(name, shape, dt=F32):
            return ctx.enter_context(nc.sbuf_tensor(name, shape, dt))

        sem = a["sem"]

        h_hi, h_lo = sb("h1_hi", [P, KT, T], F32R), sb("h1_lo", [P, KT, T], F32R)
        hraw = sb("h1_raw", [P, 2, KT, P])
        wraw = sb("w1_raw", [P, 2, D])
        w_hi, w_lo = sb("w1_hi", [P, 2, KT, P], F32R), sb("w1_lo", [P, 2, KT, P], F32R)
        cos, sin = sb("rope_cos", [P, N_LAT]), sb("rope_sin", [P, N_LAT])
        R = sb("rope_in", [P, T])
        Z = sb("rope_swap", [P, N_LAT])
        C = sb("rope_cosined", [P, N_LAT])
        H, L = sb("rot_hi", [P, T], F32R), sb("rot_lo", [P, T], F32R)
        G = sb("gate1", [P, N_LAT])
        ident = sb("ident3", [P, P])
        slab = ctx.enter_context(nc.psum_tensor("slab1", [P, 6, 512], F32))
        VP = ctx.enter_context(nc.psum_tensor("VP", [P, 2, 512], F32))

        par = sem("proj1_par")
        h_ld, hh, hl = [sem("h1_loaded0"), sem("h1_loaded1")], sem("h1_hi_done"), [sem("h1_lo0"), sem("h1_lo1")]
        w_ld, wh, wl = [sem("w1_loaded0"), sem("w1_loaded1")], [sem("w1_hi0"), sem("w1_hi1")], [sem("w1_lo0"), sem("w1_lo1")]
        kv, kvr = sem("kv_chunk"), sem("kv_chunk_read")
        sw, rc, rs, ro = sem("swapped"), sem("times_cos"), sem("times_sin"), sem("rotated")
        rh, rl = sem("rotated_hi"), sem("rotated_lo")
        kst = sem("k_spread")
        vtr, vh, vl = sem("v_transposed"), sem("v_hi_done"), sem("v_lo_done")
        qd, qr, qst = sem("q_chunk"), sem("q_chunk_read"), sem("q_stored")
        gd, gt, gg, gst = sem("g_chunk"), sem("g_tanh"), sem("g_silu"), sem("g_stored")
        blk = ctx.enter_context(nc.Block())
        V_GROUPS = [(0, 4), (4, 4), (8, 2)]

        def v_psum(s, g, n):
            return VP[:, (3 * s + g) % 2, 0:n * P].rearrange("p (t c d) -> p t c d", c=2, d=HEAD)

        def v_part(s, t0, n, part):
            return vs[:, t0:t0 + n, 2 * s:2 * s + 2, HEAD * part:HEAD * (part + 1)]

        def loops(eng, body, n=KT):
            body(0, True, False)
            with eng.Fori(1, n - 1) as t:
                body(t, False, False)
            body(n - 1, False, True)

        @blk.sync
        def _(sp):
            def load_slab(at, j, use):
                if not (isinstance(use, int) and use == 0):
                    sp.wait_ge(wl[j], use)
                sp.dma_start(wraw[:, j, :], a["w_in1"][at]).then_inc(w_ld[j], 16)

            load_slab(0, 0, 0)
            for i in range(TT):
                if i >= 2:
                    sp.wait_ge(hl[i % 2], i // 2)
                sp.dma_start(hraw[:, i % 2], a["hT1"][i]).then_inc(h_ld[i % 2], 16)
                if i == 3:
                    load_slab(1, 1, 0)
            sp.dma_start(cos[:], a["rope"][0]).then_inc(par, 16)
            sp.dma_start(sin[:], a["rope"][1]).then_inc(par, 16)
            sp.dma_start(ident[:], a["ident"]).then_inc(par, 16)
            load_slab(2, 0, 1)
            load_slab(3, 1, 1)
            for s in range(2):
                for ready, part, dst in ((rh, H, kd_hi), (rl, L, kd_lo)):
                    sp.wait_ge(ready, s + 1)
                    for c in range(2):
                        for v in range(2):
                            sp.dma_start(v32(dst[HEAD * v:HEAD * (v + 1), 2 * s + c, :]),
                                         v32(part[HEAD * c:HEAD * (c + 1), :])).then_inc(kst, 16)

            def store(t):
                for v, (ready, part) in enumerate(((rh, H), (rl, L))):
                    sp.wait_ge(ready, t + 3)
                    sp.dma_start(a["qT"][:, v, :, t, :].rearrange("b p n -> p b n"),
                                 v32(part[:, 0:N_LAT]).rearrange("p (b n) -> p b n", n=P)).then_inc(qst, 16)
                sp.wait_ge(gg, 2 * t + 2)
                sp.dma_start(a["sgT"][:, :, t, :].rearrange("b p n -> p b n"),
                             G[:].rearrange("p (b n) -> p b n", n=P)).then_inc(gst, 16)

            def body(t, first, last):
                load_slab(2 * t + 4, 0, t + 2)
                load_slab(2 * t + 5, 1, t + 2)
                if not first:
                    store(t - 1)

            loops(sp, body)
            store(KT - 1)
            sp.wait_ge(kst, 256)
            sp.wait_ge(qst, 32 * KT)
            sp.wait_ge(gst, 16 * KT)

        @blk.scalar
        def _(act):
            def split(j, use):
                act.wait_ge(w_ld[j], 16 * use + 16)
                nc.scalar.activation(w_hi[:, j].rearrange("p k n -> p (k n)"), wraw[:, j, :], ACT.Copy).then_inc(wh[j], 1)

            split(0, 0)
            for i in range(TT):
                act.wait_ge(h_ld[i % 2], 16 * (i // 2 + 1))
                nc.scalar.activation(h_hi[:, :, i * P:(i + 1) * P], hraw[:, i % 2], ACT.Copy).then_inc(hh, 1)
                if i == 3:
                    split(1, 0)
            for s in range(4):
                if s in (1, 2):
                    act.wait_ge(rl, s)
                elif s == 3:
                    act.wait_ge(vtr, 3)
                for c, (at, n) in enumerate(CHUNKS):
                    act.wait_ge(kv, 3 * s + c + 1)
                    nc.scalar.activation(R[:, at:at + n], slab[:, 3 * (s % 2) + c, 0:n], ACT.Copy).then_inc(kvr, 1)
                split(s % 2, s // 2 + 1)
                if s < 2:
                    act.wait_ge(ro, s + 1)
                    if s == 1:
                        act.wait_ge(kst, 128)
                    nc.scalar.activation(H[:], R[:], ACT.Copy).then_inc(rh, 1)
                else:
                    for g, (t0, n) in enumerate(V_GROUPS):
                        act.wait_ge(vtr, 3 * (s - 2) + g + 1)
                        nc.scalar.activation(v_part(s - 2, t0, n, 0), v_psum(s - 2, g, n), ACT.Copy).then_inc(vh, 1)

            def body(t, first, last):
                if first:
                    act.wait_ge(vtr, 6)
                else:
                    act.wait_ge(rl, t + 2)
                for c in range(2):
                    act.wait_ge(qd, 2 * t + c + 1)
                    nc.scalar.activation(R[:, 512 * c:512 * c + 512], slab[:, c, :], ACT.Copy).then_inc(qr, 1)
                if not last:
                    split(0, t + 3)
                if not first:
                    act.wait_ge(gst, 16 * t)
                for c in range(2):
                    act.wait_ge(gd, 2 * t + c + 1)
                    nc.scalar.activation(G[:, 512 * c:512 * c + 512], slab[:, 3 + c, :], ACT.Tanh, scale=0.5)\
                        .then_inc(gt, 1)
                if not last:
                    split(1, t + 3)
                act.wait_ge(ro, t + 3)
                if first:
                    act.wait_ge(kst, 256)
                else:
                    act.wait_ge(qst, 32 * t)
                nc.scalar.activation(H[:, 0:N_LAT], R[:, 0:N_LAT], ACT.Copy).then_inc(rh, 1)

            loops(act, body)

        @blk.vector
        def _(dve):
            tt = nc.vector.tensor_tensor
            for i in range(1, TT, 2):
                dve.wait_ge(hh, i + 1)
                tt(h_lo[:, :, i * P:(i + 1) * P], hraw[:, 1], v32(h_hi[:, :, i * P:(i + 1) * P]), ALU.subtract)\
                    .then_inc(hl[1], 1)
            dve.wait_ge(par, 48)

            def rotate(ready, value, n):
                dve.wait_ge(ready, value)
                if not (isinstance(n, int) and n == 0):
                    dve.wait_ge(ro, n)
                tt(C[:], R[:, 0:N_LAT], cos[:], ALU.mult).then_inc(rc, 1)
                nc.vector.stream_shuffle(Z[:], R[:, 0:N_LAT], [(i + 16) % 32 for i in range(32)]).then_inc(sw, 1)
                dve.wait_ge(rc, n + 1)
                dve.wait_ge(sw, n + 1)
                dve.wait_ge(rs, n + 1)
                tt(R[:, 0:N_LAT], C[:], Z[:], ALU.add).then_inc(ro, 1)

            rotate(kvr, 3, 0)
            rotate(kvr, 6, 1)
            for s in range(2):
                for g, (t0, n) in enumerate(V_GROUPS):
                    dve.wait_ge(vh, 3 * s + g + 1)
                    tt(v_part(s, t0, n, 1), v_psum(s, g, n), v32(v_part(s, t0, n, 0)), ALU.subtract).then_inc(vl, 1)

            def body(t, first, last):
                rotate(qr, 2 * t + 2, t + 2)
                for c in range(2):
                    dve.wait_ge(gt, 2 * t + c + 1)
                    nc.vector.scalar_tensor_tensor(out=G[:, 512 * c:512 * c + 512], in0=G[:, 512 * c:512 * c + 512],
                                                   scalar=1.0, in1=slab[:, 3 + c, :], op0=ALU.add,
                                                   op1=ALU.mult).then_inc(gg, 1)

            loops(dve, body)

        @blk.gpsimd
        def _(pool):
            tt = nc.gpsimd.tensor_tensor

            def split(j, use):
                pool.wait_ge(wh[j], use + 1)
                tt(w_lo[:, j].rearrange("p k n -> p (k n)"), wraw[:, j, :],
                   v32(w_hi[:, j].rearrange("p k n -> p (k n)")), ALU.subtract).then_inc(wl[j], 1)

            def sines(n):
                pool.wait_ge(sw, n + 1)
                tt(Z[:], Z[:], sin[:], ALU.mult).then_inc(rs, 1)

            split(0, 0)
            for i in range(0, TT, 2):
                pool.wait_ge(hh, i + 1)
                tt(h_lo[:, :, i * P:(i + 1) * P], hraw[:, 0], v32(h_hi[:, :, i * P:(i + 1) * P]), ALU.subtract)\
                    .then_inc(hl[0], 1)
                if i == 4:
                    split(1, 0)
            pool.wait_ge(par, 48)
            for s in range(2):
                split(s, 1)
                sines(s)
                pool.wait_ge(rh, s + 1)
                tt(L[:], R[:], v32(H[:]), ALU.subtract).then_inc(rl, 1)
            split(0, 2)
            split(1, 2)

            def body(t, first, last):
                if not last:
                    split(0, t + 3)
                sines(t + 2)
                if not last:
                    split(1, t + 3)
                pool.wait_ge(rh, t + 3)
                tt(L[:, 0:N_LAT], R[:, 0:N_LAT], v32(H[:, 0:N_LAT]), ALU.subtract).then_inc(rl, 1)

            loops(pool, body)

        @blk.tensor
        def _(pe):
            def product(j, use, c, at, n):
                out = slab[:, 3 * j + c, 0:n]
                for k in range(KT):
                    rhs_hi, rhs_lo = h_hi[:, k, at:at + n], h_lo[:, k, at:at + n]
                    nc.tensor.matmul(out, w_hi[:, j, k, :], rhs_hi, start=(k == 0), stop=False)
                    nc.tensor.matmul(out, w_hi[:, j, k, :], rhs_lo, start=False, stop=False)
                    last = nc.tensor.matmul(out, w_lo[:, j, k, :], rhs_hi, start=False, stop=(k == KT - 1))
                return last

            def transposes(s):
                pe.wait_ge(kvr, 3 * (s + 2) + 3)
                for g, (t0, n) in enumerate(V_GROUPS):
                    if 3 * s + g >= 2:
                        pe.wait_ge(vl, 3 * s + g - 1)
                    for i in range(n):
                        last = nc.tensor.transpose(VP[:, (3 * s + g) % 2, i * P:(i + 1) * P], R[:, (t0 + i) * P:(t0 + i + 1) * P],
                                                   ident[:])
                    last.then_inc(vtr, 1)

            for s in range(4):
                pe.wait_ge(wl[s % 2], s // 2 + 1)
                for c, (at, n) in enumerate(CHUNKS):
                    if s == 0:
                        tiles = (at + n) // P
                        pe.wait_ge(hl[0], (tiles + 1) // 2)
                        pe.wait_ge(hl[1], tiles // 2)
                    if s >= 2:
                        pe.wait_ge(kvr, 3 * (s - 2) + c + 1)
                    product(s % 2, s // 2, c, at, n).then_inc(kv, 1)
                if s == 3:
                    pe.wait_ge(par, 48)
                    transposes(0)

            def body(t, first, last):
                pe.wait_ge(wl[0], t + 3)
                for c in range(2):
                    if first:
                        pe.wait_ge(kvr, 9)
                    else:
                        pe.wait_ge(qr, 2 * (t - 1) + c + 1)
                    product(0, t + 2, c, 512 * c, 512).then_inc(qd, 1)
                if first:
                    transposes(1)
                pe.wait_ge(wl[1], t + 3)
                for c in range(2):
                    if not first:
                        pe.wait_ge(gg, 2 * (t - 1) + c + 1)
                    product(1, t + 2, c, 512 * c, 512).then_inc(gd, 1)

            loops(pe, body)


N_HD = 4
WIN = 5
AHEAD = 10
UNIT_AHEAD = 11


def attention(nc, a, kd_hi, kd_lo, vs):
    ctx = ExitStack()
    with ctx:
        def sb(name, shape, dt=F32):
            return ctx.enter_context(nc.sbuf_tensor(name, shape, dt))

        sem = a["sem"]
        NB = LT
        vw = sb("v_window", [P, 2, 3, N_KV, P], F32R)
        q = sb("q_parts", [P, 2, N_HEADS, P], F32R)
        pr = sb("probs", [P, 4, N_HD, WIN * P])
        pt_hi, pt_lo = sb("pt_hi", [P, WIN, 512], F32R), sb("pt_lo", [P, WIN, 512], F32R)
        ost = sb("o_out", [P, 2, N_KV, N_HD * P])
        mask = sb("mask", [P, (2 * WIN - 1) * P])
        sink, nsink = sb("sink", [P, N_HEADS]), sb("nsink", [P, N_HEADS])
        nm, es, rsum, den, rden = (sb(n, [P, 4, N_HD]) for n in ("neg_max", "sink_term", "row_sum", "denom", "rdenom"))
        ident = sb("ident4", [P, P])
        S = ctx.enter_context(nc.psum_tensor("S", [P, 2, 1024], F32))
        TB = ctx.enter_context(nc.psum_tensor("TB", [P, 2, 512], F32))
        O = ctx.enter_context(nc.psum_tensor("O", [P, 2, 512], F32))

        par, nsk = sem("att_par"), sem("neg_sink")
        v_ld = [sem("v_window0"), sem("v_window1")]
        q_ld = [sem("q_loaded0"), sem("q_loaded1")]
        sd, td, ed = sem("scores"), sem("scaled_max"), sem("exp_done")
        sa, se, dn, rc, pn = sem("sink_minus_max"), sem("sink_exp"), sem("denom_done"), sem("rdenom_done"), sem("normalised")
        tr, ph, pl, pv = sem("p_transposed"), sem("pt_hi_done"), sem("pt_lo_done"), sem("value_product")
        oe, ost_s = sem("o_copied"), [sem("o_stored0"), sem("o_stored1")]
        blk = ctx.enter_context(nc.Block())

        def loops(eng, body):
            body(0, 0)
            with eng.Fori(0, NB // 2 - 2) as j:
                body(2 * j + 1, 1)
                body(2 * j + 2, 0)
            body(NB - 3, 1)
            body(NB - 2, 0)
            body(NB - 1, 1)

        def is_block(b, n):
            return isinstance(b, int) and b == n

        def tiles(b):
            return WIN - 1 if is_block(b, 0) or is_block(b, NB - 1) else WIN

        def tiles_before(b):
            return 0 if is_block(b, 0) else 20 * b - 4

        def n_par(b, u, x):
            return (tiles(b) * u + x) % 2

        def head_steps(b):
            return range(tiles(b) - N_HD, tiles(b))

        def take(head, b, j):
            if j < N_HEADS:
                head(b, j)
            elif not is_block(b, NB - 1):
                head(b + 1, j - N_HEADS)

        def row(b, buf):
            return buf[..., 0:tiles(b) * P]

        @blk.sync
        def _(sp):
            def load_q(b, s):
                for v in range(2):
                    for c in range(2):
                        sp.dma_start(v32(q[HEAD * v:HEAD * (v + 1), s]).rearrange("d (p c h) n -> d c p h n", p=2, c=2)[:, c],
                                     a["qT"][b, v, HEAD * c:HEAD * (c + 1)].rearrange("d (p h) n -> d p h n", p=2))\
                            .then_inc(q_ld[s], 16)

            def load_v(b, s):
                sp.dma_start(v32(vw[:, s]), v32(vs[:, bass.ds(b - 1, 3)])).then_inc(v_ld[s], 16)

            load_q(0, 0)
            sp.dma_start(sink[:], a["sink"]).then_inc(par, 16)
            sp.dma_start(mask[:], a["mask"]).then_inc(par, 16)
            sp.dma_start(ident[:], a["ident"]).then_inc(par, 16)
            load_q(1, 1)
            load_v(1, 1)

            def body(b, s):
                if not isinstance(b, int) or b < NB - 2:
                    sp.wait_ge(sd, 16 * b + 16)
                    load_q(b + 2, s)
                if not isinstance(b, int) or b < NB - 3:
                    sp.wait_ge(pv, tiles_before(b + 1))
                    load_v(b + 2, s)
                sp.wait_ge(oe, 4 * b + 4)
                sp.dma_start(a["oT"][b], ost[:, s]).then_inc(ost_s[s], 16)

            loops(sp, body)
            for s in range(2):
                sp.wait_ge(ost_s[s], 8 * NB)

        @blk.scalar
        def _(act):
            def head(b, j):
                u, h = j // 4, j % 4
                act.wait_ge(td, 16 * b + j + 1)
                r = row(b, pr[:, u, h, :])
                nc.scalar.activation(r, r, ACT.Exp, bias=nm[:, u, h:h + 1], scale=-1.0,
                                     accum_out=rsum[:, u, h:h + 1]).then_inc(ed, 1)
                if h == N_HD - 1:
                    act.wait_ge(sa, 4 * b + u + 1)
                    nc.scalar.activation(es[:, u, :], es[:, u, :], ACT.Exp).then_inc(se, 1)

            def copy_o(b, s, u):
                act.wait_ge(pv, tiles_before(b) + tiles(b) * (u + 1))
                if u == 0 and not (isinstance(b, int) and b < 2):
                    act.wait_ge(ost_s[s], 8 * (b - s))
                nc.scalar.activation(ost[:, s, u, :], O[:, u % 2, :], ACT.Copy).then_inc(oe, 1)

            for j in range(AHEAD - 1):
                head(0, j)

            def body(b, s):
                for u in range(4):
                    for x in range(tiles(b)):
                        n = tiles_before(b) + tiles(b) * u + x
                        act.wait_ge(tr, n + 1)
                        if u:
                            act.wait_ge(pv, n + 1 - tiles(b))
                        elif not is_block(b, 0):
                            before = 4 if is_block(b, 1) else 5
                            act.wait_ge(pv, tiles_before(b) - before + min(x + 1, before))
                        nc.scalar.activation(pt_hi[:, x, :], TB[:, n_par(b, u, x), :], ACT.Copy).then_inc(ph, 1)
                        if x in head_steps(b):
                            take(head, b, 4 * u + head_steps(b).index(x) + AHEAD - 1)
                        if x == 1:
                            if u:
                                copy_o(b, s, u - 1)
                            elif not is_block(b, 0):
                                copy_o(b - 1, 1 - s, 3)

            loops(act, body)
            copy_o(NB - 1, 1, 3)

        @blk.vector
        def _(dve):
            tt = nc.vector.tensor_tensor
            dve.wait_ge(par, 48)
            nc.vector.tensor_scalar(nsink[:], sink[:], -1.0, None, ALU.mult).then_inc(nsk, 1)
            dve.wait_ge(nsk, 1)

            def head_waits(b, j):
                dve.wait_ge(sd, 16 * b + j + 1)
                if not is_block(b, 0):
                    dve.wait_ge(tr, tiles_before(b - 1) + tiles(b - 1) * (j // 4 + 1))

            def head(b, j):
                u, h = j // 4, j % 4
                at = P if tiles(b) == WIN else 2 * P
                m = mask[:, WIN * P:] if is_block(b, NB - 1) else mask[:, P:WIN * P] if is_block(b, 0) else mask[:, 0:WIN * P]
                nc.vector.tensor_tensor_reduce(
                    out=row(b, pr[:, u, h, :]), in0=S[:, j % 2, at:768], in1=m, scale=-SCALE, scalar=nsink[:, j:j + 1],
                    op0=ALU.add, op1=ALU.min, accum_out=nm[:, u, h:h + 1]).then_inc(td, 1)

            def reciprocals(b, j):
                u = j // 4
                dve.wait_ge(dn, 4 * b + u + 1)
                nc.vector.reciprocal(rden[:, u, :], den[:, u, :]).then_inc(rc, 1)

            for j in range(AHEAD):
                head_waits(0, j)
                head(0, j)
                if j in (5, 9):
                    reciprocals(0, j - 2)

            def body(b, s):
                for u in range(4):
                    for x in range(tiles(b)):
                        n = tiles_before(b) + tiles(b) * u + x
                        k = x - head_steps(b)[0]
                        if k >= 0:
                            take(head_waits, b, 4 * u + k + AHEAD)
                        dve.wait_ge(ph, n + 1)
                        tt(pt_lo[:, x, :], TB[:, n_par(b, u, x), :], v32(pt_hi[:, x, :]), ALU.subtract).then_inc(pl, 1)
                        if k >= 0:
                            take(head, b, 4 * u + k + AHEAD)
                        if k == 3:
                            take(reciprocals, b, 4 * u + UNIT_AHEAD)

            loops(dve, body)

        @blk.gpsimd
        def _(pool):
            def sinks(b, j):
                u = j // 4
                pool.wait_ge(td, 16 * b + j + 1)
                nc.gpsimd.tensor_tensor(es[:, u, :], nm[:, u, :], sink[:, 4 * u:4 * u + 4], ALU.add).then_inc(sa, 1)

            def unit(b, j):
                u = j // 4
                pool.wait_ge(se, 4 * b + u + 1)
                nc.gpsimd.tensor_tensor(den[:, u, :], es[:, u, :], rsum[:, u, :], ALU.add).then_inc(dn, 1)
                pool.wait_ge(rc, 4 * b + u + 1)
                rows = row(b, pr[:, u])
                nc.gpsimd.tensor_tensor(rows, rows, rden[:, u, :].unsqueeze(2).to_broadcast(rows.shape),
                                        ALU.mult).then_inc(pn, 1)

            pool.wait_ge(par, 48)
            for j in (3, 7):
                sinks(0, j)
                unit(0, j)

            def body(b, s):
                for u in range(4):
                    take(sinks, b, 4 * u + UNIT_AHEAD)
                    take(unit, b, 4 * u + UNIT_AHEAD)

            loops(pool, body)

        @blk.tensor
        def _(pe):
            def scores(b, j, s):
                u = j // 4
                if j == 0:
                    pe.wait_ge(q_ld[s], 32 * (b - s) + 64)
                if not (is_block(b, 0) and j < 2):
                    pe.wait_ge(td, 16 * b + j - 1)
                n = (tiles(b) - 2) * P
                at = 0 if is_block(b, 0) else (b - 1) * P
                for out, start, size in ((S[:, j % 2, 512 - n:512], at, n), (S[:, j % 2, 512:768], N_LAT, N_CTX)):
                    nc.tensor.matmul(out, q[:, s, j, :], kd_hi[:, u, bass.ds(start, size)], start=True, stop=False)
                    last = nc.tensor.matmul(out, q[:, s, j, :], kd_lo[:, u, bass.ds(start, size)], start=False, stop=True)
                last.then_inc(sd, 1)

            def values(b, s, u, x):
                n = tiles_before(b) + tiles(b) * u + x
                pe.wait_ge(pl, n + 1)
                if x == 0 and not (is_block(b, 0) and u < 2):
                    pe.wait_ge(oe, 4 * b + u - 1)
                if tiles(b) == WIN and x == 0 and u == 0:
                    pe.wait_ge(v_ld[s], 8 * b + 8 * s)
                left = tiles(b) - 2
                if x >= left:
                    v = vs[:, LT + x - left, u, :]
                elif tiles(b) == WIN:
                    v = vw[:, s, x, u, :]
                else:
                    v = vs[:, x if b == 0 else NB - 2 + x, u, :]
                out = O[:, u % 2, :]
                nc.tensor.matmul(out, v, pt_hi[:, x, :], start=(x == 0), stop=False)
                nc.tensor.matmul(out, v, pt_lo[:, x, :], start=False, stop=(x == tiles(b) - 1)).then_inc(pv, 1)

            pe.wait_ge(par, 48)
            for j in range(AHEAD):
                scores(0, j, 0)

            def body(b, s):
                for u in range(4):
                    for x in range(tiles(b)):
                        n = tiles_before(b) + tiles(b) * u + x
                        if x == 0:
                            pe.wait_ge(pn, 4 * b + u + 1)
                        if not (is_block(b, 0) and u == 0 and x < 2):
                            pe.wait_ge(pl, n - 1)
                        for h in range(N_HD):
                            last = nc.tensor.transpose(TB[:, n_par(b, u, x), h * P:(h + 1) * P],
                                                       pr[:, u, h, x * P:(x + 1) * P], ident[:])
                        last.then_inc(tr, 1)
                        j = 4 * u + x - head_steps(b)[0] + AHEAD
                        if x in head_steps(b) and j < N_HEADS:
                            scores(b, j, s)
                        elif x in head_steps(b) and not is_block(b, NB - 1):
                            scores(b + 1, j - N_HEADS, 1 - s)
                        if x >= 1:
                            values(b, s, u, x - 1)
                    values(b, s, u, tiles(b) - 1)

            loops(pe, body)


def out_projection1(nc, a):
    ctx = ExitStack()
    with ctx:
        def sb(name, shape, dt=F32):
            return ctx.enter_context(nc.sbuf_tensor(name, shape, dt))

        sem = a["sem"]

        wo_hi, wo_lo = sb("wo1_hi", [P, KT, D], F32R), sb("wo1_lo", [P, KT, D], F32R)
        wr = sb("wr1", [P, 2, D])
        oraw = sb("o_raw", [P, 2, 2, KT, P])
        graw = sb("g_raw", [P, 2, KT, P])
        m_hi, m_lo = sb("m1_hi", [P, 2, KT, P], F32R), sb("m1_lo", [P, 2, KT, P], F32R)
        gpb = sb("gpb1", [P, D])
        xt = sb("xt5", [P, 2, D])
        out = sb("out_tiles", [P, 2, D])
        junk = sb("junk5", [P, D])
        st = sb("st5", [P, 3, 2])
        eps = sb("eps5", [P, 1])
        Y = ctx.enter_context(nc.psum_tensor("Y1", [P, 2, D], F32))

        par, wr_ld = sem("out1_par"), [sem("wo1_loaded0"), sem("wo1_loaded1")]
        woh, wol = sem("wo1_hi_done"), [sem("wo1_lo_pool"), sem("wo1_lo_dve")]
        m_ld = [sem("o_loaded0"), sem("o_loaded1")]
        os_ = sem("o_summed")
        md, mh, ml = sem("mixed1"), sem("m1_hi_done"), sem("m1_lo_done")
        x_ld = [sem("x5_loaded0"), sem("x5_loaded1")]
        yd = sem("y1_product")
        y1, y2, y3, yn, xd = sem("y1_sum"), sem("y1_root"), sem("y1_rstd"), sem("y1_scaled"), sem("out_ready")
        ost, es = [sem("out_stored0"), sem("out_stored1")], sem("eps5_set")
        blk = ctx.enter_context(nc.Block())

        def loops(eng, body):
            body(0, 0, True, False)
            body(1, 1, False, False)
            with eng.Fori(1, LT // 2 - 1) as j:
                body(2 * j, 0, False, False)
                body(2 * j + 1, 1, False, False)
            body(LT - 2, 0, False, False)
            body(LT - 1, 1, False, True)

        def early(t):
            return isinstance(t, int) and t < 2

        @blk.sync
        def _(sp):
            def load(t, s):
                if not early(t):
                    sp.wait_ge(ml, t - 1)
                for part in range(2):
                    for c in range(2):
                        sp.dma_start(oraw[HEAD * c:HEAD * (c + 1), s, part].rearrange("d (p h) n -> d p (h n)", p=2),
                                     a["oT"][t, HEAD * part:HEAD * (part + 1)].rearrange("d (p c) n -> d c p n", c=2)[:, c])\
                            .then_inc(m_ld[s], 16)
                sp.dma_start(graw[:, s], a["sgT"][t]).then_inc(m_ld[s], 16)
                if not early(t):
                    sp.wait_ge(xd, t - 1)
                sp.dma_start(xt[:, s, :], a["x1"][bass.ds(t * P, P), :]).then_inc(x_ld[s], 16)

            def store(t, s):
                sp.wait_ge(xd, t + 1)
                sp.dma_start(a["out"][0, bass.ds(t * P, P), :], out[:, s, :]).then_inc(ost[s], 16)

            load(0, 0)
            for k in range(KT):
                if k >= 2:
                    sp.wait_ge(wol[k % 2], k // 2)
                sp.dma_start(wr[:, k % 2, :], a["w_out1"][k]).then_inc(wr_ld[k % 2], 16)
            sp.dma_start(gpb[:], a["gp"][1, 0:1].partition_broadcast(P)).then_inc(par, 16)
            load(1, 1)

            def body(t, s, first, last):
                if not first and not last:
                    load(t + 1, 1 - s)
                if not first:
                    store(t - 1, 1 - s)

            loops(sp, body)
            store(LT - 1, 1)
            for s in range(2):
                sp.wait_ge(ost[s], 8 * LT)

        @blk.scalar
        def _(act):
            def split(t, s):
                act.wait_ge(md, t + 1)
                if not early(t):
                    act.wait_ge(yd, t - 1)
                nc.scalar.activation(m_hi[:, s], oraw[:, s, 0], ACT.Copy).then_inc(mh, 1)

            def epilogue(t, s):
                act.wait_ge(yd, t + 1)
                nc.scalar.activation(junk[:], Y[:, s, :], ACT.Square, accum_out=st[:, 0, s:s + 1]).then_inc(y1, 1)
                act.wait_ge(y1, t + 1)
                nc.scalar.activation(st[:, 1, s:s + 1], st[:, 0, s:s + 1], ACT.Sqrt, bias=eps[:, 0:1],
                                     scale=1.0 / D).then_inc(y2, 1)

            split(0, 0)
            for k in range(KT):
                act.wait_ge(wr_ld[k % 2], 16 * (k // 2 + 1))
                nc.scalar.activation(wo_hi[:, k, :], wr[:, k % 2, :], ACT.Copy).then_inc(woh, 1)
            split(1, 1)
            act.wait_ge(es, 1)

            def body(t, s, first, last):
                if not first:
                    epilogue(t - 1, 1 - s)
                    if not last:
                        split(t + 1, 1 - s)

            loops(act, body)
            epilogue(LT - 1, 1)

        @blk.vector
        def _(dve):
            tt, stt = nc.vector.tensor_tensor, nc.vector.scalar_tensor_tensor
            nc.vector.memset(eps[:], EPS).then_inc(es, 1)

            def mix(t, s):
                dve.wait_ge(m_ld[s], 40 * (t - s) + 80)
                tt(oraw[:, s, 0], oraw[:, s, 0], oraw[:, s, 1], ALU.add).then_inc(os_, 1)
                dve.wait_ge(os_, t + 1)
                stt(out=oraw[:, s, 0], in0=oraw[:, s, 0], scalar=0.5, in1=graw[:, s], op0=ALU.mult, op1=ALU.mult)\
                    .then_inc(md, 1)

            def epilogue(t, s):
                dve.wait_ge(y2, t + 1)
                nc.vector.reciprocal(st[:, 2, s:s + 1], st[:, 1, s:s + 1]).then_inc(y3, 1)
                dve.wait_ge(y3, t + 1)
                if not early(t):
                    dve.wait_ge(ost[s], 8 * (t - s))
                stt(out=out[:, s, :], in0=Y[:, s, :], scalar=st[:, 2, s:s + 1], in1=gpb[:], op0=ALU.mult,
                    op1=ALU.mult).then_inc(yn, 1)

            mix(0, 0)
            for k in range(1, KT, 2):
                dve.wait_ge(woh, k + 1)
                tt(wo_lo[:, k, :], wr[:, 1, :], v32(wo_hi[:, k, :]), ALU.subtract).then_inc(wol[1], 1)
            mix(1, 1)
            dve.wait_ge(par, 16)

            def body(t, s, first, last):
                if not first:
                    epilogue(t - 1, 1 - s)
                    if not last:
                        mix(t + 1, 1 - s)

            loops(dve, body)
            epilogue(LT - 1, 1)

        @blk.gpsimd
        def _(pool):
            tt = nc.gpsimd.tensor_tensor

            def split(t, s):
                pool.wait_ge(mh, t + 1)
                tt(m_lo[:, s], oraw[:, s, 0], v32(m_hi[:, s]), ALU.subtract).then_inc(ml, 1)

            def epilogue(t, s):
                pool.wait_ge(x_ld[s], 8 * (t - s) + 16)
                pool.wait_ge(yn, t + 1)
                tt(out[:, s, :], out[:, s, :], xt[:, s, :], ALU.add).then_inc(xd, 1)

            split(0, 0)
            for k in range(0, KT, 2):
                pool.wait_ge(woh, k + 1)
                tt(wo_lo[:, k, :], wr[:, 0, :], v32(wo_hi[:, k, :]), ALU.subtract).then_inc(wol[0], 1)
            split(1, 1)

            def body(t, s, first, last):
                if not first:
                    epilogue(t - 1, 1 - s)
                    if not last:
                        split(t + 1, 1 - s)

            loops(pool, body)
            epilogue(LT - 1, 1)

        @blk.tensor
        def _(pe):
            def body(t, s, first, last):
                pe.wait_ge(ml, t + 1)
                if not early(t):
                    pe.wait_ge(yn, t - 1)
                for k in range(KT):
                    if first:
                        pe.wait_ge(wol[k % 2], k // 2 + 1)
                    for n in (0, 512):
                        o = Y[:, s, n:n + 512]
                        w_hi, w_lo = wo_hi[:, k, n:n + 512], wo_lo[:, k, n:n + 512]
                        nc.tensor.matmul(o, m_hi[:, s, k, :], w_hi, start=(k == 0), stop=False)
                        nc.tensor.matmul(o, m_hi[:, s, k, :], w_lo, start=False, stop=False)
                        l = nc.tensor.matmul(o, m_lo[:, s, k, :], w_hi, start=False, stop=(k == KT - 1))
                l.then_inc(yd, 1)

            loops(pe, body)


def rev(buf):
    return buf[:, T - 1::-1]


def tables():
    m = np.arange(P)[:, None].astype(np.float64)
    k = np.arange(P)[None, :].astype(np.float64)
    out = np.zeros((P, TAB_N), np.float64)
    for key, at in TAB_AT.items():
        if isinstance(key, str):
            n, rad, r = N_CTX, 2, int(key[1])
        else:
            n, rad, r = N_LAT, RAD, key
        ang = 2 * np.pi * m * (rad * k + r) / n
        f = 1.0 / np.sqrt(n * P)
        if key in (1, 2, 3):
            out[:, at:at + P] = -np.sin(ang) * f
            at += P
        out[:, at:at + P] = np.cos(ang) * f
        out[:, at + P:at + 256] = np.sin(ang) * f
    ang = 2 * np.pi * m * k / P
    return out.astype(np.float32), np.concatenate([np.cos(ang), np.sin(ang)], 1).astype(np.float32)


def rope_tables():
    p = np.arange(P) % HEAD
    i = (p % 16).astype(np.float32)
    freq = (np.float32(ROPE_BASE) ** (-(2 * i) / np.float32(HEAD // 2))).astype(np.float32)
    tok = np.arange(N_LAT)
    pos = np.where((p < 32)[:, None], tok[None, :] // GRID_W, tok[None, :] % GRID_W).astype(np.float32)
    ang = (pos * freq[:, None]).astype(np.float64)
    sign = np.where(p % 32 < 16, -1.0, 1.0)[:, None]
    return np.stack([np.cos(ang), np.sin(ang) * sign]).astype(np.float32)


def window_mask():
    q, k = np.arange(P)[:, None], np.arange(P)[None, :]
    left, right, none = np.where(k >= q, 0.0, NEG_INF), np.where(k <= q, 0.0, NEG_INF), np.zeros((P, P))
    return np.concatenate([left, none, right, none, none, left, none, none, none], 1).astype(np.float32)


def paired(w):
    return w.reshape(w.shape[0], 2, 2, N_HD, HEAD).transpose(0, 1, 3, 2, 4).reshape(w.shape[0], D)


def build(nc, a):
    def layer1():
        with nc.sbuf_tensor("gs1", [P, 2, KT, 2], F32) as gs1:
            out_projection0(nc, a, gs1)
        with ExitStack() as ctx:
            kd_hi, kd_lo = (ctx.enter_context(nc.sbuf_tensor(n, [P, N_KV, T], F32R)) for n in ("kd_hi", "kd_lo"))
            vs = ctx.enter_context(nc.sbuf_tensor("vs", [P, TT, N_KV, P], F32R))
            projections1(nc, a, kd_hi, kd_lo, vs)
            attention(nc, a, kd_hi, kd_lo, vs)
        out_projection1(nc, a)

    with_semaphores(nc, a, lambda: layer0(nc, a))
    with_semaphores(nc, a, layer1)


def kernel(**inputs):
    import concourse.bacc as _bacc
    from concourse.bass_utils import run_bass_kernel_spmd as _run

    g = {k: np.ascontiguousarray(v) for k, v in inputs.items()}

    def col(v):
        return v.reshape(-1, KT, P).transpose(2, 0, 1)

    def slabs(w):
        return w.reshape(KT, P, -1, P).transpose(2, 1, 0, 3)

    def rows(layer):
        r = np.concatenate([g[layer + "_b_mod"], g[layer + "_g_pre"], g[layer + "_g_post"]])
        return np.stack([r, r])

    tab, dft_ch = tables()
    w0 = slabs(g["l0_w_in"])
    w_gate = np.stack([g["l0_w_a"][0], g["l0_w_x"][0], g["l0_w_a"][1], g["l0_w_x"][1]])
    w1, kv = g["l1_w_in"], N_KV * HEAD
    qg = np.stack([slabs(paired(w1[:, 0:D])), slabs(paired(w1[:, D + 2 * kv:]))], 1).reshape(2 * KT, P, KT, P)
    w_in1 = np.concatenate([slabs(w1[:, D:D + 2 * kv]), qg]).reshape(-1, P, D)
    arrays = {
        "x": np.concatenate([g["x"][0], g["ctx"][0]]),
        "cvec": np.stack([g["c"][0], g["c_ctx"]]).reshape(2, KT, P).transpose(2, 1, 0),
        "rows0": rows("l0"),
        "rows1": rows("l1"),
        "cols": np.concatenate([col(g["l0_w_conv"]), col(g["l0_b_conv"]), col(g["l0_b_a"]), col(g["l0_b_x"]),
                                col(g["l0_lam"]), col(g["l0_b_f"])], 1),
        "ident": np.eye(P, dtype=np.float32),
        "tables": tab,
        "dft_ch": dft_ch,
        "wm0": g["l0_w_mod"],
        "wm1": g["l1_w_mod"].reshape(KT, P, 2 * KT, MOD_C).transpose(2, 1, 0, 3),
        "w_in0": np.stack([w0[0:8], w0[16:24], w0[24:32], w0[8:16]], 1).reshape(4 * KT, P, D),
        "w_gate": w_gate.reshape(4, KT, 2 * HEAD, HEAD).transpose(1, 2, 0, 3),
        "w_f": g["l0_w_f"],
        "w_out0": g["l0_w_out"],
        "w_in1": w_in1,
        "rope": rope_tables(),
        "sink": np.broadcast_to(g["l1_sink"], (P, N_HEADS)),
        "mask": window_mask(),
        "w_out1": paired(g["l1_w_out"].T).T.reshape(KT, P, D),
    }
    nc = _bacc.Bacc("TRN2", target_bir_lowering=False, num_devices=1, dynamic_dma_scratch_size=1024)
    a = {}
    for name, v in list(arrays.items()):
        arrays[name] = v = np.ascontiguousarray(v)
        a[name] = nc.dram_tensor("in_" + name, v.shape, F32, kind="ExternalInput").ap()
    for name, shape in (("gp", (2, 2, D)), ("mod1", (2, 2 * KT, MOD_C)), ("mixT", (2 * KT, P, T)),
                        ("x1", (N_LAT, D)), ("hT1", (TT, P, KT, P)), ("qT", (LT, 2, P, KT, P)), ("sgT", (LT, P, KT, P)),
                        ("oT", (LT, P, N_KV, N_HD * P))):
        a[name] = nc.dram_tensor(name, shape, F32, kind="Internal").ap()
    a["out"] = nc.dram_tensor("out", (1, N_LAT, D), F32, kind="ExternalOutput").ap()
    build(nc, a)
    r = _run(nc, [{"in_" + k: v for k, v in arrays.items()}], core_ids=[0])
    return r.results[0]["out"]
```

```python
import numpy as np
from contextlib import ExitStack

import concourse.bass as bass
from concourse import mybir

F32 = mybir.dt.float32
F32R = mybir.dt.float32r
ALU = mybir.AluOpType
ACT = mybir.ActivationFunctionType

P = 128
D = 1024
KT = D // P
N_LAT, N_CTX = 1024, 256
T = N_LAT + N_CTX
TT = T // P
LT = N_LAT // P
EPS = 1e-6
CHUNKS = [(0, 512), (512, 512), (1024, 256)]
GRID_W = 64
HEAD = 64
N_HEADS, N_KV = 16, 4
ROPE_BASE = 10000.0
NEG_INF = -1e30
SCALE = HEAD ** -0.5

CONV_W, CONV_LEFT = 4, 2
CTX_AT = N_LAT + CONV_LEFT
CONV_N = CTX_AT + N_CTX

RAD = N_LAT // P
N_R = RAD // 2 + 1
TAB_AT = {0: 0, 4: 256, 1: 512, 2: 896, 3: 1280, "c0": 1664, "c1": 1920}
TAB_N = 2176
PQ_N = (N_R + 2) * 256
UV_N = (N_R + 2) * P

MOD_C = 192
ROWS = 5 * D

C_CONV, C_BCONV, C_BA, C_BX, C_LAM, C_BF, N_COLS = 0, 4, 5, 7, 9, 11, 12
C_HALF, C_KPOS, C_KNEG, C_KNEG2, ALL_COLS = 12, 16, 18, 20, 22


def v32(ap):
    return ap.bitcast(F32)


def with_semaphores(nc, a, stages):
    used = []

    def sem(name):
        used.append(nc.alloc_semaphore(name=name))
        return used[-1]

    a["sem"] = sem
    stages()
    nc.clear_and_free_semaphores(used)
    nc.all_engine_barrier()


def layer0(nc, a):
    ctx = ExitStack()
    with ctx:
        def sb(name, shape, dt=F32):
            return ctx.enter_context(nc.sbuf_tensor(name, shape, dt))

        sem = a["sem"]

        h_hi, h_lo = sb("h_hi", [P, KT, T], F32R), sb("h_lo", [P, KT, T], F32R)
        cols = sb("cols", [P, ALL_COLS, KT])
        silu_c = sb("silu_c", [P, KT, 2])
        gs = sb("gs", [P, 2, KT, 2])
        work = sb("work", [P, KT, T])
        wraw = sb("wraw", [P, 2, D])
        w_ld = [sem("w_loaded0"), sem("w_loaded1")]
        setup(nc, a, work, cols, silu_c, gs, wraw, w_ld)
        mixers(nc, a, h_hi, h_lo, work, cols, silu_c, gs, wraw, w_ld)


def setup(nc, a, xT, cols, silu_c, gs, wraw, w_ld):
    ctx = ExitStack()
    with ctx:
        def sb(name, shape, dt=F32):
            return ctx.enter_context(nc.sbuf_tensor(name, shape, dt))

        sem = a["sem"]

        xt = sb("xt", [P, 2, D])
        junk = sb("junk", [P, D])
        xn = sb("xn", [P, 2, D])
        stat = sb("stat", [P, 3, TT])
        ident = sb("ident0", [P, P])
        cvec = sb("cvec", [P, KT, 2])
        th_c = sb("th_c", [P, KT, 2])
        wm = sb("wm", [P, 2, 3 * D])
        rows = sb("rows", [2, ROWS])
        mod = sb("mod", [2, 3 * D])
        sp_t = sb("sp_t", [P, 6, 2 * KT])
        eps = sb("eps0", [P, 1])
        pm = ctx.enter_context(nc.psum_tensor("pm", [2, 3 * D], F32))
        pt = ctx.enter_context(nc.psum_tensor("pt", [P, 2, 4, P], F32))

        par = sem("par_loaded")
        x_ld = [sem("x_loaded0"), sem("x_loaded1")]
        wm_ld = [sem("wm_loaded0"), sem("wm_loaded1")]
        ss, rt, rs, xs = sem("ss_done"), sem("root_done"), sem("rstd_done"), sem("xn_done")
        tr, te = sem("x_transposed"), sem("xT_written")
        kstep = sem("k_step")
        thc, sc_ = sem("tanh_c"), sem("silu_c_done")
        modk, mrow, mtr, gsd = sem("mod_k_done"), sem("mod_row_done"), sem("mod_transposed"), sem("gs_done")
        spre, spost = sem("exp_lam_in"), sem("exp_lam")
        gst, est = sem("gate_row_stored"), sem("eps_set")
        blk = ctx.enter_context(nc.Block())

        def x_tile(i):
            return a["x"][i * P:(i + 1) * P, :]

        @blk.sync
        def _(sp):
            sp.dma_start(cvec[:], a["cvec"]).then_inc(par, 16)
            sp.dma_start(rows[:], a["rows0"]).then_inc(par, 16)
            sp.dma_start(cols[:, 0:N_COLS, :], a["cols"]).then_inc(par, 16)
            sp.dma_start(ident[:], a["ident"]).then_inc(par, 16)
            for i in range(TT):
                if i >= 2:
                    sp.wait_ge(xs, i - 1)
                sp.dma_start(xt[:, i % 2, :], x_tile(i)).then_inc(x_ld[i % 2], 16)
                if i < KT:
                    if i >= 2:
                        sp.wait_ge(modk, i - 1)
                    sp.dma_start(wm[:, i % 2, :], a["wm0"][i * P:(i + 1) * P, :]).then_inc(wm_ld[i % 2], 16)
            for j in range(2):
                sp.dma_start(wraw[:, j, :], a["w_in0"][j]).then_inc(w_ld[j], 16)
                sp.wait_ge(w_ld[j], 16)
            sp.wait_ge(mrow, 8)
            sp.dma_start(a["gp"][0], mod[:, 2 * D:3 * D]).then_inc(gst, 16)
            sp.wait_ge(gst, 16)

        @blk.scalar
        def _(act):
            act.wait_ge(par, 64)
            nc.scalar.activation(th_c[:], cvec[:], ACT.Tanh, scale=0.5).then_inc(thc, 1)
            act.wait_ge(spre, 1)
            nc.scalar.activation(sp_t[:, 1, :], sp_t[:, 0, :], ACT.Exp).then_inc(spost, 1)
            act.wait_ge(est, 1)
            for i in range(TT):
                act.wait_ge(x_ld[i % 2], 16 * (i // 2 + 1))
                nc.scalar.activation(junk[:], xt[:, i % 2, :], ACT.Square,
                                     accum_out=stat[:, 0, i:i + 1]).then_inc(ss, 1)
                act.wait_ge(ss, i + 1)
                nc.scalar.activation(stat[:, 1, i:i + 1], stat[:, 0, i:i + 1], ACT.Sqrt,
                                     bias=eps[:, 0:1], scale=1.0 / D).then_inc(rt, 1)
                if i >= 1:
                    for h in range(2):
                        act.wait_ge(tr, 2 * (i - 1) + h + 1)
                        nc.scalar.activation(xT[:, 4 * h:4 * h + 4, (i - 1) * P:i * P], pt[:, h, :, :],
                                             ACT.Copy).then_inc(te, 1)
            for h in range(2):
                act.wait_ge(tr, 2 * (TT - 1) + h + 1)
                nc.scalar.activation(xT[:, 4 * h:4 * h + 4, (TT - 1) * P:TT * P], pt[:, h, :, :],
                                     ACT.Copy).then_inc(te, 1)

        @blk.vector
        def _(dve):
            nc.vector.memset(eps[:], EPS).then_inc(est, 1)
            dve.wait_ge(par, 64)
            n = [0]

            def step(ins):
                n[0] += 1
                ins.then_inc(kstep, 1)
                dve.wait_ge(kstep, n[0])

            dve.wait_ge(thc, 1)
            step(nc.vector.scalar_tensor_tensor(out=silu_c[:], in0=th_c[:], scalar=1.0, in1=cvec[:],
                                                op0=ALU.add, op1=ALU.mult))
            nc.vector.tensor_scalar(silu_c[:], silu_c[:], 0.5, None, ALU.mult).then_inc(sc_, 1)
            lam = cols[:, C_LAM:C_LAM + 2, :].rearrange("p a k -> p (a k)")
            step(nc.vector.tensor_scalar(sp_t[:, 2, :], lam, -1.0, None, ALU.mult))
            nc.vector.tensor_tensor(sp_t[:, 0, :], sp_t[:, 2, :], lam, ALU.min).then_inc(spre, 1)
            step(nc.vector.tensor_scalar(cols[:, C_HALF:C_HALF + 4, :].rearrange("p a k -> p (a k)"),
                                         cols[:, C_BA:C_BA + 4, :].rearrange("p a k -> p (a k)"),
                                         0.5, None, ALU.mult))
            def softplus_and_rates():
                dve.wait_ge(spost, 1)
                step(nc.vector.tensor_scalar(sp_t[:, 3, :], sp_t[:, 1, :], 2.0, None, ALU.add))
                step(nc.vector.reciprocal(sp_t[:, 3, :], sp_t[:, 3, :]))
                step(nc.vector.tensor_tensor(sp_t[:, 3, :], sp_t[:, 1, :], sp_t[:, 3, :], ALU.mult))
                step(nc.vector.tensor_tensor(sp_t[:, 4, :], sp_t[:, 3, :], sp_t[:, 3, :], ALU.mult))
                step(nc.vector.tensor_scalar(sp_t[:, 5, :], sp_t[:, 4, :], 1.0 / 17, 1.0 / 15, ALU.mult, ALU.add))
                for q in (13, 11, 9, 7, 5, 3, 1):
                    step(nc.vector.tensor_tensor(sp_t[:, 5, :], sp_t[:, 5, :], sp_t[:, 4, :], ALU.mult))
                    step(nc.vector.tensor_scalar(sp_t[:, 5, :], sp_t[:, 5, :], 1.0 / q, None, ALU.add))
                step(nc.vector.scalar_tensor_tensor(out=sp_t[:, 5, :], in0=sp_t[:, 5, :], scalar=2.0,
                                                    in1=sp_t[:, 3, :], op0=ALU.mult, op1=ALU.mult))
                step(nc.vector.scalar_tensor_tensor(out=sp_t[:, 5, :], in0=sp_t[:, 2, :], scalar=0.0,
                                                    in1=sp_t[:, 5, :], op0=ALU.max, op1=ALU.add))
                for at, f in ((C_KPOS, 4.0), (C_KNEG, -4.0), (C_KNEG2, -8.0)):
                    step(nc.vector.tensor_scalar(cols[:, at:at + 2, :].rearrange("p a k -> p (a k)"), sp_t[:, 5, :], f, None,
                                                 ALU.mult))

            for i in range(TT):
                dve.wait_ge(rt, i + 1)
                nc.vector.reciprocal(stat[:, 2, i:i + 1], stat[:, 1, i:i + 1]).then_inc(rs, 1)
                dve.wait_ge(rs, i + 1)
                if i >= 2:
                    dve.wait_ge(tr, 2 * (i - 1))
                nc.vector.tensor_scalar(xn[:, i % 2, :], xt[:, i % 2, :], stat[:, 2, i:i + 1], None,
                                        ALU.mult).then_inc(xs, 1)
                if i == TT // 2:
                    softplus_and_rates()
            dve.wait_ge(modk, KT)
            def bias(c):
                nc.vector.tensor_tensor(mod[:, c * 512:(c + 1) * 512], pm[:, c * 512:(c + 1) * 512],
                                        rows[:, c * 512:(c + 1) * 512], ALU.add).then_inc(mrow, 1)

            for c in range(4):
                bias(c)
            dve.wait_ge(mrow, 4)
            nc.vector.scalar_tensor_tensor(out=mod[:, D:2 * D], in0=mod[:, D:2 * D], scalar=1.0,
                                           in1=rows[:, 3 * D:4 * D], op0=ALU.add, op1=ALU.mult).then_inc(mrow, 1)
            for c in (4, 5):
                bias(c)
            dve.wait_ge(mrow, 7)
            nc.vector.tensor_tensor(mod[:, 2 * D:3 * D], mod[:, 2 * D:3 * D], rows[:, 4 * D:5 * D],
                                    ALU.mult).then_inc(mrow, 1)
            dve.wait_ge(mtr, 1)
            nc.vector.tensor_copy(gs[:].rearrange("p a k w -> p (a k w)"), pm_cols(pt)).then_inc(gsd, 1)

        @blk.tensor
        def _(pe):
            pe.wait_ge(sc_, 1)
            for i in range(TT):
                pe.wait_ge(xs, i + 1)
                for h in range(2):
                    if i >= 1:
                        pe.wait_ge(te, 2 * (i - 1) + h + 1)
                    for q in range(4):
                        last = nc.tensor.transpose(pt[:, h, q, :], xn[:, i % 2, (4 * h + q) * P:(4 * h + q + 1) * P],
                                                   ident[:])
                    last.then_inc(tr, 1)
                if i < KT:
                    pe.wait_ge(wm_ld[i % 2], 16 * (i // 2 + 1))
                    for c in range(6):
                        last = nc.tensor.matmul(pm[:, c * 512:(c + 1) * 512], silu_c[:, i, :],
                                                wm[:, i % 2, c * 512:(c + 1) * 512], start=(i == 0), stop=(i == KT - 1))
                    last.then_inc(modk, 1)
            pe.wait_ge(te, 2 * TT)
            pe.wait_ge(mrow, 5)
            for q in range(2 * KT):
                last = nc.tensor.transpose(pt[:, 0, 0, 2 * q:2 * q + 2], mod[:, q * P:(q + 1) * P], ident[0:2, 0:2])
            last.then_inc(mtr, 1)


def pm_cols(pt):
    return pt[:, 0, 0, 0:4 * KT]


def mixers(nc, a, h_hi, h_lo, work, cols, silu_c, gs, wraw, w_ld):
    ctx = ExitStack()
    with ctx:
        def sb(name, shape, dt=F32):
            return ctx.enter_context(nc.sbuf_tensor(name, shape, dt))

        sem = a["sem"]

        w_hi, w_lo = sb("w_hi", [P, 2, KT, P], F32R), sb("w_lo", [P, 2, KT, P], F32R)
        tab_hi, tab_lo = sb("tab_hi", [P, TAB_N], F32R), sb("tab_lo", [P, TAB_N], F32R)
        dft_ch = sb("dft_ch", [P, 256])
        ident = sb("ident1", [P, P])
        u_raw = sb("u_raw", [P, CONV_N + CONV_W - 1])
        u_hi, u_lo = sb("u_hi", [P, T], F32R), sb("u_lo", [P, T], F32R)
        cur = sb("cur", [P, ALL_COLS])
        gw = sb("gw", [P, 4, P])
        gw_hi, gw_lo = sb("gw_hi", [P, 4, P], F32R), sb("gw_lo", [P, 4, P], F32R)
        A, B, C, H, sgf, fT, xf, u = (work[:, i, :] for i in range(KT))
        E = sb("E", [P, CONV_N])
        y_hi, y_lo = sb("y_hi", [P, T], F32R), sb("y_lo", [P, T], F32R)
        pq_hi, pq_lo = sb("pq_hi", [P, PQ_N], F32R), sb("pq_lo", [P, PQ_N], F32R)
        wf = sb("wf", [P, P])
        ab_hi, ab_lo = sb("ab_hi", [P, 2 * P], F32R), sb("ab_lo", [P, 2 * P], F32R)
        wm1 = sb("wm1", [P, KT, MOD_C])
        m_row = sb("m_row", [2, MOD_C])
        slab = ctx.enter_context(nc.psum_tensor("slab", [P, 3, 512], F32))
        W = ctx.enter_context(nc.psum_tensor("W", [P, 4, 512], F32))
        W4 = ctx.enter_context(nc.psum_tensor("W4", [P, 512], F32))
        Wf = W[:].rearrange("p b n -> p (b n)")

        par = sem("mix_par_loaded")
        tab_ld, tab_h, tab_l = sem("table_loaded"), sem("table_hi"), sem("table_lo")
        zero, cu_ = sem("zeros_set"), sem("columns_copied")
        hh, h32, hl = sem("h_hi_done"), sem("h32_done"), [sem("h_lo_pool"), sem("h_lo_dve")]
        wh = [sem("w_hi_done0"), sem("w_hi_done1")]
        wl = [sem("w_lo_done0"), sem("w_lo_done1")]
        gw_ld, gwh, gwl = sem("gate_w_loaded"), sem("gate_w_hi"), sem("gate_w_lo")
        wf_ld, abp, abh, abl = sem("wf_loaded"), sem("ab_product"), sem("ab_hi_done"), sem("ab_lo_done")
        s_u, s_f, s_gf, s_g = sem("slab_u"), sem("slab_f"), sem("slab_gf"), sem("slab_g")
        ur, tap0, taps, conv = sem("u_raw_ready"), sem("tap0"), sem("taps"), sem("conv_done")
        uh, ul = sem("u_hi_done"), sem("u_lo_done")
        fr, trd, xr = sem("fT_ready"), sem("f_transposed"), sem("x_ready")
        bf2, bf3, yc = sem("butterfly2"), sem("butterfly3"), sem("y_parts")
        bf, yr, yh, yl = sem("butterfly"), sem("y_ready"), sem("y_hi_done"), sem("y_lo_done")
        dft, pqh, pql, uv, us, yd = sem("dft_done"), sem("pq_hi"), sem("pq_lo"), sem("uv_done"), sem("us_ready"), sem("y_combined")
        tgf, sgfd, tg, sg = sem("tanh_gf"), sem("silu_gf"), sem("tanh_g"), sem("silu_g")
        gp_, gr = sem("gate_product"), sem("gate_read")
        th, e2, ea = sem("tanh_loga"), sem("a_squared"), sem("a_ready")
        iu, om, sq, bt, hd, hs = sem("iu"), sem("one_minus_a2"), sem("root"), sem("b_ready"), sem("scan_done"), sem("h_sum")
        cf = sem("scan_ctx")
        mf, mr, mfs, mrs = sem("mix_f"), sem("mix_r"), sem("mix_f_stored"), sem("mix_r_stored")
        m_ld, mp, me, ms = sem("wmod1_loaded"), sem("mod1_product"), sem("mod1_row"), sem("mod1_stored")
        blk = ctx.enter_context(nc.Block())
        SLAB_U, SLAB_F, SLAB_GF, SLAB_G = range(4)
        done = [s_u, s_f, s_gf, s_g]
        half = TAB_N // 2
        tab_pieces = [(E[:, 0:half], slice(0, half)), (u_raw[:, 0:half], slice(half, TAB_N))]

        def loops(eng, body, n=KT):
            body(0, True, False)
            with eng.Fori(1, n - 1) as t:
                body(t, False, False)
            body(n - 1, False, True)

        @blk.sync
        def _(sp):
            sp.dma_start(dft_ch[:], a["dft_ch"]).then_inc(par, 16)
            sp.dma_start(ident[:], a["ident"]).then_inc(par, 16)

            def load_slab(t, j, first):
                if not (first and j < 2):
                    sp.wait_ge(wl[j % 2], 2 * t + j // 2)
                sp.dma_start(wraw[:, j % 2, :], a["w_in0"][4 * t + j]).then_inc(w_ld[j % 2], 16)

            def store(t):
                sp.wait_ge(mr, t + 1)
                sp.dma_start(a["mixT"][t], H[:]).then_inc(mrs, 16)
                sp.wait_ge(mf, t + 1)
                sp.dma_start(a["mixT"][t + KT], xf[:]).then_inc(mfs, 16)
                store_mod(t, 1)

            def store_mod(t, q):
                sp.wait_ge(me, 2 * t + q + 1)
                sp.dma_start(a["mod1"][:, 2 * t + q, :], m_row[:]).then_inc(ms, 16)

            def load_mod(t, q, first):
                if not (first and q == 0):
                    sp.wait_ge(mp, 2 * t + q)
                sp.dma_start(wm1[:], a["wm1"][2 * t + q]).then_inc(m_ld, 16)

            def body(t, first, last):
                if first:
                    for raw, at in tab_pieces:
                        sp.dma_start(raw, a["tables"][:, at]).then_inc(tab_ld, 16)
                load_mod(t, 0, first)
                if first:
                    sp.wait_ge(zero, 2)
                else:
                    sp.wait_ge(gwl, t)
                for c in range(2):
                    sp.dma_start(gw[HEAD * c:HEAD * (c + 1), :, HEAD * c:HEAD * (c + 1)],
                                 a["w_gate"][t, HEAD * c:HEAD * (c + 1), :, :]).then_inc(gw_ld, 16)
                if not first:
                    sp.wait_ge(abp, t)
                sp.dma_start(wf[:], a["w_f"][t]).then_inc(wf_ld, 16)
                load_slab(t, SLAB_GF, first)
                load_slab(t, SLAB_G, first)
                if not first:
                    store(t - 1)
                store_mod(t, 0)
                load_mod(t, 1, first)
                if not last:
                    load_slab(t + 1, SLAB_U, False)
                    load_slab(t + 1, SLAB_F, False)

            loops(sp, body)
            store(KT - 1)
            sp.wait_ge(mrs, 16 * KT)
            sp.wait_ge(mfs, 16 * KT)
            sp.wait_ge(ms, 32 * KT)

        @blk.scalar
        def _(act):
            def split_hi(t, j, first=False):
                act.wait_ge(w_ld[j % 2], 16 * (2 * t + j // 2 + 1))
                if j >= 2:
                    act.wait_ge(done[j - 2], 3 * t + 3)
                elif not first:
                    act.wait_ge(done[j + 2], 3 * t)
                nc.scalar.activation(w_hi[:, j % 2].rearrange("p k n -> p (k n)"), wraw[:, j % 2, :],
                                     ACT.Copy).then_inc(wh[j % 2], 1)

            def gates(t, d, first):
                for x in range(2):
                    dst = (A, B)[x]
                    if x == 0:
                        if d == 1:
                            act.wait_ge(hd, 2 * t + 1)
                        elif not first:
                            act.wait_ge(mr, t)
                    for c, (at, n) in enumerate(CHUNKS):
                        k = 6 * d + 3 * x + c
                        act.wait_ge(gp_, 12 * t + k + 1)
                        nc.scalar.activation(dst[:, at:at + n], W[:, k % 4, 0:n], ACT.Tanh, scale=0.5,
                                             bias=cur[:, C_HALF + 2 * x + d:C_HALF + 2 * x + d + 1]).then_inc(gr, 1)
                act.wait_ge(gr, 12 * t + 6 * d + 3)
                if d == 0:
                    act.wait_ge(conv, 2 * t + 2)
                else:
                    act.wait_ge(bt, 2 * t + 1)
                nc.scalar.activation(E[:, 0:T], A[:], ACT.Tanh, scale=cur[:, C_KPOS + d:C_KPOS + d + 1],
                                     bias=cur[:, C_KPOS + d:C_KPOS + d + 1]).then_inc(th, 1)
                nc.scalar.activation(C[:], A[:], ACT.Exp, scale=cur[:, C_KNEG2 + d:C_KNEG2 + d + 1],
                                     bias=cur[:, C_KNEG2 + d:C_KNEG2 + d + 1]).then_inc(e2, 1)
                act.wait_ge(e2, 2 * t + d + 1)
                act.wait_ge(th, 2 * t + d + 1)
                nc.scalar.activation(A[:], A[:], ACT.Exp, scale=cur[:, C_KNEG + d:C_KNEG + d + 1],
                                     bias=cur[:, C_KNEG + d:C_KNEG + d + 1]).then_inc(ea, 1)

            def root(t, d):
                act.wait_ge(om, 2 * t + d + 1)
                nc.scalar.activation(C[:], C[:], ACT.Sqrt).then_inc(sq, 1)

            def mod_row(t, q, first):
                act.wait_ge(mp, 2 * t + q + 1)
                if not (first and q == 0):
                    act.wait_ge(ms, 16 * (2 * t + q))
                nc.scalar.activation(m_row[:], W4[0:2, 0:MOD_C], ACT.Copy).then_inc(me, 1)

            def body(t, first, last):
                if not first:
                    split_hi(t, SLAB_F)
                if first:
                    act.wait_ge(zero, 2)
                else:
                    act.wait_ge(conv, 2 * t)
                for c, (at, n) in enumerate(CHUNKS):
                    act.wait_ge(s_u, 3 * t + c + 1)
                    to = CONV_LEFT + at + (CTX_AT - N_LAT if c == 2 else 0)
                    nc.scalar.activation(u_raw[:, to:to + n], slab[:, c, 0:n], ACT.Copy).then_inc(ur, 1)
                if first:
                    act.wait_ge(tab_l, 2)
                else:
                    act.wait_ge(hs, t)
                act.wait_ge(ur, 3 * t + 3)
                act.wait_ge(cu_, t + 1)
                nc.scalar.activation(E[:], u_raw[:, 0:CONV_N], ACT.Identity, scale=cur[:, C_CONV:C_CONV + 1],
                                     bias=cur[:, C_BCONV:C_BCONV + 1]).then_inc(tap0, 1)
                mod_row(t, 0, first)
                split_hi(t, SLAB_GF)
                act.wait_ge(gw_ld, 32 * t + 32)
                if not first:
                    act.wait_ge(gp_, 12 * t)
                nc.scalar.activation(gw_hi[:], gw[:], ACT.Copy).then_inc(gwh, 1)
                act.wait_ge(conv, 2 * t + 2)
                nc.scalar.activation(u_hi[:], u[:], ACT.Copy).then_inc(uh, 1)
                if not first:
                    act.wait_ge(yd, t)
                for c, (at, n) in enumerate(CHUNKS):
                    act.wait_ge(s_f, 3 * t + c + 1)
                    nc.scalar.activation(fT[:, at:at + n], slab[:, c, 0:n], ACT.Copy).then_inc(fr, 1)
                if not first:
                    act.wait_ge(mfs, 16 * t)
                for c, (at, n) in enumerate(CHUNKS):
                    act.wait_ge(trd, 3 * t + c + 1)
                    nc.scalar.activation(xf[:, at:at + n], W[:, c, 0:n], ACT.Copy).then_inc(xr, 1)
                act.wait_ge(abp, t + 1)
                nc.scalar.activation(ab_hi[:], W4[:, 0:256], ACT.Copy).then_inc(abh, 1)
                gates(t, 0, first)
                split_hi(t, SLAB_G)
                act.wait_ge(yr, t + 1)
                if not first:
                    act.wait_ge(dft, t)
                nc.scalar.activation(y_hi[:], xf[:], ACT.Copy).then_inc(yh, 1)
                root(t, 0)
                if not first:
                    act.wait_ge(mf, t)
                for c, (at, n) in enumerate(CHUNKS):
                    act.wait_ge(s_gf, 3 * t + c + 1)
                    nc.scalar.activation(sgf[:, at:at + n], slab[:, c, 0:n], ACT.Tanh, scale=0.5).then_inc(tgf, 1)
                gates(t, 1, first)
                act.wait_ge(dft, t + 1)
                if not first:
                    act.wait_ge(uv, t)
                nc.scalar.activation(pq_hi[:], Wf[:, 0:PQ_N], ACT.Copy).then_inc(pqh, 1)
                if not last:
                    split_hi(t + 1, SLAB_U)
                root(t, 1)
                act.wait_ge(hd, 2 * t + 2)
                for c, (at, n) in enumerate(CHUNKS):
                    act.wait_ge(s_g, 3 * t + c + 1)
                    nc.scalar.activation(B[:, at:at + n], slab[:, c, 0:n], ACT.Tanh, scale=0.5).then_inc(tg, 1)
                act.wait_ge(uv, t + 1)
                nc.scalar.activation(fT[:, 0:UV_N], Wf[:, 0:UV_N], ACT.Identity,
                                     bias=cur[:, C_BF:C_BF + 1]).then_inc(us, 1)
                mod_row(t, 1, first)

            split_hi(0, SLAB_U, True)
            split_hi(0, SLAB_F, True)
            for k in range(KT):
                for w, (at, n) in enumerate([(0, N_LAT), (N_LAT, N_CTX)]):
                    nc.scalar.activation(h_hi[:, k, at:at + n], work[:, k, at:at + n], ACT.Identity,
                                         scale=gs[:, 1, k, w:w + 1], bias=gs[:, 0, k, w:w + 1]).then_inc(hh, 1)
            act.wait_ge(tab_ld, 32)
            for raw, at in tab_pieces:
                nc.scalar.activation(tab_hi[:, at], raw, ACT.Copy).then_inc(tab_h, 1)
            loops(act, body)

        @blk.vector
        def _(dve):
            for k in range(KT):
                dve.wait_ge(hh, 2 * k + 2)
                for w, (at, n) in enumerate([(0, N_LAT), (N_LAT, N_CTX)]):
                    nc.vector.tensor_scalar(work[:, k, at:at + n], work[:, k, at:at + n], gs[:, 1, k, w:w + 1],
                                            gs[:, 0, k, w:w + 1], ALU.mult, ALU.add).then_inc(h32, 1)
                if k % 2 == 1:
                    dve.wait_ge(h32, 2 * k + 2)
                    nc.vector.tensor_tensor(h_lo[:, k, :], work[:, k, :], v32(h_hi[:, k, :]),
                                            ALU.subtract).then_inc(hl[1], 1)
            for i, (raw, at) in enumerate(tab_pieces):
                dve.wait_ge(tab_h, i + 1)
                nc.vector.tensor_tensor(tab_lo[:, at], raw, v32(tab_hi[:, at]), ALU.subtract).then_inc(tab_l, 1)
            dve.wait_ge(tab_l, 2)
            nc.vector.memset(u_raw[:], 0.0).then_inc(zero, 1)
            nc.vector.memset(gw[:], 0.0).then_inc(zero, 1)

            def body(t, first, last):
                if not first:
                    dve.wait_ge(us, t)
                nc.vector.tensor_scalar(cur[:], cols[:, :, t], 1.0, None, ALU.mult).then_inc(cu_, 1)
                dve.wait_ge(tap0, t + 1)
                for k in (1, 2):
                    nc.vector.scalar_tensor_tensor(out=E[:], in0=u_raw[:, k:k + CONV_N],
                                                   scalar=cur[:, C_CONV + k:C_CONV + k + 1], in1=E[:],
                                                   op0=ALU.mult, op1=ALU.add).then_inc(taps, 1)
                    dve.wait_ge(taps, 2 * t + k)
                if not first:
                    dve.wait_ge(ul, t)
                for at, to, n in ((0, 0, N_LAT), (CTX_AT, N_LAT, N_CTX)):
                    nc.vector.scalar_tensor_tensor(out=u[:, to:to + n], in0=u_raw[:, at + 3:at + 3 + n],
                                                   scalar=cur[:, C_CONV + 3:C_CONV + 4], in1=E[:, at:at + n],
                                                   op0=ALU.mult, op1=ALU.add).then_inc(conv, 1)
                b0 = 8 * t

                def q(buf, i, n=1):
                    return buf[:, i * P:(i + n) * P]

                dve.wait_ge(xr, 3 * t + 3)
                tt = nc.vector.tensor_tensor
                tt(q(fT, 0, 4), q(xf, 0, 4), q(xf, 4, 4), ALU.add).then_inc(bf, 1)
                tt(q(fT, 4, 4), q(xf, 0, 4), q(xf, 4, 4), ALU.subtract).then_inc(bf, 1)
                tt(q(fT, 8), q(xf, 8), q(xf, 9), ALU.subtract).then_inc(bf, 1)
                tt(q(fT, 9), q(xf, 8), q(xf, 9), ALU.add).then_inc(bf, 1)
                dve.wait_ge(bf, b0 + 4)
                tt(q(xf, 6, 2), q(fT, 0, 2), q(fT, 2, 2), ALU.add).then_inc(bf, 1)
                tt(q(xf, 4, 2), q(fT, 0, 2), q(fT, 2, 2), ALU.subtract).then_inc(bf, 1)
                dve.wait_ge(bf, b0 + 6)
                tt(q(fT, 0), q(fT, 5), q(fT, 7), ALU.add).then_inc(bf, 1)
                tt(q(fT, 1), q(fT, 5), q(fT, 7), ALU.subtract).then_inc(bf, 1)
                dve.wait_ge(bf, b0 + 8)
                stt = nc.vector.scalar_tensor_tensor
                s = float(np.sqrt(0.5))
                tt(q(xf, 0), q(xf, 6), q(xf, 7), ALU.add).then_inc(bf2, 1)
                tt(q(xf, 1), q(xf, 6), q(xf, 7), ALU.subtract).then_inc(bf2, 1)
                stt(out=q(xf, 2), in0=q(fT, 1), scalar=s, in1=q(fT, 4), op0=ALU.mult, op1=ALU.add).then_inc(bf2, 1)
                stt(out=q(xf, 3), in0=q(fT, 0), scalar=s, in1=q(fT, 6), op0=ALU.mult, op1=ALU.add).then_inc(bf2, 1)
                dve.wait_ge(bf2, 4 * t + 4)
                stt(out=q(xf, 6), in0=q(fT, 1), scalar=-s, in1=q(fT, 4), op0=ALU.mult, op1=ALU.add).then_inc(bf3, 1)
                stt(out=q(xf, 7), in0=q(fT, 0), scalar=s, in1=q(fT, 6), op0=ALU.mult, op1=ALU.subtract).then_inc(bf3, 1)
                nc.vector.tensor_copy(q(xf, 8), q(fT, 9)).then_inc(bf3, 1)
                nc.vector.tensor_copy(q(xf, 9), q(fT, 8)).then_inc(yr, 1)
                dve.wait_ge(abh, t + 1)
                tt(ab_lo[:], W4[:, 0:256], v32(ab_hi[:]), ALU.subtract).then_inc(abl, 1)

                def direction(d):
                    dve.wait_ge(gr, 12 * t + 6 * d + 6)
                    stt(out=B[:], in0=B[:], scalar=1.0, in1=u[:], op0=ALU.add, op1=ALU.mult).then_inc(iu, 1)
                    dve.wait_ge(th, 2 * t + d + 1)
                    dve.wait_ge(e2, 2 * t + d + 1)
                    stt(out=C[:], in0=C[:], scalar=1.0, in1=E[:, 0:T], op0=ALU.add, op1=ALU.mult).then_inc(om, 1)

                def scan(d):
                    dve.wait_ge(sq, 2 * t + d + 1)
                    dve.wait_ge(iu, 2 * t + d + 1)
                    stt(out=B[:], in0=C[:], scalar=0.5, in1=B[:], op0=ALU.mult, op1=ALU.mult).then_inc(bt, 1)
                    dve.wait_ge(bt, 2 * t + d + 1)
                    dve.wait_ge(ea, 2 * t + d + 1)
                    if d == 0:
                        if not first:
                            dve.wait_ge(mrs, 16 * t)
                        nc.vector.tensor_tensor_scan(H[:, N_LAT:T], A[:, N_LAT:T], B[:, N_LAT:T], 0.0,
                                                     ALU.mult, ALU.add).then_inc(cf, 1)
                        dve.wait_ge(cf, t + 1)
                        nc.vector.tensor_tensor_scan(H[:, 0:N_LAT], A[:, 0:N_LAT], B[:, 0:N_LAT], H[:, T - 1:T],
                                                     ALU.mult, ALU.add).then_inc(hd, 1)
                    else:
                        nc.vector.tensor_tensor_scan(rev(E), rev(A), rev(B), 0.0,
                                                     ALU.mult, ALU.add).then_inc(hd, 1)

                direction(0)
                scan(0)
                for c, (at, n) in enumerate(CHUNKS):
                    dve.wait_ge(tgf, 3 * t + c + 1)
                    stt(out=sgf[:, at:at + n], in0=sgf[:, at:at + n], scalar=1.0, in1=slab[:, c, 0:n],
                        op0=ALU.add, op1=ALU.mult).then_inc(sgfd, 1)
                direction(1)
                dve.wait_ge(pqh, t + 1)
                tt(pq_lo[:], Wf[:, 0:PQ_N], v32(pq_hi[:]), ALU.subtract).then_inc(pql, 1)
                scan(1)
                for c, (at, n) in enumerate(CHUNKS):
                    dve.wait_ge(tg, 3 * t + c + 1)
                    stt(out=B[:, at:at + n], in0=B[:, at:at + n], scalar=1.0, in1=slab[:, c, 0:n],
                        op0=ALU.add, op1=ALU.mult).then_inc(sg, 1)
                dve.wait_ge(us, t + 1)
                dve.wait_ge(yl, t + 1)
                lat = xf[:, 0:N_LAT].rearrange("p (k r) -> p r k", r=RAD)
                cu = fT[:, 0:UV_N].rearrange("p (r k) -> p r k", k=P)
                sv = Wf[:, 2 * 512:2 * 512 + UV_N].rearrange("p (r k) -> p r k", k=P)
                tt(lat[:, 0:N_R, :], cu[:, 0:N_R, :], sv[:, 0:N_R, :], ALU.subtract).then_inc(yc, 1)
                for r in range(1, RAD - N_R + 1):
                    tt(lat[:, RAD - r, ::-1], cu[:, r, :], sv[:, r, :], ALU.add).then_inc(yc, 1)
                cx = xf[:, N_LAT:T].rearrange("p (k r) -> p r k", r=2)
                tt(cx, cu[:, N_R:N_R + 2, :], sv[:, N_R:N_R + 2, :], ALU.subtract).then_inc(yd, 1)
                dve.wait_ge(yc, 4 * t + 4)
                dve.wait_ge(yd, t + 1)
                dve.wait_ge(sgfd, 3 * t + 3)
                stt(out=xf[:], in0=xf[:], scalar=0.5, in1=sgf[:], op0=ALU.mult, op1=ALU.mult).then_inc(mf, 1)
                dve.wait_ge(hs, t + 1)
                dve.wait_ge(sg, 3 * t + 3)
                stt(out=H[:], in0=H[:], scalar=0.5, in1=B[:], op0=ALU.mult, op1=ALU.mult).then_inc(mr, 1)

            loops(dve, body)

        @blk.gpsimd
        def _(pool):
            sub = nc.gpsimd.tensor_tensor

            def split_lo(t, j):
                pool.wait_ge(wh[j % 2], 2 * t + j // 2 + 1)
                sub(w_lo[:, j % 2].rearrange("p k n -> p (k n)"), wraw[:, j % 2, :],
                    v32(w_hi[:, j % 2].rearrange("p k n -> p (k n)")), ALU.subtract).then_inc(wl[j % 2], 1)

            def body(t, first, last):
                split_lo(t, SLAB_F)
                split_lo(t, SLAB_GF)
                pool.wait_ge(gwh, t + 1)
                sub(gw_lo[:], gw[:], v32(gw_hi[:]), ALU.subtract).then_inc(gwl, 1)
                pool.wait_ge(uh, t + 1)
                sub(u_lo[:], u[:], v32(u_hi[:]), ALU.subtract).then_inc(ul, 1)
                split_lo(t, SLAB_G)
                pool.wait_ge(yh, t + 1)
                sub(y_lo[:], xf[:], v32(y_hi[:]), ALU.subtract).then_inc(yl, 1)
                if not last:
                    split_lo(t + 1, SLAB_U)
                pool.wait_ge(hd, 2 * t + 2)
                sub(H[:], H[:], E[:, 0:T], ALU.add).then_inc(hs, 1)

            split_lo(0, SLAB_U)
            for k in range(0, KT, 2):
                pool.wait_ge(h32, 2 * k + 2)
                sub(h_lo[:, k, :], work[:, k, :], v32(h_hi[:, k, :]), ALU.subtract).then_inc(hl[0], 1)
            loops(pool, body)

        @blk.tensor
        def _(pe):
            def mm3(out, l_hi, l_lo, r_hi, r_lo, start, stop):
                nc.tensor.matmul(out, l_hi, r_hi, start=start, stop=False)
                nc.tensor.matmul(out, l_hi, r_lo, start=False, stop=False)
                return nc.tensor.matmul(out, l_lo, r_hi, start=False, stop=stop)

            def first_product():
                pe.wait_ge(wl[0], 1)
                for k in range(KT):
                    pe.wait_ge(hl[k % 2], k // 2 + 1)
                    for c, (at, n) in enumerate(CHUNKS):
                        last = mm3(slab[:, c, 0:n], w_hi[:, 0, k, :], w_lo[:, 0, k, :],
                                   h_hi[:, k, at:at + n], h_lo[:, k, at:at + n], k == 0, k == KT - 1)
                        if k == KT - 1:
                            last.then_inc(s_u, 1)

            def slab_product(t, j, first):
                pe.wait_ge(wl[j % 2], 2 * t + j // 2 + 1)
                for c, (at, n) in enumerate(CHUNKS):
                    if j == SLAB_F:
                        pe.wait_ge(ur, 3 * t + c + 1)
                    elif j == SLAB_GF:
                        pe.wait_ge(fr, 3 * t + c + 1)
                    elif j == SLAB_G:
                        pe.wait_ge(sgfd, 3 * t + c + 1)
                    elif not first:
                        pe.wait_ge(sg, 3 * (t - 1) + c + 1)
                    for k in range(KT):
                        last = mm3(slab[:, c, 0:n], w_hi[:, j % 2, k, :], w_lo[:, j % 2, k, :],
                                   h_hi[:, k, at:at + n], h_lo[:, k, at:at + n], k == 0, k == KT - 1)
                    last.then_inc(done[j], 1)

            def gate_products(t, d):
                for x in range(2):
                    for c, (at, n) in enumerate(CHUNKS):
                        k = 6 * d + 3 * x + c
                        if k < 3:
                            pe.wait_ge(xr, 3 * t + k + 1)
                        elif k > 3:
                            pe.wait_ge(gr, 12 * t + k - 3)
                        mm3(W[:, k % 4, 0:n], gw_hi[:, 2 * d + x, :], gw_lo[:, 2 * d + x, :],
                            u_hi[:, at:at + n], u_lo[:, at:at + n], True, True).then_inc(gp_, 1)

            def mod_product(t, q, first):
                pe.wait_ge(m_ld, 16 * (2 * t + q + 1))
                if q == 1:
                    pe.wait_ge(abl, t + 1)
                elif not first:
                    pe.wait_ge(me, 2 * t)
                for k in range(KT):
                    last = nc.tensor.matmul(W4[0:2, 0:MOD_C], silu_c[:, k, :], wm1[:, k, :],
                                            start=(k == 0), stop=(k == KT - 1))
                last.then_inc(mp, 1)

            def dft_product(t):
                pe.wait_ge(gr, 12 * t + 12)
                pe.wait_ge(tab_l, 2)
                pe.wait_ge(yl, t + 1)
                for i in range(N_R + 2):
                    key = i if i < N_R else ("c0", "c1")[i - N_R]
                    at = TAB_AT[key]
                    out = Wf[:, 256 * i:256 * i + 256]
                    if key in (1, 2, 3):
                        re, im = ((2, 3), (4, 5), (6, 7))[key - 1]
                        ys = slice(re * P, re * P + P)
                        mm3(out, y_hi[:, ys], y_lo[:, ys], tab_hi[:, at + P:at + P + 256],
                            tab_lo[:, at + P:at + P + 256], True, False)
                        ys = slice(im * P, im * P + P)
                        last = mm3(out, y_hi[:, ys], y_lo[:, ys], tab_hi[:, at:at + 256],
                                   tab_lo[:, at:at + 256], False, True)
                    else:
                        y = {0: 0, 4: 1, "c0": 8, "c1": 9}[key]
                        ys = slice(y * P, y * P + P)
                        last = mm3(out, y_hi[:, ys], y_lo[:, ys], tab_hi[:, at:at + 256], tab_lo[:, at:at + 256],
                                   True, True)
                last.then_inc(dft, 1)

            def body(t, first, last_):
                if first:
                    first_product()
                else:
                    slab_product(t, SLAB_U, first)
                mod_product(t, 0, first)
                slab_product(t, SLAB_F, first)
                pe.wait_ge(fr, 3 * t + 3)
                if first:
                    pe.wait_ge(par, 32)
                else:
                    pe.wait_ge(yd, t)
                for i in range(TT):
                    last = nc.tensor.transpose(W[:, i // 4, (i % 4) * P:(i % 4 + 1) * P], fT[:, i * P:(i + 1) * P],
                                               ident[:])
                    if i % 4 == 3 or i == TT - 1:
                        last.then_inc(trd, 1)
                pe.wait_ge(wf_ld, 16 * t + 16)
                pe.wait_ge(me, 2 * t + 1)
                for x in range(2):
                    last = nc.tensor.matmul(W4[:, x * P:(x + 1) * P], dft_ch[:, x * P:(x + 1) * P], wf[:],
                                            start=True, stop=True)
                last.then_inc(abp, 1)
                pe.wait_ge(gwl, t + 1)
                pe.wait_ge(ul, t + 1)
                gate_products(t, 0)
                slab_product(t, SLAB_GF, first)
                gate_products(t, 1)
                dft_product(t)
                slab_product(t, SLAB_G, first)
                pe.wait_ge(pql, t + 1)
                pe.wait_ge(abl, t + 1)
                for x in range(2):
                    hi = pq_hi[:].rearrange("p (r x k) -> p r x k", x=2, k=P)[:, :, x, :]
                    lo = pq_lo[:].rearrange("p (r x k) -> p r x k", x=2, k=P)[:, :, x, :]
                    for b, (r0, r1) in enumerate(((0, 4), (4, N_R + 2))):
                        last = mm3(W[:, 2 * x + b, 0:(r1 - r0) * P], ab_hi[:, x * P:(x + 1) * P],
                                   ab_lo[:, x * P:(x + 1) * P], hi[:, r0:r1, :], lo[:, r0:r1, :], True, True)
                last.then_inc(uv, 1)
                mod_product(t, 1, first)

            loops(pe, body)


def pool_share(n):
    return range(2, n, 3)


def dve_share(n):
    return [k for k in range(n) if k % 3 != 2]


def wait_low(engine, made, k):
    if k % 3 == 2:
        engine.wait_ge(made[0], k // 3 + 1)
    else:
        engine.wait_ge(made[1], k - k // 3 + 1)


def out_projection0(nc, a, gs1, early, h1_ld, w1_ld):
    ctx = ExitStack()
    with ctx:
        def sb(name, shape, dt=F32):
            return ctx.enter_context(nc.sbuf_tensor(name, shape, dt))

        sem = a["sem"]

        K2 = 2 * KT
        wo_hi, wo_lo = sb("wo_hi", [P, K2, D], F32R), sb("wo_lo", [P, K2, D], F32R)
        mraw = sb("mraw", [P, 2, KT, P])
        m_hi, m_lo = (sb(n, [P, 2, 2, KT, P], F32R) for n in ("m_hi", "m_lo"))
        gpb = sb("gpb", [P, 2, D])
        xt = sb("xt2", [P, 2, D])
        x1 = sb("x1_tiles", [P, 2, D])
        xn = sb("xn2", [P, D])
        hb = sb("hb", [P, 2, KT, P])
        junk = sb("junk2", [P, D])
        ident = sb("ident2", [P, P])
        st = sb("st2", [P, 6, 2])
        eps = sb("eps2", [P, 1])
        Y = ctx.enter_context(nc.psum_tensor("Y", [P, 2, D], F32))
        TP = ctx.enter_context(nc.psum_tensor("TP", [P, 2, D], F32))

        par, wr_ld = sem("out0_par"), [sem(f"wo_loaded{i}") for i in range(4)]
        woh, wol = sem("wo_hi_done"), [sem("wo_lo_pool"), sem("wo_lo_dve")]
        m_ld, mh, ml = [sem("m_loaded0"), sem("m_loaded1")], [sem("m_hi0"), sem("m_hi1")], [sem("m_lo0"), sem("m_lo1")]
        x_ld = [sem("x2_loaded0"), sem("x2_loaded1")]
        half = [sem("y_half0"), sem("y_half1")]
        y1, y2, y3, yn, xd = sem("y_sum"), sem("y_root"), sem("y_rstd"), sem("y_scaled"), sem("x1_ready")
        z1, z2, z3, xnd = sem("x1_sum"), sem("x1_root"), sem("x1_rstd"), sem("xn2_ready")
        tr, hg, hd = sem("xn_transposed"), sem("h_gained"), sem("h_ready")
        xst, hst = [sem("x1_stored0"), sem("x1_stored1")], [sem("h_stored0"), sem("h_stored1")]
        gst = sem("gp1_stored")
        xd_last, hd_last = sem("x1_ready_last"), sem("h_ready_last")
        r1, r2, mt, gsd, es = sem("mod1_rows"), sem("mod1_gain"), sem("mod1_transposed"), sem("gs1_done"), sem("eps2_set")
        blk = ctx.enter_context(nc.Block())

        def mrow(q):
            return x1[0:2, q, :] if q < 2 else xn[0:2, :]

        hrow = [hb[:, i].rearrange("p k n -> p (k n)") for i in range(2)]
        brow = [hrow[0][0:2], hrow[1][0:2], junk[0:2, :], xt[0:2, 0, :], xt[0:2, 1, :]]
        wr = [x1[:, 0, :], x1[:, 1, :], hrow[0], hrow[1]]

        def loops(eng, body):
            body(0, 0, True, False)
            body(1, 1, False, False)
            with eng.Fori(1, LT // 2) as j:
                body(2 * j, 0, False, False)
                body(2 * j + 1, 1, False, False)
            body(LT, 0, False, False)
            body(LT + 1, 1, False, True)

        def is_last(t):
            return isinstance(t, int) and t == TT - 1

        def is_ctx(t):
            return isinstance(t, int) and t >= LT

        @blk.sync
        def _(sp):
            def at(t):
                return t * P if isinstance(t, int) else sp.snap(t * P)

            def load_mix(t, h, first):
                n = at(t)
                if not first:
                    sp.wait_ge(ml[h], t)
                sp.dma_start(mraw[:, h], a["mixT"][h * KT:(h + 1) * KT, :, bass.ds(n, P)].rearrange("k p n -> p k n"))\
                    .then_inc(m_ld[h], 16)

            def load_x(t, s, first):
                n = at(t)
                if not first:
                    sp.wait_ge(xd, t - 1)
                sp.dma_start(xt[:, s, :], a["x"][bass.ds(n, P), :]).then_inc(x_ld[s], 16)

            def store(t, s):
                n = at(t)
                if not is_ctx(t):
                    sp.wait_ge(xd, t + 1)
                    sp.dma_start(a["x1"][bass.ds(n, P), :], x1[:, s, :]).then_inc(xst[s], 16)
                if is_last(t):
                    sp.wait_ge(hd_last, 1)
                else:
                    sp.wait_ge(hd, t + 1)
                sp.dma_start(a["hT1"][t], hb[:, s]).then_inc(hst[s], 16)

            def load_w(k):
                if k >= 4:
                    wait_low(sp, wol, k - 4)
                sp.dma_start(wr[k % 4], a["w_out0"][k * P:(k + 1) * P, :]).then_inc(wr_ld[k % 4], 16)

            load_w(0)
            load_mix(0, 0, True)
            load_w(1)
            load_mix(0, 1, True)
            for k in range(2, K2):
                load_w(k)
                if k == K2 - 4:
                    load_mix(1, 0, False)
                    load_mix(1, 1, False)
            sp.dma_start(gpb[:], a["gp"][0].partition_broadcast(P)).then_inc(par, 16)
            sp.dma_start(ident[:], a["ident"]).then_inc(par, 16)
            wait_low(sp, wol, K2 - 2)
            wait_low(sp, wol, K2 - 1)
            for q in range(3):
                sp.dma_start(mrow(q), a["mod1"].rearrange("w a b -> w (a b)")[:, q * D:(q + 1) * D]).then_inc(par, 16)
            for q in range(5):
                sp.dma_start(brow[q], a["rows1"][:, q * D:(q + 1) * D]).then_inc(par, 16)
            sp.wait_ge(r2, 2)
            sp.dma_start(a["gp"][1], mrow(2)).then_inc(gst, 16)
            load_x(0, 0, True)
            load_x(1, 1, True)

            def body(t, s, first, last):
                if not first and not last:
                    load_mix(t + 1, 0, False)
                    load_mix(t + 1, 1, False)
                    load_x(t + 1, 1 - s, False)
                if not first:
                    store(t - 1, 1 - s)

            loops(sp, body)
            sp.dma_start(early[:, 2, :], a["w_in1"][0]).then_inc(w1_ld[0], 16)
            for i in range(2):
                if i == 0:
                    sp.wait_ge(hst[0], 8 * TT)
                else:
                    sp.wait_ge(hst[1], 8 * (TT - 2))
                sp.dma_start(early[:, i, :].rearrange("p (k n) -> p k n", n=P), a["hT1"][i]).then_inc(h1_ld[i], 16)
            store(TT - 1, 1)
            for s in range(2):
                sp.wait_ge(xst[s], 8 * LT)
                sp.wait_ge(hst[s], 8 * TT)
            sp.wait_ge(gst, 16)

        @blk.scalar
        def _(act):
            def split(t, s, h):
                act.wait_ge(m_ld[h], 16 * t + 16)
                if not (isinstance(t, int) and t < 2):
                    act.wait_ge(half[h], t - 1)
                nc.scalar.activation(m_hi[:, s, h], mraw[:, h], ACT.Copy).then_inc(mh[h], 1)

            def epilogue(t, s):
                act.wait_ge(half[1], t + 1)
                nc.scalar.activation(junk[:], Y[:, s, :], ACT.Square, accum_out=st[:, 0, s:s + 1]).then_inc(y1, 1)
                act.wait_ge(y1, t + 1)
                nc.scalar.activation(st[:, 1, s:s + 1], st[:, 0, s:s + 1], ACT.Sqrt, bias=eps[:, 0:1],
                                     scale=1.0 / D).then_inc(y2, 1)
                if is_last(t):
                    act.wait_ge(xd_last, 1)
                else:
                    act.wait_ge(xd, t + 1)
                nc.scalar.activation(junk[:], x1[:, s, :], ACT.Square, accum_out=st[:, 3, s:s + 1]).then_inc(z1, 1)
                act.wait_ge(z1, t + 1)
                nc.scalar.activation(st[:, 4, s:s + 1], st[:, 3, s:s + 1], ACT.Sqrt, bias=eps[:, 0:1],
                                     scale=1.0 / D).then_inc(z2, 1)

            split(0, 0, 0)
            act.wait_ge(es, 1)
            for k in range(K2):
                if k == 2:
                    split(0, 0, 1)
                act.wait_ge(wr_ld[k % 4], 16 * (k // 4 + 1))
                nc.scalar.activation(wo_hi[:, k, :], wr[k % 4], ACT.Copy).then_inc(woh, 1)

            def body(t, s, first, last):
                if not last:
                    split(t + 1, 1 - s, 0)
                    split(t + 1, 1 - s, 1)
                if not first:
                    epilogue(t - 1, 1 - s)

            loops(act, body)
            epilogue(TT - 1, 1)

        @blk.vector
        def _(dve):
            nc.vector.memset(eps[:], EPS).then_inc(es, 1)
            tt, stt = nc.vector.tensor_tensor, nc.vector.scalar_tensor_tensor
            for k in dve_share(K2):
                dve.wait_ge(woh, k + 1)
                tt(wo_lo[:, k, :], wr[k % 4], v32(wo_hi[:, k, :]), ALU.subtract).then_inc(wol[1], 1)
            dve.wait_ge(par, 160)
            for q in range(3):
                tt(mrow(q), mrow(q), brow[q], ALU.add).then_inc(r1, 1)
            dve.wait_ge(r1, 3)
            stt(out=mrow(1), in0=mrow(1), scalar=1.0, in1=brow[3], op0=ALU.add, op1=ALU.mult).then_inc(r2, 1)
            tt(mrow(2), mrow(2), brow[4], ALU.mult).then_inc(r2, 1)
            dve.wait_ge(mt, 1)
            nc.vector.tensor_copy(gs1[:].rearrange("p a k w -> p (a k w)"), TP[:, 0, 0:4 * KT]).then_inc(gsd, 1)

            def epilogue(t, s):
                w = 1 if is_ctx(t) else 0
                dve.wait_ge(y2, t + 1)
                nc.vector.reciprocal(st[:, 2, s:s + 1], st[:, 1, s:s + 1]).then_inc(y3, 1)
                dve.wait_ge(y3, t + 1)
                if isinstance(t, int) and t < 2:
                    dve.wait_ge(gst, 16)
                else:
                    dve.wait_ge(xst[s], 8 * (t - s))
                stt(out=x1[:, s, :], in0=Y[:, s, :], scalar=st[:, 2, s:s + 1], in1=gpb[:, w, :], op0=ALU.mult,
                    op1=ALU.mult).then_inc(yn, 1)
                if is_last(t):
                    dve.wait_ge(x_ld[s], 8 * (t - s) + 16)
                    dve.wait_ge(yn, TT)
                    tt(x1[:, s, :], x1[:, s, :], xt[:, s, :], ALU.add).then_inc(xd_last, 1)
                dve.wait_ge(z2, t + 1)
                nc.vector.reciprocal(st[:, 5, s:s + 1], st[:, 4, s:s + 1]).then_inc(z3, 1)
                dve.wait_ge(z3, t + 1)
                if not (isinstance(t, int) and t == 0):
                    dve.wait_ge(tr, t)
                nc.vector.tensor_scalar(xn[:], x1[:, s, :], st[:, 5, s:s + 1], None, ALU.mult).then_inc(xnd, 1)
                dve.wait_ge(tr, t + 1)
                if not (isinstance(t, int) and t < 2):
                    dve.wait_ge(hst[s], 8 * (t - s))
                tt(hb[:, s], TP[:, s, :].rearrange("p (k n) -> p k n", n=P),
                   gs1[:, 1, :, w:w + 1].to_broadcast([P, KT, P]), ALU.mult).then_inc(hg, 1)
                if is_last(t):
                    dve.wait_ge(hg, TT)
                    tt(hb[:, s], hb[:, s], gs1[:, 0, :, w:w + 1].to_broadcast([P, KT, P]), ALU.add).then_inc(hd_last, 1)

            def body(t, s, first, last):
                if not first:
                    epilogue(t - 1, 1 - s)

            loops(dve, body)
            epilogue(TT - 1, 1)

        @blk.gpsimd
        def _(pool):
            tt = nc.gpsimd.tensor_tensor

            def split(t, s, h):
                pool.wait_ge(mh[h], t + 1)
                tt(m_lo[:, s, h], mraw[:, h], v32(m_hi[:, s, h]), ALU.subtract).then_inc(ml[h], 1)

            split(0, 0, 0)
            for k in pool_share(K2):
                if k == 5:
                    split(0, 0, 1)
                pool.wait_ge(woh, k + 1)
                tt(wo_lo[:, k, :], wr[k % 4], v32(wo_hi[:, k, :]), ALU.subtract).then_inc(wol[0], 1)

            def epilogue(t, s):
                w = 1 if is_ctx(t) else 0
                pool.wait_ge(x_ld[s], 8 * (t - s) + 16)
                pool.wait_ge(yn, t + 1)
                tt(x1[:, s, :], x1[:, s, :], xt[:, s, :], ALU.add).then_inc(xd, 1)
                pool.wait_ge(gsd, 1)
                pool.wait_ge(hg, t + 1)
                tt(hb[:, s], hb[:, s], gs1[:, 0, :, w:w + 1].to_broadcast([P, KT, P]), ALU.add).then_inc(hd, 1)

            def body(t, s, first, last):
                if not last:
                    split(t + 1, 1 - s, 0)
                    split(t + 1, 1 - s, 1)
                if not first:
                    epilogue(t - 1, 1 - s)

            loops(pool, body)

        @blk.tensor
        def _(pe):
            def modulation_columns():
                pe.wait_ge(par, 160)
                pe.wait_ge(r2, 2)
                for q in range(2 * KT):
                    last = nc.tensor.transpose(TP[:, 0, 2 * q:2 * q + 2],
                                               mrow(q // KT)[:, (q % KT) * P:(q % KT + 1) * P], ident[0:2, 0:2])
                last.then_inc(mt, 1)

            def product(t, s, first):
                for h in range(2):
                    pe.wait_ge(ml[h], t + 1)
                    if h == 0 and not (isinstance(t, int) and t < 2):
                        pe.wait_ge(yn, t - 1)
                    for k in range(KT):
                        if first:
                            wait_low(pe, wol, h * KT + k)
                        for n in (0, 512):
                            out = Y[:, s, n:n + 512]
                            w_hi, w_lo = wo_hi[:, h * KT + k, n:n + 512], wo_lo[:, h * KT + k, n:n + 512]
                            nc.tensor.matmul(out, m_hi[:, s, h, k, :], w_hi, start=(h == 0 and k == 0), stop=False)
                            nc.tensor.matmul(out, m_hi[:, s, h, k, :], w_lo, start=False, stop=False)
                            last = nc.tensor.matmul(out, m_lo[:, s, h, k, :], w_hi, start=False,
                                                    stop=(h == 1 and k == KT - 1))
                    last.then_inc(half[h], 1)

            def transposes(t, s):
                pe.wait_ge(xnd, t + 1)
                if isinstance(t, int) and t < 2:
                    pe.wait_ge(gsd, 1)
                else:
                    pe.wait_ge(hg, t - 1)
                for k in range(KT):
                    last = nc.tensor.transpose(TP[:, s, k * P:(k + 1) * P], xn[:, k * P:(k + 1) * P], ident[:])
                last.then_inc(tr, 1)

            def body(t, s, first, last):
                product(t, s, first)
                if isinstance(t, int) and t == 1:
                    modulation_columns()
                if not first:
                    transposes(t - 1, 1 - s)

            loops(pe, body)
            transposes(TT - 1, 1)

def projections1(nc, a, kd_hi, kd_lo, vs, early, h_ld, w_ld):
    ctx = ExitStack()
    with ctx:
        def sb(name, shape, dt=F32):
            return ctx.enter_context(nc.sbuf_tensor(name, shape, dt))

        sem = a["sem"]

        h_hi, h_lo = sb("h1_hi", [P, KT, T], F32R), sb("h1_lo", [P, KT, T], F32R)
        wraw = [early[:, 2, :], sb("w1_raw", [P, D])[:]]
        w_hi, w_lo = sb("w1_hi", [P, 2, KT, P], F32R), sb("w1_lo", [P, 2, KT, P], F32R)
        cos, sin = early[:, 0, :], early[:, 1, :]
        R = sb("rope_in", [P, T])
        Z = sb("rope_swap", [P, N_LAT])
        C = sb("rope_cosined", [P, N_LAT])
        H, L = sb("rot_hi", [P, T], F32R), sb("rot_lo", [P, T], F32R)
        G = sb("gate1", [P, N_LAT])
        hraw = [cos, sin, C[:], Z[:]]
        ident = sb("ident3", [P, P])
        slab = ctx.enter_context(nc.psum_tensor("slab1", [P, 6, 512], F32))
        VP = ctx.enter_context(nc.psum_tensor("VP", [P, 2, 512], F32))

        par = sem("proj1_par")
        hh, hl = sem("h1_hi_done"), [sem("h1_lo0"), sem("h1_lo1")]
        wh, wl = [sem("w1_hi0"), sem("w1_hi1")], [sem("w1_lo0"), sem("w1_lo1")]
        kv, kvr = sem("kv_chunk"), sem("kv_chunk_read")
        sw, rc, rs, ro = sem("swapped"), sem("times_cos"), sem("times_sin"), sem("rotated")
        rh, rl = sem("rotated_hi"), sem("rotated_lo")
        kst = sem("k_spread")
        vtr, vh, vl = sem("v_transposed"), sem("v_hi_done"), sem("v_lo_done")
        qd, qr, qst = sem("q_chunk"), sem("q_chunk_read"), sem("q_stored")
        gd, gt, gg, gst = sem("g_chunk"), sem("g_tanh"), sem("g_silu"), sem("g_stored")
        blk = ctx.enter_context(nc.Block())
        V_GROUPS = [(0, 4), (4, 4), (8, 2)]

        def h_tile(i):
            return hraw[i % 4].rearrange("p (k n) -> p k n", n=P)

        def v_psum(s, g, n):
            return VP[:, (3 * s + g) % 2, 0:n * P].rearrange("p (t c d) -> p t c d", c=2, d=HEAD)

        def v_part(s, t0, n, part):
            return vs[:, t0:t0 + n, 2 * s:2 * s + 2, HEAD * part:HEAD * (part + 1)]

        def loops(eng, body, n=KT):
            body(0, True, False)
            with eng.Fori(1, n - 1) as t:
                body(t, False, False)
            body(n - 1, False, True)

        @blk.sync
        def _(sp):
            def load_slab(at, j, use):
                if not (isinstance(use, int) and use == 0):
                    sp.wait_ge(wl[j], use)
                sp.dma_start(wraw[j], a["w_in1"][at]).then_inc(w_ld[j], 16)

            for i in range(2, TT):
                if i >= 4:
                    wait_low(sp, hl, i - 4)
                sp.dma_start(h_tile(i), a["hT1"][i]).then_inc(h_ld[i % 4], 16)
                if i == 3:
                    load_slab(1, 1, 0)
            for i in range(TT - 4, TT):
                wait_low(sp, hl, i)
            sp.dma_start(cos, a["rope"][0]).then_inc(par, 16)
            sp.dma_start(sin, a["rope"][1]).then_inc(par, 16)
            sp.dma_start(ident[:], a["ident"]).then_inc(par, 16)
            load_slab(2, 0, 1)
            load_slab(3, 1, 1)
            for s in range(2):
                for ready, part, dst in ((rh, H, kd_hi), (rl, L, kd_lo)):
                    sp.wait_ge(ready, s + 1)
                    for c in range(2):
                        for v in range(2):
                            sp.dma_start(v32(dst[HEAD * v:HEAD * (v + 1), 2 * s + c, :]),
                                         v32(part[HEAD * c:HEAD * (c + 1), :])).then_inc(kst, 16)

            def store(t):
                for v, (ready, part) in enumerate(((rh, H), (rl, L))):
                    sp.wait_ge(ready, t + 3)
                    sp.dma_start(a["qT"][:, v, :, t, :].rearrange("b p n -> p b n"),
                                 v32(part[:, 0:N_LAT]).rearrange("p (b n) -> p b n", n=P)).then_inc(qst, 16)
                sp.wait_ge(gg, 2 * t + 2)
                sp.dma_start(a["sgT"][:, :, t, :].rearrange("b p n -> p b n"),
                             G[:].rearrange("p (b n) -> p b n", n=P)).then_inc(gst, 16)

            def body(t, first, last):
                load_slab(2 * t + 4, 0, t + 2)
                load_slab(2 * t + 5, 1, t + 2)
                if not first:
                    store(t - 1)

            loops(sp, body)
            store(KT - 1)
            sp.wait_ge(kst, 256)
            sp.wait_ge(qst, 32 * KT)
            sp.wait_ge(gst, 16 * KT)

        @blk.scalar
        def _(act):
            def split(j, use):
                act.wait_ge(w_ld[j], 16 * use + 16)
                nc.scalar.activation(w_hi[:, j].rearrange("p k n -> p (k n)"), wraw[j], ACT.Copy).then_inc(wh[j], 1)

            split(0, 0)
            for i in range(TT):
                act.wait_ge(h_ld[i % 4], 16 * (i // 4 + 1))
                nc.scalar.activation(h_hi[:, :, i * P:(i + 1) * P], h_tile(i),
                                     ACT.Copy).then_inc(hh, 1)
                if i == 3:
                    split(1, 0)
            for s in range(4):
                if s in (1, 2):
                    act.wait_ge(rl, s)
                elif s == 3:
                    act.wait_ge(vtr, 3)
                for c, (at, n) in enumerate(CHUNKS):
                    act.wait_ge(kv, 3 * s + c + 1)
                    nc.scalar.activation(R[:, at:at + n], slab[:, 3 * (s % 2) + c, 0:n], ACT.Copy).then_inc(kvr, 1)
                split(s % 2, s // 2 + 1)
                if s < 2:
                    act.wait_ge(ro, s + 1)
                    if s == 1:
                        act.wait_ge(kst, 128)
                    nc.scalar.activation(H[:], R[:], ACT.Copy).then_inc(rh, 1)
                else:
                    for g, (t0, n) in enumerate(V_GROUPS):
                        act.wait_ge(vtr, 3 * (s - 2) + g + 1)
                        nc.scalar.activation(v_part(s - 2, t0, n, 0), v_psum(s - 2, g, n), ACT.Copy).then_inc(vh, 1)

            def body(t, first, last):
                if first:
                    act.wait_ge(vtr, 6)
                else:
                    act.wait_ge(rl, t + 2)
                for c in range(2):
                    act.wait_ge(qd, 2 * t + c + 1)
                    nc.scalar.activation(R[:, 512 * c:512 * c + 512], slab[:, c, :], ACT.Copy).then_inc(qr, 1)
                if not last:
                    split(0, t + 3)
                if not first:
                    act.wait_ge(gst, 16 * t)
                for c in range(2):
                    act.wait_ge(gd, 2 * t + c + 1)
                    nc.scalar.activation(G[:, 512 * c:512 * c + 512], slab[:, 3 + c, :], ACT.Tanh, scale=0.5)\
                        .then_inc(gt, 1)
                    if c == 0:
                        act.wait_ge(ro, t + 3)
                        if first:
                            act.wait_ge(kst, 256)
                        else:
                            act.wait_ge(qst, 32 * t)
                        nc.scalar.activation(H[:, 0:N_LAT], R[:, 0:N_LAT], ACT.Copy).then_inc(rh, 1)
                if not last:
                    split(1, t + 3)

            loops(act, body)

        @blk.vector
        def _(dve):
            tt = nc.vector.tensor_tensor
            for i in dve_share(TT):
                at = slice(i * P, (i + 1) * P)
                dve.wait_ge(hh, i + 1)
                tt(h_lo[:, :, at], h_tile(i), v32(h_hi[:, :, at]), ALU.subtract).then_inc(hl[1], 1)
            dve.wait_ge(par, 48)

            def rotate(ready, value, n):
                dve.wait_ge(ready, value)
                if not (isinstance(n, int) and n == 0):
                    dve.wait_ge(ro, n)
                tt(C[:], R[:, 0:N_LAT], cos, ALU.mult).then_inc(rc, 1)
                nc.vector.stream_shuffle(Z[:], R[:, 0:N_LAT], [(i + 16) % 32 for i in range(32)]).then_inc(sw, 1)
                dve.wait_ge(rc, n + 1)
                dve.wait_ge(sw, n + 1)
                dve.wait_ge(rs, n + 1)
                tt(R[:, 0:N_LAT], C[:], Z[:], ALU.add).then_inc(ro, 1)

            rotate(kvr, 3, 0)
            rotate(kvr, 6, 1)
            for s in range(2):
                for g, (t0, n) in enumerate(V_GROUPS):
                    dve.wait_ge(vh, 3 * s + g + 1)
                    tt(v_part(s, t0, n, 1), v_psum(s, g, n), v32(v_part(s, t0, n, 0)), ALU.subtract).then_inc(vl, 1)

            def body(t, first, last):
                rotate(qr, 2 * t + 2, t + 2)
                for c in range(2):
                    dve.wait_ge(gt, 2 * t + c + 1)
                    nc.vector.scalar_tensor_tensor(out=G[:, 512 * c:512 * c + 512], in0=G[:, 512 * c:512 * c + 512],
                                                   scalar=1.0, in1=slab[:, 3 + c, :], op0=ALU.add,
                                                   op1=ALU.mult).then_inc(gg, 1)

            loops(dve, body)

        @blk.gpsimd
        def _(pool):
            tt = nc.gpsimd.tensor_tensor

            def split(j, use):
                pool.wait_ge(wh[j], use + 1)
                tt(w_lo[:, j].rearrange("p k n -> p (k n)"), wraw[j],
                   v32(w_hi[:, j].rearrange("p k n -> p (k n)")), ALU.subtract).then_inc(wl[j], 1)

            def sines(n):
                pool.wait_ge(sw, n + 1)
                tt(Z[:], Z[:], sin, ALU.mult).then_inc(rs, 1)

            split(0, 0)
            for i in pool_share(TT):
                at = slice(i * P, (i + 1) * P)
                pool.wait_ge(hh, i + 1)
                tt(h_lo[:, :, at], h_tile(i), v32(h_hi[:, :, at]), ALU.subtract).then_inc(hl[0], 1)
                if i == 5:
                    split(1, 0)
            pool.wait_ge(par, 48)
            for s in range(2):
                split(s, 1)
                sines(s)
                pool.wait_ge(rh, s + 1)
                tt(L[:], R[:], v32(H[:]), ALU.subtract).then_inc(rl, 1)
            split(0, 2)
            split(1, 2)

            def body(t, first, last):
                if not last:
                    split(0, t + 3)
                sines(t + 2)
                pool.wait_ge(rh, t + 3)
                tt(L[:, 0:N_LAT], R[:, 0:N_LAT], v32(H[:, 0:N_LAT]), ALU.subtract).then_inc(rl, 1)
                if not last:
                    split(1, t + 3)

            loops(pool, body)

        @blk.tensor
        def _(pe):
            def product(j, use, c, at, n):
                out = slab[:, 3 * j + c, 0:n]
                for k in range(KT):
                    rhs_hi, rhs_lo = h_hi[:, k, at:at + n], h_lo[:, k, at:at + n]
                    nc.tensor.matmul(out, w_hi[:, j, k, :], rhs_hi, start=(k == 0), stop=False)
                    nc.tensor.matmul(out, w_hi[:, j, k, :], rhs_lo, start=False, stop=False)
                    last = nc.tensor.matmul(out, w_lo[:, j, k, :], rhs_hi, start=False, stop=(k == KT - 1))
                return last

            def transposes(s):
                pe.wait_ge(kvr, 3 * (s + 2) + 3)
                for g, (t0, n) in enumerate(V_GROUPS):
                    if 3 * s + g >= 2:
                        pe.wait_ge(vl, 3 * s + g - 1)
                    for i in range(n):
                        last = nc.tensor.transpose(VP[:, (3 * s + g) % 2, i * P:(i + 1) * P], R[:, (t0 + i) * P:(t0 + i + 1) * P],
                                                   ident[:])
                    last.then_inc(vtr, 1)

            for s in range(4):
                pe.wait_ge(wl[s % 2], s // 2 + 1)
                for c, (at, n) in enumerate(CHUNKS):
                    if s == 0:
                        for i in range(at // P, (at + n) // P):
                            wait_low(pe, hl, i)
                    if s >= 2:
                        pe.wait_ge(kvr, 3 * (s - 2) + c + 1)
                    product(s % 2, s // 2, c, at, n).then_inc(kv, 1)
                if s == 3:
                    pe.wait_ge(par, 48)
                    transposes(0)

            def body(t, first, last):
                pe.wait_ge(wl[0], t + 3)
                for c in range(2):
                    if first:
                        pe.wait_ge(kvr, 9)
                    else:
                        pe.wait_ge(qr, 2 * (t - 1) + c + 1)
                    product(0, t + 2, c, 512 * c, 512).then_inc(qd, 1)
                if first:
                    transposes(1)
                pe.wait_ge(wl[1], t + 3)
                for c in range(2):
                    if not first:
                        pe.wait_ge(gg, 2 * (t - 1) + c + 1)
                    product(1, t + 2, c, 512 * c, 512).then_inc(gd, 1)

            loops(pe, body)


N_HD = 4
WIN = 5
AHEAD = 10
UNIT_AHEAD = 11


def attention(nc, a, kd_hi, kd_lo, vs, wo, early, m_ld):
    ctx = ExitStack()
    with ctx:
        def sb(name, shape, dt=F32):
            return ctx.enter_context(nc.sbuf_tensor(name, shape, dt))

        sem = a["sem"]
        NB = LT
        vw = sb("v_window", [P, 2, 3, N_KV, P], F32R)
        q = sb("q_parts", [P, 2, N_HEADS, P], F32R)
        pr = sb("probs", [P, 4, N_HD, WIN * P])
        pt_hi, pt_lo = sb("pt_hi", [P, WIN, 512], F32R), sb("pt_lo", [P, WIN, 512], F32R)
        ost = sb("o_out", [P, 2, N_KV, N_HD * P])
        mask = sb("mask", [P, (2 * WIN - 1) * P])
        sink, nsink = sb("sink", [P, N_HEADS]), sb("nsink", [P, N_HEADS])
        nm, es, rsum, den, rden = (sb(n, [P, 4, N_HD]) for n in ("neg_max", "sink_term", "row_sum", "denom", "rdenom"))
        ident = sb("ident4", [P, P])
        S = ctx.enter_context(nc.psum_tensor("S", [P, 2, 1024], F32))
        TB = ctx.enter_context(nc.psum_tensor("TB", [P, 2, 512], F32))
        O = ctx.enter_context(nc.psum_tensor("O", [P, 2, 512], F32))

        par, nsk, wo_ld = sem("att_par"), sem("neg_sink"), sem("w_out1_loaded")
        v_ld = [sem("v_window0"), sem("v_window1")]
        q_ld = [sem("q_loaded0"), sem("q_loaded1")]
        sd, td, ed = sem("scores"), sem("scaled_max"), sem("exp_done")
        sa, se, dn, rc, pn = sem("sink_minus_max"), sem("sink_exp"), sem("denom_done"), sem("rdenom_done"), sem("normalised")
        tr, ph, pl, pv = sem("p_transposed"), sem("pt_hi_done"), sem("pt_lo_done"), sem("value_product")
        oe, ost_s = sem("o_copied"), [sem("o_stored0"), sem("o_stored1")]
        blk = ctx.enter_context(nc.Block())

        def loops(eng, body):
            body(0, 0)
            body(1, 1)
            with eng.Fori(1, NB // 2 - 1) as j:
                body(2 * j, 0)
                body(2 * j + 1, 1)
            body(NB - 2, 0)
            body(NB - 1, 1)

        def is_block(b, n):
            return isinstance(b, int) and b == n

        def tiles(b):
            return WIN - 1 if is_block(b, 0) or is_block(b, NB - 1) else WIN

        def tiles_before(b):
            return 0 if is_block(b, 0) else 20 * b - 4

        def n_par(b, u, x):
            return (tiles(b) * u + x) % 2

        def head_steps(b):
            return range(tiles(b) - N_HD, tiles(b))

        def take(head, b, j):
            if j < N_HEADS:
                head(b, j)
            elif not is_block(b, NB - 1):
                head(b + 1, j - N_HEADS)

        def row(b, buf):
            return buf[..., 0:tiles(b) * P]

        @blk.sync
        def _(sp):
            def load_q(b, s):
                for v in range(2):
                    for c in range(2):
                        sp.dma_start(v32(q[HEAD * v:HEAD * (v + 1), s]).rearrange("d (p c h) n -> d c p h n", p=2, c=2)[:, c],
                                     a["qT"][b, v, HEAD * c:HEAD * (c + 1)].rearrange("d (p h) n -> d p h n", p=2))\
                            .then_inc(q_ld[s], 16)

            def load_v(b, s):
                sp.dma_start(v32(vw[:, s]), v32(vs[:, bass.ds(b - 1, 3)])).then_inc(v_ld[s], 16)

            load_q(0, 0)
            sp.dma_start(sink[:], a["sink"]).then_inc(par, 16)
            sp.dma_start(mask[:], a["mask"]).then_inc(par, 16)
            sp.dma_start(ident[:], a["ident"]).then_inc(par, 16)
            load_q(1, 1)
            load_v(1, 1)
            for k in range(KT):
                sp.dma_start(wo[:, k, :], a["w_out1"][k]).then_inc(wo_ld, 16)

            def body(b, s):
                if not isinstance(b, int) or b < NB - 2:
                    sp.wait_ge(sd, 16 * b + 16)
                    load_q(b + 2, s)
                if not isinstance(b, int) or b < NB - 3:
                    sp.wait_ge(pv, tiles_before(b + 1))
                    load_v(b + 2, s)
                if is_block(b, NB - 1):
                    sp.wait_ge(ost_s[0], 8 * NB)
                    load_mixed(nc, a, 0, early[:, 0:2].rearrange("p a (k n) -> p a k n", n=P),
                               early[:, 2].rearrange("p (k n) -> p k n", n=P), m_ld[0])
                sp.wait_ge(oe, 4 * b + 4)
                sp.dma_start(a["oT"][b], ost[:, s]).then_inc(ost_s[s], 16)

            body(0, 0)
            with sp.Fori(0, NB // 2 - 2) as j:
                body(2 * j + 1, 1)
                body(2 * j + 2, 0)
            for b in range(NB - 3, NB):
                body(b, b % 2)
            sp.wait_ge(wo_ld, 16 * KT)
            for s in range(2):
                sp.wait_ge(ost_s[s], 8 * NB)

        @blk.scalar
        def _(act):
            def head(b, j):
                u, h = j // 4, j % 4
                act.wait_ge(td, 16 * b + j + 1)
                r = row(b, pr[:, u, h, :])
                nc.scalar.activation(r, r, ACT.Exp, bias=nm[:, u, h:h + 1], scale=-1.0,
                                     accum_out=rsum[:, u, h:h + 1]).then_inc(ed, 1)
                if h == N_HD - 1:
                    act.wait_ge(sa, 4 * b + u + 1)
                    nc.scalar.activation(es[:, u, :], es[:, u, :], ACT.Exp).then_inc(se, 1)

            def copy_o(b, s, u):
                act.wait_ge(pv, tiles_before(b) + tiles(b) * (u + 1))
                if u == 0 and not (isinstance(b, int) and b < 2):
                    act.wait_ge(ost_s[s], 8 * (b - s))
                nc.scalar.activation(ost[:, s, u, :], O[:, u % 2, :], ACT.Copy).then_inc(oe, 1)

            for j in range(AHEAD - 1):
                head(0, j)

            def body(b, s):
                for u in range(4):
                    for x in range(tiles(b)):
                        n = tiles_before(b) + tiles(b) * u + x
                        act.wait_ge(tr, n + 1)
                        if u:
                            act.wait_ge(pv, n + 1 - tiles(b))
                        elif not is_block(b, 0):
                            before = 4 if is_block(b, 1) else 5
                            act.wait_ge(pv, tiles_before(b) - before + min(x + 1, before))
                        nc.scalar.activation(pt_hi[:, x, :], TB[:, n_par(b, u, x), :], ACT.Copy).then_inc(ph, 1)
                        if x in head_steps(b):
                            take(head, b, 4 * u + head_steps(b).index(x) + AHEAD - 1)
                        if x == 1:
                            if u:
                                copy_o(b, s, u - 1)
                            elif not is_block(b, 0):
                                copy_o(b - 1, 1 - s, 3)

            loops(act, body)
            copy_o(NB - 1, 1, 3)

        @blk.vector
        def _(dve):
            tt = nc.vector.tensor_tensor
            dve.wait_ge(par, 48)
            nc.vector.tensor_scalar(nsink[:], sink[:], -1.0, None, ALU.mult).then_inc(nsk, 1)
            dve.wait_ge(nsk, 1)

            def head_waits(b, j):
                dve.wait_ge(sd, 16 * b + j + 1)
                if not is_block(b, 0):
                    dve.wait_ge(tr, tiles_before(b - 1) + tiles(b - 1) * (j // 4 + 1))

            def head(b, j):
                u, h = j // 4, j % 4
                at = P if tiles(b) == WIN else 2 * P
                m = mask[:, WIN * P:] if is_block(b, NB - 1) else mask[:, P:WIN * P] if is_block(b, 0) else mask[:, 0:WIN * P]
                nc.vector.tensor_tensor_reduce(
                    out=row(b, pr[:, u, h, :]), in0=S[:, j % 2, at:768], in1=m, scale=-SCALE, scalar=nsink[:, j:j + 1],
                    op0=ALU.add, op1=ALU.min, accum_out=nm[:, u, h:h + 1]).then_inc(td, 1)

            def reciprocals(b, j):
                u = j // 4
                dve.wait_ge(dn, 4 * b + u + 1)
                nc.vector.reciprocal(rden[:, u, :], den[:, u, :]).then_inc(rc, 1)

            for j in range(AHEAD):
                head_waits(0, j)
                head(0, j)
                if j in (5, 9):
                    reciprocals(0, j - 2)

            def body(b, s):
                for u in range(4):
                    for x in range(tiles(b)):
                        n = tiles_before(b) + tiles(b) * u + x
                        k = x - head_steps(b)[0]
                        if k >= 0:
                            take(head_waits, b, 4 * u + k + AHEAD)
                        dve.wait_ge(ph, n + 1)
                        tt(pt_lo[:, x, :], TB[:, n_par(b, u, x), :], v32(pt_hi[:, x, :]), ALU.subtract).then_inc(pl, 1)
                        if k >= 0:
                            take(head, b, 4 * u + k + AHEAD)
                        if k == 3:
                            take(reciprocals, b, 4 * u + UNIT_AHEAD)

            loops(dve, body)

        @blk.gpsimd
        def _(pool):
            def sinks(b, j):
                u = j // 4
                pool.wait_ge(td, 16 * b + j + 1)
                nc.gpsimd.tensor_tensor(es[:, u, :], nm[:, u, :], sink[:, 4 * u:4 * u + 4], ALU.add).then_inc(sa, 1)

            def unit(b, j):
                u = j // 4
                pool.wait_ge(se, 4 * b + u + 1)
                nc.gpsimd.tensor_tensor(den[:, u, :], es[:, u, :], rsum[:, u, :], ALU.add).then_inc(dn, 1)
                pool.wait_ge(rc, 4 * b + u + 1)
                rows = row(b, pr[:, u])
                nc.gpsimd.tensor_tensor(rows, rows, rden[:, u, :].unsqueeze(2).to_broadcast(rows.shape),
                                        ALU.mult).then_inc(pn, 1)

            pool.wait_ge(par, 48)
            for j in (3, 7):
                sinks(0, j)
                unit(0, j)

            def body(b, s):
                for u in range(4):
                    take(sinks, b, 4 * u + UNIT_AHEAD)
                    take(unit, b, 4 * u + UNIT_AHEAD)

            loops(pool, body)

        @blk.tensor
        def _(pe):
            def scores(b, j, s):
                u = j // 4
                if j == 0:
                    pe.wait_ge(q_ld[s], 32 * (b - s) + 64)
                if not (is_block(b, 0) and j < 2):
                    pe.wait_ge(td, 16 * b + j - 1)
                n = (tiles(b) - 2) * P
                at = 0 if is_block(b, 0) else (b - 1) * P
                for out, start, size in ((S[:, j % 2, 512 - n:512], at, n), (S[:, j % 2, 512:768], N_LAT, N_CTX)):
                    nc.tensor.matmul(out, q[:, s, j, :], kd_hi[:, u, bass.ds(start, size)], start=True, stop=False)
                    last = nc.tensor.matmul(out, q[:, s, j, :], kd_lo[:, u, bass.ds(start, size)], start=False, stop=True)
                last.then_inc(sd, 1)

            def values(b, s, u, x):
                n = tiles_before(b) + tiles(b) * u + x
                pe.wait_ge(pl, n + 1)
                if x == 0 and not (is_block(b, 0) and u < 2):
                    pe.wait_ge(oe, 4 * b + u - 1)
                if tiles(b) == WIN and x == 0 and u == 0:
                    pe.wait_ge(v_ld[s], 8 * b + 8 * s)
                left = tiles(b) - 2
                if x >= left:
                    v = vs[:, LT + x - left, u, :]
                elif tiles(b) == WIN:
                    v = vw[:, s, x, u, :]
                else:
                    v = vs[:, x if b == 0 else NB - 2 + x, u, :]
                out = O[:, u % 2, :]
                nc.tensor.matmul(out, v, pt_hi[:, x, :], start=(x == 0), stop=False)
                nc.tensor.matmul(out, v, pt_lo[:, x, :], start=False, stop=(x == tiles(b) - 1)).then_inc(pv, 1)

            for j in range(AHEAD):
                scores(0, j, 0)
            pe.wait_ge(par, 48)

            def body(b, s):
                for u in range(4):
                    for x in range(tiles(b)):
                        n = tiles_before(b) + tiles(b) * u + x
                        if x == 0:
                            pe.wait_ge(pn, 4 * b + u + 1)
                        if not (is_block(b, 0) and u == 0 and x < 2):
                            pe.wait_ge(pl, n - 1)
                        for h in range(N_HD):
                            last = nc.tensor.transpose(TB[:, n_par(b, u, x), h * P:(h + 1) * P],
                                                       pr[:, u, h, x * P:(x + 1) * P], ident[:])
                        last.then_inc(tr, 1)
                        j = 4 * u + x - head_steps(b)[0] + AHEAD
                        if x in head_steps(b) and j < N_HEADS:
                            scores(b, j, s)
                        elif x in head_steps(b) and not is_block(b, NB - 1):
                            scores(b + 1, j - N_HEADS, 1 - s)
                        if x >= 1:
                            values(b, s, u, x - 1)
                        elif u:
                            values(b, s, u - 1, tiles(b) - 1)
                        elif not is_block(b, 0):
                            values(b - 1, 1 - s, 3, tiles(b - 1) - 1)

            loops(pe, body)
            values(NB - 1, 1, 3, tiles(NB - 1) - 1)


def load_mixed(nc, a, t, oraw, graw, loaded):
    for part in range(2):
        for c in range(2):
            nc.sync.dma_start(oraw[HEAD * c:HEAD * (c + 1), part].rearrange("d (p h) n -> d p (h n)", p=2),
                              a["oT"][t, HEAD * part:HEAD * (part + 1)].rearrange("d (p c) n -> d c p n", c=2)[:, c])\
                .then_inc(loaded, 16)
    nc.sync.dma_start(graw, a["sgT"][t]).then_inc(loaded, 16)


def out_projection1(nc, a, wo, early, m_ld):
    ctx = ExitStack()
    with ctx:
        def sb(name, shape, dt=F32):
            return ctx.enter_context(nc.sbuf_tensor(name, shape, dt))

        sem = a["sem"]

        wo_hi, wo_lo = sb("wo1_hi", [P, KT, D], F32R), sb("wo1_lo", [P, KT, D], F32R)
        oraw = [early[:, 0:2].rearrange("p a (k n) -> p a k n", n=P), sb("o_raw", [P, 2, KT, P])[:]]
        graw = [early[:, 2].rearrange("p (k n) -> p k n", n=P), sb("g_raw", [P, KT, P])[:]]
        m_hi, m_lo = sb("m1_hi", [P, 2, KT, P], F32R), sb("m1_lo", [P, 2, KT, P], F32R)
        gpb = sb("gpb1", [P, D])
        xt = sb("xt5", [P, 2, D])
        out = sb("out_tiles", [P, 2, D])
        junk = sb("junk5", [P, D])
        st = sb("st5", [P, 3, 2])
        eps = sb("eps5", [P, 1])
        Y = ctx.enter_context(nc.psum_tensor("Y1", [P, 2, D], F32))

        par = sem("out1_par")
        woh, wol = sem("wo1_hi_done"), [sem("wo1_lo_pool"), sem("wo1_lo_dve")]
        os_, xd_last = sem("o_summed"), sem("out_ready_last")
        md, mh, ml = sem("mixed1"), sem("m1_hi_done"), sem("m1_lo_done")
        x_ld = [sem("x5_loaded0"), sem("x5_loaded1")]
        yd = sem("y1_product")
        y1, y2, y3, yn, xd = sem("y1_sum"), sem("y1_root"), sem("y1_rstd"), sem("y1_scaled"), sem("out_ready")
        ost, es = [sem("out_stored0"), sem("out_stored1")], sem("eps5_set")
        blk = ctx.enter_context(nc.Block())

        def loops(eng, body):
            body(0, 0, True, False)
            body(1, 1, False, False)
            with eng.Fori(1, LT // 2 - 1) as j:
                body(2 * j, 0, False, False)
                body(2 * j + 1, 1, False, False)
            body(LT - 2, 0, False, False)
            body(LT - 1, 1, False, True)

        def is_early(t):
            return isinstance(t, int) and t < 2

        @blk.sync
        def _(sp):
            def load(t, s):
                if not is_early(t):
                    sp.wait_ge(ml, t - 1)
                if not (isinstance(t, int) and t == 0):
                    load_mixed(nc, a, t, oraw[s], graw[s], m_ld[s])
                if not is_early(t):
                    sp.wait_ge(xd, t - 1)
                sp.dma_start(xt[:, s, :], a["x1"][bass.ds(t * P, P), :]).then_inc(x_ld[s], 16)

            def store(t, s):
                if isinstance(t, int) and t == LT - 1:
                    sp.wait_ge(xd_last, 1)
                else:
                    sp.wait_ge(xd, t + 1)
                sp.dma_start(a["out"][0, bass.ds(t * P, P), :], out[:, s, :]).then_inc(ost[s], 16)

            load(0, 0)
            sp.dma_start(gpb[:], a["gp"][1, 0:1].partition_broadcast(P)).then_inc(par, 16)
            load(1, 1)

            def body(t, s, first, last):
                if not first and not last:
                    load(t + 1, 1 - s)
                if not first:
                    store(t - 1, 1 - s)

            loops(sp, body)
            store(LT - 1, 1)
            for s in range(2):
                sp.wait_ge(ost[s], 8 * LT)

        @blk.scalar
        def _(act):
            def split(t, s):
                act.wait_ge(md, t + 1)
                if not is_early(t):
                    act.wait_ge(yd, t - 1)
                nc.scalar.activation(m_hi[:, s], oraw[s][:, 0], ACT.Copy).then_inc(mh, 1)

            def epilogue(t, s):
                act.wait_ge(yd, t + 1)
                nc.scalar.activation(junk[:], Y[:, s, :], ACT.Square, accum_out=st[:, 0, s:s + 1]).then_inc(y1, 1)
                act.wait_ge(y1, t + 1)
                nc.scalar.activation(st[:, 1, s:s + 1], st[:, 0, s:s + 1], ACT.Sqrt, bias=eps[:, 0:1],
                                     scale=1.0 / D).then_inc(y2, 1)

            nc.scalar.activation(wo_hi[:, 0, :], wo[:, 0, :], ACT.Copy).then_inc(woh, 1)
            split(0, 0)
            for k in range(1, KT):
                nc.scalar.activation(wo_hi[:, k, :], wo[:, k, :], ACT.Copy).then_inc(woh, 1)
            split(1, 1)
            act.wait_ge(es, 1)

            def body(t, s, first, last):
                if not first:
                    epilogue(t - 1, 1 - s)
                    if not last:
                        split(t + 1, 1 - s)

            loops(act, body)
            epilogue(LT - 1, 1)

        @blk.vector
        def _(dve):
            tt, stt = nc.vector.tensor_tensor, nc.vector.scalar_tensor_tensor
            nc.vector.memset(eps[:], EPS).then_inc(es, 1)

            def mix(t, s):
                dve.wait_ge(m_ld[s], 40 * (t - s) + 80)
                tt(oraw[s][:, 0], oraw[s][:, 0], oraw[s][:, 1], ALU.add).then_inc(os_, 1)
                dve.wait_ge(os_, t + 1)
                stt(out=oraw[s][:, 0], in0=oraw[s][:, 0], scalar=0.5, in1=graw[s], op0=ALU.mult, op1=ALU.mult)\
                    .then_inc(md, 1)

            def epilogue(t, s):
                dve.wait_ge(y2, t + 1)
                nc.vector.reciprocal(st[:, 2, s:s + 1], st[:, 1, s:s + 1]).then_inc(y3, 1)
                dve.wait_ge(y3, t + 1)
                if not is_early(t):
                    dve.wait_ge(ost[s], 8 * (t - s))
                stt(out=out[:, s, :], in0=Y[:, s, :], scalar=st[:, 2, s:s + 1], in1=gpb[:], op0=ALU.mult,
                    op1=ALU.mult).then_inc(yn, 1)

            mix(0, 0)
            for k in dve_share(KT):
                dve.wait_ge(woh, k + 1)
                tt(wo_lo[:, k, :], wo[:, k, :], v32(wo_hi[:, k, :]), ALU.subtract).then_inc(wol[1], 1)
            mix(1, 1)
            dve.wait_ge(par, 16)

            def body(t, s, first, last):
                if not first:
                    epilogue(t - 1, 1 - s)
                    if not last:
                        mix(t + 1, 1 - s)

            loops(dve, body)
            epilogue(LT - 1, 1)
            dve.wait_ge(x_ld[1], 8 * LT)
            dve.wait_ge(yn, LT)
            tt(out[:, 1, :], out[:, 1, :], xt[:, 1, :], ALU.add).then_inc(xd_last, 1)

        @blk.gpsimd
        def _(pool):
            tt = nc.gpsimd.tensor_tensor

            def split(t, s):
                pool.wait_ge(mh, t + 1)
                tt(m_lo[:, s], oraw[s][:, 0], v32(m_hi[:, s]), ALU.subtract).then_inc(ml, 1)

            def epilogue(t, s):
                pool.wait_ge(x_ld[s], 8 * (t - s) + 16)
                pool.wait_ge(yn, t + 1)
                tt(out[:, s, :], out[:, s, :], xt[:, s, :], ALU.add).then_inc(xd, 1)

            split(0, 0)
            for k in pool_share(KT):
                pool.wait_ge(woh, k + 1)
                tt(wo_lo[:, k, :], wo[:, k, :], v32(wo_hi[:, k, :]), ALU.subtract).then_inc(wol[0], 1)
            split(1, 1)

            def body(t, s, first, last):
                if not first:
                    epilogue(t - 1, 1 - s)
                    if not last:
                        split(t + 1, 1 - s)

            loops(pool, body)

        @blk.tensor
        def _(pe):
            def body(t, s, first, last):
                pe.wait_ge(ml, t + 1)
                if not is_early(t):
                    pe.wait_ge(yn, t - 1)
                for k in range(KT):
                    if first:
                        wait_low(pe, wol, k)
                    for n in (0, 512):
                        o = Y[:, s, n:n + 512]
                        w_hi, w_lo = wo_hi[:, k, n:n + 512], wo_lo[:, k, n:n + 512]
                        nc.tensor.matmul(o, m_hi[:, s, k, :], w_hi, start=(k == 0), stop=False)
                        nc.tensor.matmul(o, m_hi[:, s, k, :], w_lo, start=False, stop=False)
                        l = nc.tensor.matmul(o, m_lo[:, s, k, :], w_hi, start=False, stop=(k == KT - 1))
                l.then_inc(yd, 1)

            loops(pe, body)


def rev(buf):
    return buf[:, T - 1::-1]


def tables():
    m = np.arange(P)[:, None].astype(np.float64)
    k = np.arange(P)[None, :].astype(np.float64)
    out = np.zeros((P, TAB_N), np.float64)
    for key, at in TAB_AT.items():
        if isinstance(key, str):
            n, rad, r = N_CTX, 2, int(key[1])
        else:
            n, rad, r = N_LAT, RAD, key
        ang = 2 * np.pi * m * (rad * k + r) / n
        f = 1.0 / np.sqrt(n * P)
        if key in (1, 2, 3):
            out[:, at:at + P] = -np.sin(ang) * f
            at += P
        out[:, at:at + P] = np.cos(ang) * f
        out[:, at + P:at + 256] = np.sin(ang) * f
    ang = 2 * np.pi * m * k / P
    return out.astype(np.float32), np.concatenate([np.cos(ang), np.sin(ang)], 1).astype(np.float32)


def rope_tables():
    p = np.arange(P) % HEAD
    i = (p % 16).astype(np.float32)
    freq = (np.float32(ROPE_BASE) ** (-(2 * i) / np.float32(HEAD // 2))).astype(np.float32)
    tok = np.arange(N_LAT)
    pos = np.where((p < 32)[:, None], tok[None, :] // GRID_W, tok[None, :] % GRID_W).astype(np.float32)
    ang = (pos * freq[:, None]).astype(np.float64)
    sign = np.where(p % 32 < 16, -1.0, 1.0)[:, None]
    return np.stack([np.cos(ang), np.sin(ang) * sign]).astype(np.float32)


def window_mask():
    q, k = np.arange(P)[:, None], np.arange(P)[None, :]
    left, right, none = np.where(k >= q, 0.0, NEG_INF), np.where(k <= q, 0.0, NEG_INF), np.zeros((P, P))
    return np.concatenate([left, none, right, none, none, left, none, none, none], 1).astype(np.float32)


def paired(w):
    return w.reshape(w.shape[0], 2, 2, N_HD, HEAD).transpose(0, 1, 3, 2, 4).reshape(w.shape[0], D)


def build(nc, a):
    def layer1():
        with ExitStack() as ctx:
            def sb(name, shape, dt=F32):
                return ctx.enter_context(nc.sbuf_tensor(name, shape, dt))

            def sems(name, n):
                return [a["sem"](f"{name}{i}") for i in range(n)]

            early = sb("early", [P, 3, D])
            h_ld, w_ld, m_ld = sems("h1_loaded", 4), sems("w1_loaded", 2), sems("o_loaded", 2)
            gs1 = sb("gs1", [P, 2, KT, 2])
            out_projection0(nc, a, gs1, early, h_ld, w_ld)
            kd_hi, kd_lo = sb("kd_hi", [P, N_KV, T], F32R), sb("kd_lo", [P, N_KV, T], F32R)
            vs = sb("vs", [P, TT, N_KV, P], F32R)
            projections1(nc, a, kd_hi, kd_lo, vs, early, h_ld, w_ld)
            wo = sb("wo1_raw", [P, KT, D])
            attention(nc, a, kd_hi, kd_lo, vs, wo, early, m_ld)
            out_projection1(nc, a, wo, early, m_ld)

    with_semaphores(nc, a, lambda: layer0(nc, a))
    with_semaphores(nc, a, layer1)


def kernel(**inputs):
    import concourse.bacc as _bacc
    from concourse.bass_utils import run_bass_kernel_spmd as _run

    g = {k: np.ascontiguousarray(v) for k, v in inputs.items()}

    def col(v):
        return v.reshape(-1, KT, P).transpose(2, 0, 1)

    def slabs(w):
        return w.reshape(KT, P, -1, P).transpose(2, 1, 0, 3)

    def rows(layer):
        r = np.concatenate([g[layer + "_b_mod"], g[layer + "_g_pre"], g[layer + "_g_post"]])
        return np.stack([r, r])

    tab, dft_ch = tables()
    w0 = slabs(g["l0_w_in"])
    w_gate = np.stack([g["l0_w_a"][0], g["l0_w_x"][0], g["l0_w_a"][1], g["l0_w_x"][1]])
    w1, kv = g["l1_w_in"], N_KV * HEAD
    qg = np.stack([slabs(paired(w1[:, 0:D])), slabs(paired(w1[:, D + 2 * kv:]))], 1).reshape(2 * KT, P, KT, P)
    w_in1 = np.concatenate([slabs(w1[:, D:D + 2 * kv]), qg]).reshape(-1, P, D)
    arrays = {
        "x": np.concatenate([g["x"][0], g["ctx"][0]]),
        "cvec": np.stack([g["c"][0], g["c_ctx"]]).reshape(2, KT, P).transpose(2, 1, 0),
        "rows0": rows("l0"),
        "rows1": rows("l1"),
        "cols": np.concatenate([col(g["l0_w_conv"]), col(g["l0_b_conv"]), col(g["l0_b_a"]), col(g["l0_b_x"]),
                                col(g["l0_lam"]), col(g["l0_b_f"])], 1),
        "ident": np.eye(P, dtype=np.float32),
        "tables": tab,
        "dft_ch": dft_ch,
        "wm0": g["l0_w_mod"],
        "wm1": g["l1_w_mod"].reshape(KT, P, 2 * KT, MOD_C).transpose(2, 1, 0, 3),
        "w_in0": np.stack([w0[0:8], w0[16:24], w0[24:32], w0[8:16]], 1).reshape(4 * KT, P, D),
        "w_gate": w_gate.reshape(4, KT, 2 * HEAD, HEAD).transpose(1, 2, 0, 3),
        "w_f": g["l0_w_f"],
        "w_out0": g["l0_w_out"],
        "w_in1": w_in1,
        "rope": rope_tables(),
        "sink": np.broadcast_to(g["l1_sink"], (P, N_HEADS)),
        "mask": window_mask(),
        "w_out1": paired(g["l1_w_out"].T).T.reshape(KT, P, D),
    }
    nc = _bacc.Bacc("TRN2", target_bir_lowering=False, num_devices=1, dynamic_dma_scratch_size=1024)
    a = {}
    for name, v in list(arrays.items()):
        arrays[name] = v = np.ascontiguousarray(v)
        a[name] = nc.dram_tensor("in_" + name, v.shape, F32, kind="ExternalInput").ap()
    for name, shape in (("gp", (2, 2, D)), ("mod1", (2, 2 * KT, MOD_C)), ("mixT", (2 * KT, P, T)),
                        ("x1", (N_LAT, D)), ("hT1", (TT, P, KT, P)), ("qT", (LT, 2, P, KT, P)), ("sgT", (LT, P, KT, P)),
                        ("oT", (LT, P, N_KV, N_HD * P))):
        a[name] = nc.dram_tensor(name, shape, F32, kind="Internal").ap()
    a["out"] = nc.dram_tensor("out", (1, N_LAT, D), F32, kind="ExternalOutput").ap()
    build(nc, a)
    r = _run(nc, [{"in_" + k: v for k, v in arrays.items()}], core_ids=[0])
    return r.results[0]["out"]
```
